# Optimizing a Trainium2 kernel written in Bass

```python
import jax, jax.numpy as jnp
from jax import lax
import numpy as np
import math

D_MODEL = 1024
BATCH = 1
SEQ = 512
DEPTH = 1

HEAD_DIM = 64
RWKV_HEADS = 8
RWKV_WIDTH = RWKV_HEADS * HEAD_DIM
DECAY_LORA = 32
AAA_LORA = 32
ATTN_HEADS = 8
ATTN_WIDTH = ATTN_HEADS * HEAD_DIM
MIX_WIDTH = RWKV_WIDTH + ATTN_WIDTH
Q_RANK = 256
KV_RANK = 128
IDX_HEADS = 4
IDX_DIM = 64
TOPK_MAX = 256
Q_BLOCK = 128
NORM_EPS = 1e-6
LN_EPS = 1e-5
GN_EPS = 64e-5

SHIFT_SIZES = [RWKV_WIDTH, RWKV_WIDTH, RWKV_WIDTH, DECAY_LORA, AAA_LORA]
SHIFT_COLS = sum(SHIFT_SIZES)
IN_SIZES = [SHIFT_COLS, RWKV_WIDTH, Q_RANK, KV_RANK, IDX_DIM, IDX_HEADS, ATTN_WIDTH]
IN_COLS = sum(IN_SIZES)
SHIFT_SPLITS = np.cumsum(SHIFT_SIZES)[:-1].tolist()
IN_SPLITS = np.cumsum(IN_SIZES)[:-1].tolist()


def rmsnorm(x, g):
    xf = x.astype(jnp.float32)
    y = xf * lax.rsqrt(jnp.mean(xf * xf, axis=-1, keepdims=True) + NORM_EPS)
    return (y * g.astype(jnp.float32)).astype(x.dtype)

def layernorm(x, g, b):
    xf = x.astype(jnp.float32)
    mu = jnp.mean(xf, axis=-1, keepdims=True)
    var = jnp.mean(jnp.square(xf - mu), axis=-1, keepdims=True)
    y = (xf - mu) * lax.rsqrt(var + LN_EPS)
    return (y * g.astype(jnp.float32) + b.astype(jnp.float32)).astype(x.dtype)

def rwkv7_scan(r, decay, k, v, kk, a):
    B, T, H, D = r.shape
    tm = lambda t: jnp.moveaxis(t, 1, 0)

    def step(S, inp):
        r_t, w_t, k_t, v_t, kk_t, a_t = inp
        sa = jnp.einsum('bhij,bhj->bhi', S, -kk_t)
        S = (S * w_t[:, :, None, :]
             + sa[..., None] * (kk_t * a_t)[:, :, None, :]
             + v_t[..., None] * k_t[:, :, None, :])
        return S, jnp.einsum('bhij,bhj->bhi', S, r_t)

    S0 = jnp.zeros((B, H, D, D), jnp.float32)
    _, y = lax.scan(step, S0, (tm(r), tm(decay), tm(k), tm(v), tm(kk), tm(a)))
    return jnp.moveaxis(y, 0, 1)

def rwkv7_branch(p_shift, gate, mu_shift, w0, w_up, a0, a_up, k_k, k_a, r_k, gn_g, gn_b):
    B, T, _ = p_shift.shape
    f32 = jnp.float32
    prev = jnp.pad(p_shift, ((0, 0), (1, 0), (0, 0)))[:, :-1]
    xs = p_shift + (prev - p_shift) * mu_shift
    r, k, v, wd, ad = jnp.split(xs, SHIFT_SPLITS, axis=-1)
    wlog = -jax.nn.softplus(-(w0 + jnp.tanh(wd) @ w_up)) - 0.5
    decay = jnp.exp(-jnp.exp(wlog.astype(f32)))
    a = jax.nn.sigmoid((a0 + ad @ a_up).astype(f32))
    heads = lambda t: t.astype(f32).reshape(B, T, RWKV_HEADS, HEAD_DIM)
    r, k, v, a, decay = heads(r), heads(k), heads(v), heads(a), heads(decay)
    kk = k * k_k.astype(f32)
    kk = kk / jnp.maximum(jnp.sqrt(jnp.sum(kk * kk, axis=-1, keepdims=True)), 1e-12)
    k = k * (1.0 + (a - 1.0) * k_a.astype(f32))
    y = rwkv7_scan(r, decay, k, v, kk, a)
    mu = jnp.mean(y, axis=-1, keepdims=True)
    var = jnp.mean(jnp.square(y - mu), axis=-1, keepdims=True)
    y = (y - mu) * lax.rsqrt(var + GN_EPS) * gn_g.astype(f32) + gn_b.astype(f32)
    y = y + jnp.sum(r * k * r_k.astype(f32), axis=-1, keepdims=True) * v
    y = y.reshape(B, T, RWKV_WIDTH).astype(gate.dtype)
    return y * jax.nn.silu(gate)

def dsa_branch(q_down, kv_down, k_idx_raw, w_idx, gate, q_norm_g, kv_norm_g,
               w_uq, w_uk, w_uv, w_qidx, kidx_g, kidx_b):
    B, T, _ = q_down.shape
    f32 = jnp.float32
    c_q = rmsnorm(q_down, q_norm_g)
    c_kv = rmsnorm(kv_down, kv_norm_g)
    q = (c_q @ w_uq).reshape(B, T, ATTN_HEADS, HEAD_DIM)
    q_abs = jnp.einsum('bthd,hrd->bthr', q, w_uk) * (HEAD_DIM ** -0.5)
    q_idx = (c_q @ w_qidx).reshape(B, T, IDX_HEADS, IDX_DIM)
    k_idx = layernorm(k_idx_raw, kidx_g, kidx_b).astype(f32)
    w_i = w_idx * (IDX_HEADS ** -0.5)
    topk = min(TOPK_MAX, T // 4)
    nb = T // Q_BLOCK
    blocks = lambda t: jnp.moveaxis(t.reshape(B, nb, Q_BLOCK, *t.shape[2:]), 1, 0)
    key_pos = jnp.arange(T)

    def attend(args):
        qa, qi, wi, t0 = args
        q_pos = t0 + jnp.arange(Q_BLOCK)
        causal = key_pos[None, :] <= q_pos[:, None]
        logits = jnp.einsum('bqhd,bsd->bqhs', qi.astype(f32), k_idx)
        score = jnp.einsum('bqh,bqhs->bqs', wi.astype(f32), jax.nn.relu(logits))
        score = jnp.where(causal[None], score, -jnp.inf)
        _, idx = lax.top_k(score, topk)
        c_sel = jax.vmap(lambda c, i: c[i])(c_kv, idx).astype(f32)
        valid = idx <= q_pos[None, :, None]
        s = jnp.einsum('bqhr,bqkr->bhqk', qa.astype(f32), c_sel)
        s = jnp.where(valid[:, None], s, -jnp.inf)
        p = jax.nn.softmax(s, axis=-1)
        return jnp.einsum('bhqk,bqkr->bqhr', p, c_sel)

    o_lat = lax.map(attend, (blocks(q_abs), blocks(q_idx), blocks(w_i), jnp.arange(nb) * Q_BLOCK))
    o_lat = jnp.moveaxis(o_lat, 0, 1).reshape(B, T, ATTN_HEADS, KV_RANK).astype(gate.dtype)
    o = jnp.einsum('bthr,hrd->bthd', o_lat, w_uv).reshape(B, T, ATTN_WIDTH)
    return o * jax.nn.silu(gate)

def hybrid_layer(x, norm_g, w_in, mu_shift, w0, w_up, a0, a_up, k_k, k_a, r_k, gn_g, gn_b,
                 q_norm_g, kv_norm_g, w_uq, w_uk, w_uv, w_qidx, kidx_g, kidx_b, w_out):
    xn = rmsnorm(x, norm_g)
    p = xn @ w_in
    p_shift, g_rwkv, q_down, kv_down, k_idx_raw, w_idx, g_attn = jnp.split(p, IN_SPLITS, axis=-1)
    y_rwkv = rwkv7_branch(p_shift, g_rwkv, mu_shift, w0, w_up, a0, a_up, k_k, k_a, r_k, gn_g, gn_b)
    y_attn = dsa_branch(q_down, kv_down, k_idx_raw, w_idx, g_attn, q_norm_g, kv_norm_g,
                        w_uq, w_uk, w_uv, w_qidx, kidx_g, kidx_b)
    y = jnp.concatenate([y_rwkv, y_attn], axis=-1) @ w_out
    return x + y

def first_inputs(seed: int = 0) -> dict:
    key = jax.random.key(seed)
    ks = jax.random.split(key, 24)
    L = DEPTH
    f32 = jnp.float32
    nrm = lambda k, shape, scale: scale * jax.random.normal(k, shape, f32)
    gain = lambda k, shape: 1.0 + 0.05 * jax.random.normal(k, shape, f32)
    hd = (L, RWKV_HEADS, HEAD_DIM)
    return {
        "x": nrm(ks[0], (BATCH, SEQ, D_MODEL), 1.0),
        "norm_g": gain(ks[1], (L, D_MODEL)),
        "w_in": nrm(ks[2], (L, D_MODEL, IN_COLS), D_MODEL ** -0.5),
        "mu_shift": jax.random.uniform(ks[3], (L, SHIFT_COLS), f32),
        "w0": jax.random.uniform(ks[4], (L, RWKV_WIDTH), f32, -2.0, 2.0),
        "w_up": nrm(ks[5], (L, DECAY_LORA, RWKV_WIDTH), 0.5 * DECAY_LORA ** -0.5),
        "a0": nrm(ks[6], (L, RWKV_WIDTH), 0.5),
        "a_up": nrm(ks[7], (L, AAA_LORA, RWKV_WIDTH), 0.5 * AAA_LORA ** -0.5),
        "k_k": 0.85 + 0.05 * jax.random.normal(ks[8], hd, f32),
        "k_a": gain(ks[9], hd),
        "r_k": nrm(ks[10], hd, 0.1),
        "gn_g": gain(ks[11], hd),
        "gn_b": nrm(ks[12], hd, 0.02),
        "q_norm_g": gain(ks[13], (L, Q_RANK)),
        "kv_norm_g": gain(ks[14], (L, KV_RANK)),
        "w_uq": nrm(ks[15], (L, Q_RANK, ATTN_WIDTH), Q_RANK ** -0.5),
        "w_uk": nrm(ks[16], (L, ATTN_HEADS, KV_RANK, HEAD_DIM), KV_RANK ** -0.5),
        "w_uv": nrm(ks[17], (L, ATTN_HEADS, KV_RANK, HEAD_DIM), KV_RANK ** -0.5),
        "w_qidx": nrm(ks[18], (L, Q_RANK, IDX_HEADS * IDX_DIM), Q_RANK ** -0.5),
        "kidx_g": gain(ks[19], (L, IDX_DIM)),
        "kidx_b": nrm(ks[20], (L, IDX_DIM), 0.02),
        "w_out": nrm(ks[21], (L, MIX_WIDTH, D_MODEL), MIX_WIDTH ** -0.5),
        "final_g": gain(ks[22], (D_MODEL,)),
    }

def first_block(x, norm_g, w_in, mu_shift, w0, w_up, a0, a_up, k_k, k_a, r_k, gn_g, gn_b,
              q_norm_g, kv_norm_g, w_uq, w_uk, w_uv, w_qidx, kidx_g, kidx_b, w_out, final_g):
    for l in range(DEPTH):
        x = hybrid_layer(x, norm_g[l], w_in[l], mu_shift[l], w0[l], w_up[l], a0[l], a_up[l],
                         k_k[l], k_a[l], r_k[l], gn_g[l], gn_b[l], q_norm_g[l], kv_norm_g[l],
                         w_uq[l], w_uk[l], w_uv[l], w_qidx[l], kidx_g[l], kidx_b[l], w_out[l])
    return rmsnorm(x, final_g)


D_A = D_MODEL
K_A = 3
D_B = D_MODEL
K_B = 31
N_MEM = 256
N_HEADS = 4
HEAD_DIM_2 = D_MODEL // N_HEADS
D_ATT = N_HEADS * HEAD_DIM_2
N_BRANCH = 3
D_FF = 2816
K_F = 3
EPS = 1e-6
IN_SPLITS_2 = (3 * D_A, 3 * D_A + 2 * D_B, 3 * D_A + 2 * D_B + D_ATT)
D_IN = 3 * D_A + 2 * D_B + D_ATT + N_BRANCH * D_MODEL


def _rmsnorm(x, g):
    xf = x.astype(jnp.float32)
    r = lax.rsqrt(jnp.mean(xf * xf, axis=-1, keepdims=True) + EPS)
    return (xf * r).astype(x.dtype) * g

def _layernorm(x, g, b):
    xf = x.astype(jnp.float32)
    mu = jnp.mean(xf, axis=-1, keepdims=True)
    var = jnp.mean(jnp.square(xf - mu), axis=-1, keepdims=True)
    return ((xf - mu) * lax.rsqrt(var + EPS)).astype(x.dtype) * g + b

def _causal_dwconv(x, w):
    k, c = w.shape
    return lax.conv_general_dilated(
        x, w[:, None, :].astype(x.dtype), window_strides=(1,), padding=[(k - 1, 0)],
        dimension_numbers=("NWC", "WIO", "NWC"), feature_group_count=c)

def second_inputs(seed: int = 0) -> dict:
    key = jax.random.key(seed)
    ks = jax.random.split(key, 24)
    L, D = DEPTH, D_MODEL

    def nrm(k, shape, fan_in):
        return jax.random.normal(k, shape, jnp.float32) * (fan_in ** -0.5)

    def gain(k, shape):
        return 1.0 + 0.02 * jax.random.normal(k, shape, jnp.float32)

    def small(k, shape):
        return 0.02 * jax.random.normal(k, shape, jnp.float32)

    return {
        "x": jax.random.normal(ks[0], (BATCH, SEQ, D), jnp.float32),
        "mem": jax.random.normal(ks[1], (BATCH, N_MEM, D), jnp.float32),
        "norm_mix_g": gain(ks[2], (L, D)),
        "norm_mem_g": gain(ks[3], (L, D)),
        "w_in": nrm(ks[4], (L, D, D_IN), D),
        "b_gate": small(ks[5], (L, N_BRANCH * D)),
        "conv_a_w": nrm(ks[6], (L, K_A, D_A), K_A),
        "w_a_out": nrm(ks[7], (L, D_A, D), D_A),
        "conv_b_w": nrm(ks[8], (L, K_B, D_B), K_B),
        "conv_b_bias": small(ks[9], (L, D_B)),
        "ln_b_g": gain(ks[10], (L, D_B)),
        "ln_b_b": small(ks[11], (L, D_B)),
        "w_b_out": nrm(ks[12], (L, D_B, D), D_B),
        "w_kv": nrm(ks[13], (L, D, 2 * D_ATT), D),
        "w_att_out": nrm(ks[14], (L, D_ATT, D), D_ATT),
        "w_o": nrm(ks[15], (L, D, D), D),
        "norm_ffn_g": gain(ks[16], (L, D)),
        "w_up": nrm(ks[17], (L, D, 2 * D_FF), D),
        "conv_ffn_w": nrm(ks[18], (L, K_F, 2 * D_FF), K_F),
        "w_down": nrm(ks[19], (L, D_FF, D), D_FF),
        "norm_final_g": gain(ks[20], (D,)),
    }

def _mixer(x, mem, norm_mix_g, norm_mem_g, w_in, b_gate, conv_a_w, w_a_out,
           conv_b_w, conv_b_bias, ln_b_g, ln_b_b, w_b_out, w_kv, w_att_out, w_o):
    bsz, seq, _ = x.shape
    h = _rmsnorm(x, norm_mix_g)
    proj = h @ w_in
    p_a, p_b, q, p_g = jnp.split(proj, IN_SPLITS_2, axis=-1)

    gb, gc, v = jnp.split(p_a, 3, axis=-1)
    y_a = (gb * _causal_dwconv(gc * v, conv_a_w)) @ w_a_out

    u, ug = jnp.split(p_b, 2, axis=-1)
    u = u * jax.nn.sigmoid(ug)
    u = _causal_dwconv(u, conv_b_w) + conv_b_bias
    u = jax.nn.silu(_layernorm(u, ln_b_g, ln_b_b))
    y_b = u @ w_b_out

    memn = _rmsnorm(mem, norm_mem_g)
    k, vm = jnp.split(memn @ w_kv, 2, axis=-1)
    qh = q.reshape(bsz, seq, N_HEADS, HEAD_DIM_2)
    kh = k.reshape(bsz, N_MEM, N_HEADS, HEAD_DIM_2)
    vh = vm.reshape(bsz, N_MEM, N_HEADS, HEAD_DIM_2)
    s = jnp.einsum("bshd,bmhd->bhsm", qh, kh).astype(jnp.float32) * (1.0 / math.sqrt(HEAD_DIM_2))
    pr = jax.nn.softmax(s, axis=-1).astype(x.dtype)
    o = jnp.einsum("bhsm,bmhd->bshd", pr, vh).reshape(bsz, seq, D_ATT)
    y_c = o @ w_att_out

    g = jax.nn.sigmoid((p_g + b_gate).reshape(bsz, seq, N_BRANCH, D_MODEL))
    merged = g[:, :, 0] * y_a + g[:, :, 1] * y_b + g[:, :, 2] * y_c
    return merged @ w_o

def _conv_ffn(x, norm_ffn_g, w_up, conv_ffn_w, w_down):
    h = _rmsnorm(x, norm_ffn_g)
    u = _causal_dwconv(h @ w_up, conv_ffn_w)
    gt, up = jnp.split(u, 2, axis=-1)
    return (jax.nn.silu(gt) * up) @ w_down

def second_block(x, mem, norm_mix_g, norm_mem_g, w_in, b_gate, conv_a_w, w_a_out,
              conv_b_w, conv_b_bias, ln_b_g, ln_b_b, w_b_out, w_kv, w_att_out, w_o,
              norm_ffn_g, w_up, conv_ffn_w, w_down, norm_final_g):
    for l in range(DEPTH):
        x = x + _mixer(x, mem, norm_mix_g[l], norm_mem_g[l], w_in[l], b_gate[l],
                       conv_a_w[l], w_a_out[l], conv_b_w[l], conv_b_bias[l],
                       ln_b_g[l], ln_b_b[l], w_b_out[l], w_kv[l], w_att_out[l], w_o[l])
        x = x + _conv_ffn(x, norm_ffn_g[l], w_up[l], conv_ffn_w[l], w_down[l])
    return _rmsnorm(x, norm_final_g)


def setup_inputs(seed=0):
    out = dict(first_inputs(seed))
    for name, value in second_inputs(seed + 1).items():
        if name != "x":
            out[name + "_2"] = value
    return out


def reference(
    x, norm_g, w_in, mu_shift, w0, w_up, a0, a_up, k_k, k_a, r_k, gn_g, gn_b, q_norm_g,
    kv_norm_g, w_uq, w_uk, w_uv, w_qidx, kidx_g, kidx_b, w_out, final_g, mem_2, norm_mix_g_2,
    norm_mem_g_2, w_in_2, b_gate_2, conv_a_w_2, w_a_out_2, conv_b_w_2, conv_b_bias_2, ln_b_g_2,
    ln_b_b_2, w_b_out_2, w_kv_2, w_att_out_2, w_o_2, norm_ffn_g_2, w_up_2, conv_ffn_w_2,
    w_down_2, norm_final_g_2,
):
    x = first_block(
        x, norm_g, w_in, mu_shift, w0, w_up, a0, a_up, k_k, k_a, r_k, gn_g, gn_b, q_norm_g,
        kv_norm_g, w_uq, w_uk, w_uv, w_qidx, kidx_g, kidx_b, w_out, final_g,
    )
    return second_block(
        x, mem_2, norm_mix_g_2, norm_mem_g_2, w_in_2, b_gate_2, conv_a_w_2, w_a_out_2,
        conv_b_w_2, conv_b_bias_2, ln_b_g_2, ln_b_b_2, w_b_out_2, w_kv_2, w_att_out_2, w_o_2,
        norm_ffn_g_2, w_up_2, conv_ffn_w_2, w_down_2, norm_final_g_2,
    )


_drawn_inputs = setup_inputs


def setup_inputs(seed=0):
    import zlib

    import numpy as np

    out = dict(_drawn_inputs(seed))
    spreads = {}
    factors = {'k_k': 200.0,
     'gn_b': 5.464,
     'q_norm_g': 4.515,
     'kv_norm_g': 7.221,
     'kidx_g': 4.918,
     'kidx_b': 8.0,
     'norm_mix_g_2': 2.976,
     'norm_mem_g_2': 25.097,
     'b_gate_2': 8.0,
     'conv_b_bias_2': 18.218,
     'ln_b_g_2': 63.256,
     'ln_b_b_2': 64.0,
     'norm_ffn_g_2': 13.893,
     'norm_final_g_2': 22.62,
     'w_up': 2.744,
     'gn_g': 3.164}
    for name, (base, spread) in spreads.items():
        noise = np.random.default_rng([zlib.crc32(name.encode()), seed]).standard_normal(out[name].shape)
        drawn = base * np.exp(spread * noise) if base else spread * noise
        out[name] = __import__('jax').numpy.asarray(drawn.astype(out[name].dtype))
    for name, factor in factors.items():
        out[name] = (out[name] * factor).astype(out[name].dtype)
    return out
```

```python
from contextlib import ExitStack

import numpy as np

import concourse.bass as bass
from concourse import mybir

F32 = mybir.dt.float32
F32R = mybir.dt.float32r
ALU = mybir.AluOpType
ACT = mybir.ActivationFunctionType
X_AXIS = mybir.AxisListType.X

P = 128
D = 1024
T = 512
CH = D // P
NT = T // P
HD = 64
NH = 8
NI = NH // 2
MEM = 256
MH = 4
FF = 2816
FC = FF // P
TOPK = 128
KAPPA = float(np.exp(-0.5))
NORM_EPS, LN_EPS, GN_EPS, EPS2 = 1e-6, 1e-5, 64e-5, 1e-6
MASKED = -1.0e30
TAKEN = -3.0e38
KB, KA, KF = 31, 3, 3
BANKS = 8

C_R, C_K, C_V, C_WA, C_G, C_QD, C_KV, C_KI, C_WI, C_GA = 0, 512, 1024, 1536, 1600, 2112, 2368, 2496, 2560, 2564
C2_GB, C2_GC, C2_VA, C2_U, C2_UG, C2_Q, C2_PG = 0, 1024, 2048, 3072, 4096, 5120, 6144


def weight_units():
    units = []

    def add(what, i, pieces, nk=CH, k0=0):
        units.append((what, i, nk, [(at, w, col, n, k0) for at, w, col, n in pieces]))

    add("qd", 0, [(0, "w_in", C_QD, 256)])
    add("kvi", 0, [(0, "w_in", C_KV, 128), (128, "w_in", C_KI, 64), (192, "w_in", C_KI, 64)])
    add("wa", 0, [(0, "w_in", C_WA, 64), (64, "w_in", C_WI, 4), (68, "w_in", C_G + 4, 188)])
    for half in range(2):
        for what, col in (("r", C_R), ("k", C_K), ("v", C_V), ("g", C_G)):
            add(what, half, [(0, "w_in", col + 256 * half, 256)])
    for half in range(2):
        add("ga", half, [(0, "w_in", C_GA + 256 * half, 256)])
    for i in range(4):
        add("wout", i, [(0, "w_out", 256 * i, 256)])
    for i in range(4):
        add("kT", i, [(0, "w_kv_2", 256 * i, 256)])
    for i in range(4):
        add("vm", i, [(0, "w_kv_2", D + 256 * i, 256)])
    for i in range(8):
        add("u", i, [(0, "w_in_2", C2_U + P * i, P), (P, "w_in_2", C2_UG + P * i, P)])
    for i in range(4):
        add("q2", i, [(0, "w_in_2", C2_Q + 256 * i, 256)])

    def gated(branch, w):
        for i in range(4):
            add("pg", i, [(0, "w_in_2", C2_PG + D * branch + 256 * i, 256)])
            add("y", i, [(0, w, 256 * i, 256)])

    gated(2, "w_att_out_2")
    for i in range(4):
        add("gb", i, [(0, "w_in_2", C2_GB + 256 * i, 256)])
    for i in range(8):
        add("cv", i, [(0, "w_in_2", C2_GC + P * i, P), (P, "w_in_2", C2_VA + P * i, P)])
    gated(0, "w_a_out_2")
    gated(1, "w_b_out_2")
    for i in range(4):
        add("wo2", i, [(0, "w_o_2", 256 * i, 256)])
    for i in range(FC):
        add("up", i, [(0, "w_up_2", P * i, P), (P, "w_up_2", FF + P * i, P)])
    for i in range(4):
        for k0, nk in ((0, 8), (8, 8), (16, 6)):
            add("down", (i, k0), [(0, "w_down_2", 256 * i, 256)], nk, k0)
    return units


PARAM_ROWS = [("norm_g", 8), ("mu_r", 4), ("mu_k", 4), ("mu_v", 4), ("mu_wa", 1), ("w0", 4), ("a0", 4), ("k_k", 4),
              ("k_a", 4), ("r_k", 4), ("gn_g", 4), ("gn_b", 4), ("q_norm_g", 2), ("kv_norm_g", 1), ("kidx_g", 1),
              ("kidx_b", 1), ("final_g", 8), ("norm_mix_g_2", 8), ("norm_mem_g_2", 8), ("b_gate_2", 24),
              ("conv_b_bias_2", 8), ("ln_b_g_2", 8), ("ln_b_b_2", 8), ("norm_ffn_g_2", 8), ("norm_final_g_2", 8),
              ("conv_a_w_2", 24), ("conv_b_w_2", 248), ("conv_ffn_w_2", 132)]
PARAM_AT = {}
_at = 0
for _name, _rows in PARAM_ROWS:
    PARAM_AT[_name] = _at
    _at += _rows
PARAM_TILES = -(-_at // P)


def build(nc, dram, out):
    units = weight_units()
    NU = len(units)
    ctx = ExitStack()
    with ctx:
        base = -(-nc.sbuf_base // 32) * 32

        def at(name, offset, shape, dt=F32):
            return nc.alloc_sbuf_tensor_at(name, [P] + shape, dt, offset=base + offset)

        sems = {}

        def sem(name):
            if name not in sems:
                sems[name] = ctx.enter_context(nc.semaphore(name))
            return sems[name]

        w_raw = [at(f"w_raw{s}", 8192 * s, [CH, 256]) for s in range(2)]
        w_hi = [at(f"w_hi{s}", 16384 + 8192 * s, [CH, 256], F32R) for s in range(2)]
        w_lo = [at(f"w_lo{s}", 32768 + 8192 * s, [CH, 256], F32R) for s in range(2)]
        x_res = at("x_res", 49152, [CH, T])
        op_hi = at("op_hi", 81920, [CH, T], F32R)
        op_lo = at("op_lo", 98304, [CH, T], F32R)
        ident = at("ident", 114688, [P])
        ones = at("ones", 115200, [P])
        par = at("par", 115712, [PARAM_TILES * P])
        misc = at("misc", 118272, [128])
        S0 = 118784
        tmp = [at(f"tmp{i}", 124928 + 2176 * i, [544]) for i in range(3)]
        rs = at("rs", 131456, [T])
        R0 = 133504
        pair_ones = at("pair_ones", S0, [P])
        mask_ar = at("mask_ar", S0 + 512, [2, P])
        mask_lev = at("mask_lev", S0 + 1536, [7, P])
        mask_lowT = at("mask_lowT", S0 + 5120, [P])
        mask_low = at("mask_low", S0 + 5632, [P])
        x_tok = at("x_tok", R0, [NT, D])
        sq1 = at("sq1", R0 + 16384, [CH, T])
        par_rows = at("par_rows", R0 + 32768, [PARAM_TILES, P])
        ar = at("ar", R0, [NI, 2, T])
        bt = at("bt", R0 + 16384, [NI, T])
        kt = at("kt", R0 + 24576, [NI, T])
        vf = at("vf", R0 + 32768, [NI, T])
        gate_r = at("gate_r", R0 + 40960, [NI, T])
        gate_a = at("gate_a", R0 + 49152, [NI, T])
        tok = [[at(f"tok{j}_{s}", R0 + 57344 + 6144 * s + 2048 * j, [T]) for j in range(3)] for s in range(2)]
        lora = at("lora", R0 + 57344, [T])
        prep = [at(f"prep{j}", R0 + 59392 + 2080 * j, [4 * 129 + 4]) for j in range(4)]
        qd = at("qd", R0 + 69632, [2, T])
        ckv = at("ckv", R0 + 73728, [T])
        kidx = at("kidx", R0 + 75776, [T])
        bonus_v = at("bonus_v", 65536, [NI, T])
        y_scan = at("y_scan", 73728, [NI, T])
        g_b = at("g_b", 81920, [NH, 2, P])
        g_k = at("g_k", 90112, [NH, 2, P])
        low = at("low", 98304, [NH, P])
        inv = at("inv", 102400, [NH, P])
        invT = at("invT", 106496, [NH, P])
        wprod = at("wprod", 110592, [NH, P])
        state = at("state", R0 + 77824, [NI, HD])
        xs_t = [tmp[0][:, 0:256], tmp[0][:, 256:512]]
        us_t = [tmp[1][:, 0:256], tmp[1][:, 256:512]]
        wuq = at("wuq", 0, [2, 512])
        wqi = at("wqi", 4096, [2, 256])
        wuk = at("wuk", 6144, [512])
        probT = at("probT", 0, [NT, T])
        wukT = at("wukT", 8192, [NI, P])
        wuv = at("wuv", 10240, [512])
        qT = at("qT", 12288, [NI, T])
        qiT = at("qiT", 20480, [2, T])
        q_abs = [at(f"q_abs{s}", 24576 + 2048 * s, [T]) for s in range(2)]
        ckv_tok = at("ckv_tok", 28672, [NT, P])
        score = at("score", 30720, [NT, T])
        o_lat = [at(f"o_lat{s}", 38912 + 2048 * s, [T]) for s in range(2)]
        prob = [at(f"prob{s}", 43008 + 2048 * s, [T]) for s in range(2)]
        relu_t = [at(f"relu{s}", 47104, [T]) for s in range(1)]
        op2_hi = at("op2_hi", R0, [CH, T], F32R)
        op2_lo = at("op2_lo", R0 + 16384, [CH, T], F32R)
        memT = at("memT", R0 + 32768, [CH, MEM])
        mem_tok = at("mem_tok", R0 + 40960, [2, D])
        conv_b = at("conv_b", R0 + 32768, [CH, T])
        work = at("work", R0 + 49152, [CH, T])
        sq2 = at("sq2", R0 + 49152, [CH, T])
        gates = [at(f"gate{m}", R0 + 65536 + 2048 * m, [T]) for m in range(2)]
        prob2T = at("prob2T", R0 + 69632, [2, T])
        prob2 = [at(f"prob2_{s}", R0 + 73728 + 1024 * s, [MEM]) for s in range(2)]
        memK = at("memK", 65536, [CH, MEM])
        memV = at("memV", 73728, [2, D])
        merged = at("merged", 65536, [CH, T])
        pad_b = [at(f"pad_b{s}", S0 + 2304 * s, [KB - 1 + T]) for s in range(2)]
        pads = [at(f"pad{s}", S0 + 2112 * s, [KF - 1 + T]) for s in range(2)]
        act_hi = at("act_hi", R0, [FC, T], F32R)
        act_lo = at("act_lo", R0 + 45056, [16, T], F32R)
        act_lo2 = at("act_lo2", 65536, [FC - 16, T], F32R)
        sq3 = at("sq3", 81920, [CH, T])
        out_tok = [at(f"out_tok{s}", R0 + 4096 * s, [D]) for s in range(2)]

        omm = misc[:, 0:13]
        omka = misc[:, 13:17]
        w_idx = misc[:, 17:33]
        top8 = misc[:, 33:41]
        negmax = misc[:, 41:49]
        sums = misc[:, 49:57]
        rsum = misc[:, 57:65]
        dec = misc[:, 65:81]
        ps = [ctx.enter_context(nc.psum_tensor(f"bank{b}", [P, T], F32)) for b in range(BANKS)]

        def pcol(name, i=0):
            c = PARAM_AT[name] + i
            return par[:, c:c + 1]

        full = [sem(f"bank_full{b}") for b in range(BANKS)]
        free = [sem(f"bank_free{b}") for b in range(BANKS)]
        seq = {}

        def take(eng, key):
            n = seq[key]
            eng.wait_ge(full[n % BANKS], n // BANKS + 1)
            return ps[n % BANKS]

        def evac(ins, key):
            ins.then_inc(free[seq[key] % BANKS], 1)

        def evacuated(eng, key):
            n = seq[key]
            eng.wait_ge(free[n % BANKS], n // BANKS + 1)

        def filled(eng, key):
            n = seq[key]
            eng.wait_ge(full[n % BANKS], n // BANKS + 1)

        raw_count, tot = [], [0, 0]
        for u, (_, _, _, pieces) in enumerate(units):
            tot[u % 2] += 16 * len(pieces)
            raw_count.append(tot[u % 2])
        w_arrived = [sem("w_arrived0"), sem("w_arrived1")]
        hi_ready, lo_ready = sem("w_hi_ready"), sem("w_lo_ready")
        unit_last = {}
        first_phase2_unit = next(n for n, u in enumerate(units) if u[0] == "wout")

        par_src = []
        for name, n in PARAM_ROWS:
            if name.startswith("mu_"):
                j = ("mu_r", "mu_k", "mu_v", "mu_wa").index(name)
                src = dram["mu_shift"][0, 512 * j:512 * j + (512 if j < 3 else 64)]
                par_src.append((name, 0, src.rearrange("(n q) -> n q", n=n)))
            elif name in ("kidx_g", "kidx_b"):
                par_src += [(name, HD * d, dram[name]) for d in range(2)]
            elif name in ("final_g", "norm_final_g_2"):
                par_src.append((name, 0, dram[name].rearrange("(n q) -> n q", q=P)))
            elif name in ("conv_a_w_2", "conv_b_w_2", "conv_ffn_w_2"):
                par_src.append((name, 0, dram[name][0].rearrange("k (n q) -> (k n) q", q=P)))
            elif name in ("k_k", "k_a", "r_k", "gn_g", "gn_b"):
                par_src.append((name, 0, dram[name][0].rearrange("(n a) d -> n (a d)", a=2)))
            else:
                par_src.append((name, 0, dram[name][0].rearrange("(n q) -> n q", q=P)))
        par_dmas = []
        for name, col, src in par_src:
            row, n, a = PARAM_AT[name], src.shape[0], 0
            while a < n:
                tl, r = divmod(row + a, P)
                m = min(n - a, P - r)
                par_dmas.append((par_rows[r:r + m, tl, col:col + src.shape[1]], src[a:a + m, :]))
                a += m
        n_par_dmas = len(par_dmas)

        block = ctx.enter_context(nc.Block())

        @block.tensor
        def _(pe):
            count = [0]

            def bank(key):
                n = count[0]
                count[0] += 1
                assert key not in seq, key
                seq[key] = n
                if n >= BANKS:
                    pe.wait_ge(free[n % BANKS], n // BANKS)
                return ps[n % BANKS]

            def done(ins, key):
                ins.then_inc(full[seq[key] % BANKS], 1)

            def transposes(key, blocks, rows=P):
                b = bank(key)
                for j, src in enumerate(blocks):
                    mm = nc.tensor.transpose(b[:, j * P:j * P + rows], src, ident[0:rows, 0:rows])
                done(mm, key)

            def sum_chunks(key, sq, n, width, ready):
                b = bank(key)
                for c in range(n):
                    pe.wait_ge(sem(ready), c + 1)
                    mm = nc.tensor.matmul(b[:, 0:width], ones[:, :], sq[:, c, 0:width], start=c == 0, stop=c == n - 1)
                done(mm, key)

            unit = [0]

            def next_unit(what):
                u = unit[0]
                unit[0] += 1
                assert units[u][0] == what, (units[u], what)
                pe.wait_ge(hi_ready, u + 1)
                pe.wait_ge(lo_ready, u + 1)
                return u

            def tile(b, u, col, width, xh, xl, x0=0, start=True, stop=True):
                wh, wl, nk = w_hi[u % 2], w_lo[u % 2], units[u][2]
                for k in range(nk):
                    h, l = wh[:, k, col:col + P], wl[:, k, col:col + P]
                    nc.tensor.matmul(b[:, 0:width], h, xh[:, x0 + k, 0:width], start=start and k == 0, stop=False)
                    nc.tensor.matmul(b[:, 0:width], h, xl(x0 + k, width), start=False, stop=False)
                    mm = nc.tensor.matmul(b[:, 0:width], l, xh[:, x0 + k, 0:width], start=False,
                                          stop=stop and k == nk - 1)
                return mm

            def plain(t):
                return lambda k, width: t[:, k, 0:width]

            def unit_tiles(what, i, xh, xl, width=T, tiles=2):
                u = next_unit(what)
                for m in range(tiles):
                    b = bank((what, i, m))
                    done(tile(b, u, m * P, width, xh, xl), (what, i, m))
                unit_last[u] = (what, i, tiles - 1)

            pe.wait_ge(sem("consts"), 2)
            pe.wait_ge(sem("par_loaded"), 16 * n_par_dmas)
            transposes(("par", 0), [par_rows[:, j, :] for j in range(4)])
            transposes(("par", 1), [par_rows[:, j, :] for j in range(4, PARAM_TILES)])
            pe.wait_ge(sem("x_loaded"), 16)
            for c in range(CH):
                transposes(("xT", c), [x_tok[:, t, c * P:c * P + P] for t in range(NT)])
            sum_chunks("ss_x", sq1, CH, T, "sq_x")

            pe.wait_ge(sem("xn_ready"), CH)
            oh, ol = op_hi, plain(op_lo)
            unit_tiles("qd", 0, oh, ol)
            unit_tiles("kvi", 0, oh, ol)
            unit_tiles("wa", 0, oh, ol, tiles=1)
            for half in range(2):
                for what in "rkvg":
                    unit_tiles(what, half, oh, ol)
            for half in range(2):
                unit_tiles("ga", half, oh, ol)

            pe.wait_ge(sem("lora_loaded"), 32)
            pe.wait_ge(sem("tanh_ready"), 1)
            evacuated(pe, ("wa", 0, 0))
            pe.wait_ge(sem("consts"), 7)
            transposes("w_idx", [tmp[2][:, t * P:t * P + P] for t in range(NT)])
            for i in range(NI):
                b = bank(("z", i))
                done(nc.tensor.matmul(b[:, :], lora[0:32, i * P:i * P + P], tmp[2][0:32, 0:T], start=True, stop=True), ("z", i))
                b = bank(("a", i))
                done(nc.tensor.matmul(b[:, :], lora[32:64, i * P:i * P + P], tmp[2][32:64, 0:T], start=True, stop=True), ("a", i))
                b = bank(("kk", i))
                pe.wait_ge(sem("kk_sq"), i + 1)
                done(nc.tensor.matmul(b[:, :], pair_ones[:, :], prep[3][:, 0:T], start=True, stop=True), ("kk", i))
                b = bank(("bonus", i))
                pe.wait_ge(sem("rk_ready"), i + 1)
                done(nc.tensor.matmul(b[:, :], pair_ones[:, :], prep[3][:, 0:T], start=True, stop=True), ("bonus", i))

            pe.wait_ge(sem("prep_ready"), NI)
            for c in range(NT):
                cs = slice(c * P, c * P + P)
                for j, src in enumerate((vf, bt, kt)):
                    transposes(("tok", c, j), [src[:, i, cs] for i in range(NI)])
                for odd in range(2):
                    rows = slice(HD * odd, HD * odd + HD)
                    for name, stat in (("gb", bt), ("gk", kt)):
                        for i2 in range(2):
                            b = bank((name, c, odd, i2))
                            for n in range(2):
                                i = 2 * i2 + n
                                mm = nc.tensor.matmul(b[:, n * 256:n * 256 + 256], stat[rows, i, cs], ar[rows, i, :, cs],
                                                      start=True, stop=True)
                            done(mm, (name, c, odd, i2))
                    b = bank(("low", c, odd))
                    for i in range(NI):
                        mm = nc.tensor.matmul(b[:, i * P:i * P + P], ar[rows, i, 0, cs], bt[rows, i, cs], start=True, stop=True)
                    done(mm, ("low", c, odd))
                for lev in range(1, 7):
                    for odd in range(2):
                        hs = slice(NI * odd, NI * odd + NI)
                        if lev == 1:
                            pe.wait_ge(sem(f"inv_init{odd}"), c + 1)
                        else:
                            evacuated(pe, ("dinv", c, lev - 1, odd))
                            evacuated(pe, ("dinvT", c, lev - 1, odd))
                        b = bank(("w", c, lev, odd))
                        for i in range(NI):
                            h = NI * odd + i
                            mm = nc.tensor.matmul(b[:, i * P:i * P + P], low[:, h, :], inv[:, h, :], start=True, stop=True)
                        done(mm, ("w", c, lev, odd))
                    for odd in range(2):
                        evacuated(pe, ("w", c, lev, odd))
                        b = bank(("dinv", c, lev, odd))
                        for i in range(NI):
                            h = NI * odd + i
                            mm = nc.tensor.matmul(b[:, i * P:i * P + P], invT[:, h, :], wprod[:, h, :], start=True, stop=True)
                        done(mm, ("dinv", c, lev, odd))
                        if lev < 6:
                            b = bank(("dinvT", c, lev, odd))
                            for i in range(NI):
                                h = NI * odd + i
                                mm = nc.tensor.matmul(b[:, i * P:i * P + P], wprod[:, h, :], invT[:, h, :], start=True, stop=True)
                            done(mm, ("dinvT", c, lev, odd))
                V, B, K = tok[c % 2]
                for j in range(3):
                    evacuated(pe, ("tok", c, j))
                for odd in range(2):
                    for i2 in range(2):
                        evacuated(pe, ("gb", c, odd, i2))
                        evacuated(pe, ("gk", c, odd, i2))
                for odd in range(2):
                    rows = slice(HD * odd, HD * odd + HD)
                    if c > 0:
                        evacuated(pe, ("p", c - 1, odd))
                    b = bank(("scan_x", c, odd))
                    for i in range(NI):
                        h, f = NI * odd + i, P * i + HD * odd
                        if c > 0:
                            nc.tensor.matmul(b[:, i * HD:i * HD + HD], ar[rows, i, 0, cs], state[rows, i, :], start=True, stop=False)
                        mm = nc.tensor.matmul(b[:, i * HD:i * HD + HD], g_k[:, h, 0, :], V[:, f:f + HD], start=c == 0, stop=True)
                    done(mm, ("scan_x", c, odd))
                for odd in range(2):
                    evacuated(pe, ("dinv", c, 6, odd))
                    evacuated(pe, ("scan_x", c, odd))
                    b = bank(("scan_u", c, odd))
                    for i in range(NI):
                        h = NI * odd + i
                        mm = nc.tensor.matmul(b[:, i * HD:i * HD + HD], inv[:, h, :], xs_t[odd][:, i * HD:i * HD + HD], start=True, stop=True)
                    done(mm, ("scan_u", c, odd))
                for odd in range(2):
                    rows = slice(HD * odd, HD * odd + HD)
                    evacuated(pe, ("scan_u", c, odd))
                    b = bank(("yT", c, odd))
                    for i in range(NI):
                        h, f = NI * odd + i, P * i + HD * odd
                        o = b[rows, i * P:i * P + P]
                        if c > 0:
                            nc.tensor.matmul(o, state[rows, i, :], ar[rows, i, 1, cs], start=True, stop=False)
                        nc.tensor.matmul(o, us_t[odd][:, i * HD:i * HD + HD], g_b[:, h, 1, :], start=c == 0, stop=False)
                        mm = nc.tensor.matmul(o, V[:, f:f + HD], g_k[:, h, 1, :], start=False, stop=True)
                    done(mm, ("yT", c, odd))
                    if c < NT - 1:
                        b = bank(("p", c, odd))
                        for i in range(NI):
                            h, f = NI * odd + i, P * i + HD * odd
                            o = b[rows, i * HD:i * HD + HD]
                            if c > 0:
                                nc.tensor.matmul(o, ident[rows, rows], state[rows, i, :], start=True, stop=False)
                            nc.tensor.matmul(o, B[:, f:f + HD], us_t[odd][:, i * HD:i * HD + HD], start=c == 0, stop=False)
                            mm = nc.tensor.matmul(o, K[:, f:f + HD], V[:, f:f + HD], start=False, stop=True)
                        done(mm, ("p", c, odd))
            for i in range(NI):
                for odd in range(2):
                    evacuated(pe, ("yT", NT - 1, odd))
                b = bank(("gn_mean", i))
                done(nc.tensor.matmul(b[:, :], pair_ones[:, :], y_scan[:, i, :], start=True, stop=True), ("gn_mean", i))
                pe.wait_ge(sem("gn_sq"), i + 1)
                b = bank(("gn_var", i))
                done(nc.tensor.matmul(b[:, :], pair_ones[:, :], tmp[1][:, 0:T], start=True, stop=True), ("gn_var", i))

            pe.wait_ge(sem("sq_q"), 2)
            b = bank("ss_q")
            for m in range(2):
                mm = nc.tensor.matmul(b[:, :], ones[:, :], prob[m][:, :], start=m == 0, stop=m == 1)
            done(mm, "ss_q")
            pe.wait_ge(sem("sq_kv"), 1)
            b = bank("ss_kv")
            done(nc.tensor.matmul(b[:, :], ones[:, :], relu_t[0][:, :], start=True, stop=True), "ss_kv")
            b = bank("ki_mean")
            done(nc.tensor.matmul(b[:, :], pair_ones[:, :], kidx[:, :], start=True, stop=True), "ki_mean")
            pe.wait_ge(sem("ki_sq"), 1)
            b = bank("ki_var")
            done(nc.tensor.matmul(b[:, :], pair_ones[:, :], o_lat[0][:, :], start=True, stop=True), "ki_var")
            pe.wait_ge(sem("dsa_w"), 16 * 4)
            transposes("wukT", [wuk[:, i * P:i * P + P] for i in range(NI)])
            pe.wait_ge(sem("cq_ready"), 2)
            for i in range(NI):
                b = bank(("q", i))
                for m in range(2):
                    mm = nc.tensor.matmul(b[:, :], wuq[:, m, i * P:i * P + P], qd[:, m, :], start=m == 0, stop=m == 1)
                done(mm, ("q", i))
            for i in range(2):
                b = bank(("qi", i))
                for m in range(2):
                    mm = nc.tensor.matmul(b[:, :], wqi[:, m, i * P:i * P + P], qd[:, m, :], start=m == 0, stop=m == 1)
                done(mm, ("qi", i))
            pe.wait_ge(sem("ckv_ready"), 1)
            transposes("ckv_tok", [ckv[:, t * P:t * P + P] for t in range(NT)])
            pe.wait_ge(sem("kidx_ready"), 1)
            for i in range(2):
                evacuated(pe, ("qi", i))
            for qt in range(1, NT):
                for h in range(4):
                    rows = slice(HD * (h % 2), HD * (h % 2) + HD)
                    b = bank(("lg", qt, h))
                    done(nc.tensor.matmul(b[:, 0:P * (qt + 1)], qiT[rows, h // 2, qt * P:qt * P + P], kidx[rows, 0:P * (qt + 1)],
                                          start=True, stop=True), ("lg", qt, h))
            for i in range(NI):
                evacuated(pe, ("q", i))
            evacuated(pe, "wukT")
            evacuated(pe, "ckv_tok")
            for h in range(NH):
                rows = slice(HD * (h % 2), HD * (h % 2) + HD)
                b = bank(("qa", h))
                done(nc.tensor.matmul(b[:, :], wukT[rows, h // 2, :], qT[rows, h // 2, :], start=True, stop=True), ("qa", h))
                evacuated(pe, ("qa", h))
                for qt in range(NT):
                    b = bank(("s", h, qt))
                    done(nc.tensor.matmul(b[:, 0:P * (qt + 1)], q_abs[h % 2][:, qt * P:qt * P + P], ckv[:, 0:P * (qt + 1)],
                                          start=True, stop=True), ("s", h, qt))
                for qt in range(NT):
                    pe.wait_ge(sem("prob_ready"), NT * h + qt + 1)
                    transposes(("pT", h, qt), [prob[qt % 2][:, k * P:k * P + P] for k in range(qt + 1)])
                for qt in range(NT):
                    evacuated(pe, ("pT", h, qt))
                b = bank(("ol", h))
                for k in range(NT):
                    mm = nc.tensor.matmul(b[:, k * P:T], ckv_tok[:, k, :], probT[:, k, k * P:T], start=k == 0, stop=k == NT - 1)
                done(mm, ("ol", h))
                evacuated(pe, ("ol", h))
                b = bank(("o", h))
                done(nc.tensor.matmul(b[rows, :], wuv[:, h * HD:h * HD + HD], o_lat[h % 2][:, :], start=True, stop=True), ("o", h))

            pe.wait_ge(sem("mix_ready"), CH)
            for i in range(4):
                unit_tiles("wout", i, oh, ol)
            pe.wait_ge(sem("mem_loaded"), 16)
            for c in range(CH):
                transposes(("memT", c), [mem_tok[:, t, c * P:c * P + P] for t in range(2)])
            sum_chunks("ss_mem", sq2, CH, MEM, "sq_mem")
            pe.wait_ge(sem("memn_ready"), CH)
            mh, ml = op2_hi, plain(op2_lo)
            for i in range(4):
                unit_tiles("kT", i, mh, ml, MEM)
            for i in range(4):
                u = next_unit("vm")
                b = bank(("vm", i))
                for t in range(2):
                    o = b[:, t * 256:t * 256 + 256]
                    for k in range(CH):
                        h, l = mh[:, k, t * P:t * P + P], op2_lo[:, k, t * P:t * P + P]
                        nc.tensor.matmul(o, h, w_hi[u % 2][:, k, :], start=k == 0, stop=False)
                        nc.tensor.matmul(o, h, w_lo[u % 2][:, k, :], start=False, stop=False)
                        mm = nc.tensor.matmul(o, l, w_hi[u % 2][:, k, :], start=False, stop=k == CH - 1)
                done(mm, ("vm", i))
                unit_last[u] = ("vm", i)
            sum_chunks("ss_y", sq2, CH, T, "sq_y")
            sum_chunks("ss_mix", sq2, CH, T, "sq_mix")
            pe.wait_ge(sem("mixn_ready"), CH)
            for i in range(8):
                unit_tiles("u", i, oh, ol)
            for i in range(4):
                unit_tiles("q2", i, oh, ol)
            for h in range(MH):
                evacuated(pe, ("q2", h, 1))
                evacuated(pe, ("q2", h, 0))
                for m in range(2):
                    evacuated(pe, ("kT", h, m))
                evacuated(pe, ("vm", h))
                for qt in range(NT):
                    b = bank(("s2", h, qt))
                    for k in range(2):
                        mm = nc.tensor.matmul(b[:, 0:MEM], work[:, 2 * h + k, qt * P:qt * P + P], memK[:, 2 * h + k, :],
                                              start=k == 0, stop=k == 1)
                    done(mm, ("s2", h, qt))
                for qt in range(NT):
                    pe.wait_ge(sem("prob2_ready"), NT * h + qt + 1)
                    transposes(("p2T", h, qt), [prob2[qt % 2][:, k * P:k * P + P] for k in range(2)])
                for qt in range(NT):
                    evacuated(pe, ("p2T", h, qt))
                for d in range(2):
                    b = bank(("oc", h, d))
                    for k in range(2):
                        mm = nc.tensor.matmul(b[:, :], memV[:, k, 256 * h + P * d:256 * h + P * d + P], prob2T[:, k, :],
                                              start=k == 0, stop=k == 1)
                    done(mm, ("oc", h, d))

            def gated(branch):
                if branch == 2:
                    for h in range(MH):
                        for d in range(2):
                            evacuated(pe, ("oc", h, d))
                else:
                    pe.wait_ge(sem(f"op2_ready{branch}"), CH)
                for i in range(4):
                    u = next_unit("pg")
                    for m in range(2):
                        b = bank(("pg", branch, i, m))
                        done(tile(b, u, m * P, T, oh, ol), ("pg", branch, i, m))
                    unit_last[u] = ("pg", branch, i, 1)
                    u = next_unit("y")
                    for m in range(2):
                        b = bank(("y", branch, i, m))
                        done(tile(b, u, m * P, T, mh, ml), ("y", branch, i, m))
                    unit_last[u] = ("y", branch, i, 1)

            gated(2)
            for i in range(4):
                unit_tiles("gb", i, oh, ol)
            for i in range(8):
                unit_tiles("cv", i, oh, ol)
            gated(0)
            b = bank("ln_mean")
            for c in range(CH):
                pe.wait_ge(sem("conv_ready"), c + 1)
                mm = nc.tensor.matmul(b[:, :], ones[:, :], conv_b[:, c, :], start=c == 0, stop=c == CH - 1)
            done(mm, "ln_mean")
            sum_chunks("ln_var", sq2, CH, T, "sq_ln")
            gated(1)
            pe.wait_ge(sem("merged_ready"), CH)
            for i in range(4):
                unit_tiles("wo2", i, oh, ol)
            sum_chunks("ss_ffn", sq2, CH, T, "sq_ffn")
            pe.wait_ge(sem("ffn_ready"), CH)
            for i in range(FC):
                unit_tiles("up", i, oh, ol)
            pe.wait_ge(sem("act_ready"), FC)
            for i in range(4):
                bs = None
                for k0 in (0, 8, 16):
                    u = next_unit("down")
                    if bs is None:
                        bs = [bank(("down", i, m)) for m in range(2)]
                    for m in range(2):
                        mm = tile(bs[m], u, m * P, T, act_hi,
                                  lambda k, w: act_lo[:, k, 0:w] if k < 16 else act_lo2[:, k - 16, 0:w],
                                  x0=k0, start=k0 == 0, stop=k0 == 16)
                        if k0 == 16:
                            done(mm, ("down", i, m))
                    if k0 < 16:
                        mm.then_inc(sem("down_used"), 1)
                        unit_last[u] = ("down_used", 2 * i + k0 // 8 + 1)
                    else:
                        unit_last[u] = ("down", i, 1)
            sum_chunks("ss_fin", sq3, CH, T, "sq_fin")
            pe.wait_ge(sem("fin_ready"), CH)
            for t in range(NT):
                for g in range(2):
                    transposes(("out", t, g), [x_res[:, 4 * g + j, t * P:t * P + P] for j in range(4)])
            assert unit[0] == NU

        def slot_used(eng, u):
            key = unit_last[u]
            if key[0] == "down_used":
                eng.wait_ge(sem("down_used"), key[1])
            else:
                filled(eng, key)

        @block.sync
        def _(sp):
            x_d = dram["x"][0].rearrange("(t p) d -> p t d", p=P)
            sp.dma_start(x_tok[:, :, :], x_d).then_inc(sem("x_loaded"), 16)

            def load(u):
                _, _, nk, pieces = units[u]
                if u >= 2:
                    sp.wait_ge(hi_ready, u - 1)
                    sp.wait_ge(lo_ready, u - 1)
                for at_, w, col, n, k0 in pieces:
                    src = dram[w][0, k0 * P:(k0 + nk) * P, col:col + n].rearrange("(k p) n -> p k n", p=P)
                    sp.dma_start(w_raw[u % 2][:, 0:nk, at_:at_ + n], src).then_inc(w_arrived[u % 2], 16)

            for u in range(first_phase2_unit):
                load(u)
            for u in (first_phase2_unit - 2, first_phase2_unit - 1):
                sp.wait_ge(hi_ready, u + 1)
                sp.wait_ge(lo_ready, u + 1)
                slot_used(sp, u)
            dw = sem("dsa_w")
            sp.dma_start(wuq[:, :, :], dram["w_uq"][0].rearrange("(m p) n -> p m n", p=P)).then_inc(dw, 16)
            sp.dma_start(wqi[:, :, :], dram["w_qidx"][0].rearrange("(m p) n -> p m n", p=P)).then_inc(dw, 16)
            sp.dma_start(wuk[:, :].rearrange("p (h d) -> p h d", d=HD), dram["w_uk"][0].rearrange("h r d -> r h d")).then_inc(dw, 16)
            sp.dma_start(wuv[:, :].rearrange("p (h d) -> p h d", d=HD), dram["w_uv"][0].rearrange("h r d -> r h d")).then_inc(dw, 16)
            evacuated(sp, ("o", NH - 1))
            for u in range(first_phase2_unit, NU):
                if units[u][0] == "kT" and units[u][1] == 0:
                    sp.wait_ge(sem("mix_ready"), CH)
                    sp.dma_start(mem_tok[:, :, :], dram["mem_2"][0].rearrange("(t p) d -> p t d", p=P)).then_inc(sem("mem_loaded"), 16)
                load(u)
            for t in range(NT):
                evacuated(sp, ("out", t, 0))
                evacuated(sp, ("out", t, 1))
                sp.dma_start(out[0, t * P:t * P + P, :], out_tok[t % 2][:, :]).then_inc(sem(f"stored{t % 2}"), 16)
            for t in range(2):
                sp.wait_ge(sem(f"stored{t}"), 16 * NT // 2)

        @block.gpsimd
        def _(pool):
            steps = [0]

            def step(ins):
                steps[0] += 1
                ins.then_inc(sem("pool_steps"), 1)
                pool.wait_ge(sem("pool_steps"), steps[0])

            step(nc.gpsimd.memset(par_rows[:, :, :], 0.0))
            nc.gpsimd.memset(ones[:, :], 1.0).then_inc(sem("consts"), 1)
            pool.wait_ge(sem("consts"), 1)
            nc.gpsimd.affine_select(out=ident[:, :], in_=ones[:, :], compare_op=ALU.is_equal, fill=0.0, base=0,
                                    pattern=[[-1, P]], channel_multiplier=1).then_inc(sem("consts"), 1)
            pool.wait_ge(sem("consts"), 2)
            step(nc.gpsimd.memset(pair_ones[:, :], 0.0))
            step(nc.gpsimd.memset(pair_ones[0:HD, 0:HD], 1.0))
            nc.gpsimd.memset(pair_ones[HD:P, HD:P], 1.0).then_inc(sem("consts"), 1)
            pool.wait_ge(sem("consts"), 3)
            nc.gpsimd.affine_select(out=mask_ar[:, 0, :], in_=ones[:, :], compare_op=ALU.is_gt, fill=0.0, base=0,
                                    pattern=[[1, P]], channel_multiplier=-1).then_inc(sem("consts"), 1)
            pool.wait_ge(sem("consts"), 4)
            nc.gpsimd.affine_select(out=mask_ar[:, 1, :], in_=ones[:, :], compare_op=ALU.is_ge, fill=0.0, base=0,
                                    pattern=[[1, P]], channel_multiplier=-1).then_inc(sem("consts"), 1)
            pool.wait_ge(sem("consts"), 5)
            nc.gpsimd.affine_select(out=mask_low[:, :], in_=ones[:, :], compare_op=ALU.is_gt, fill=0.0, base=0,
                                    pattern=[[-1, P]], channel_multiplier=1).then_inc(sem("consts"), 1)
            pool.wait_ge(sem("consts"), 6)
            step(nc.gpsimd.memset(mask_lev[:, :, :], 0.0))
            for n in range(7):
                b = 1 << n
                v = mask_lev[:, n, :].rearrange("p (k h c) -> p k h c", h=2, c=b)[:, :, 1, :]
                step(nc.gpsimd.memset(v, 1.0))
                step(nc.gpsimd.affine_select(out=v, in_=v, compare_op=ALU.is_ge, fill=0.0, base=0,
                                             pattern=[[-2 * b, P // (2 * b)], [0, b]], channel_multiplier=1))
                step(nc.gpsimd.affine_select(out=v, in_=v, compare_op=ALU.is_ge, fill=0.0, base=b - 1,
                                             pattern=[[2 * b, P // (2 * b)], [0, b]], channel_multiplier=-1))
            step(nc.gpsimd.memset(mask_lowT[:, :], 0.0))
            v = mask_lowT[:, :].rearrange("p (k h) -> p k h", h=2)[:, :, 0]
            step(nc.gpsimd.memset(v, 1.0))
            nc.gpsimd.affine_select(out=v, in_=v, compare_op=ALU.is_equal, fill=0.0, base=-1,
                                    pattern=[[-2, P // 2]], channel_multiplier=1).then_inc(sem("consts"), 1)
            pool.wait_ge(sem("consts"), 7)
            v = score[:, 0, 0:P]
            slot_used(pool, first_phase2_unit - 2)
            slot_used(pool, first_phase2_unit - 1)
            step(nc.gpsimd.memset(v, 0.0))
            nc.gpsimd.affine_select(out=v, in_=v, compare_op=ALU.is_ge, fill=MASKED, base=0,
                                    pattern=[[-1, P]], channel_multiplier=1).then_inc(sem("causal"), 1)
            pool.wait_ge(sem("causal"), 1)
            for qt in range(1, NT):
                v = score[:, qt, qt * P:qt * P + P]
                pool.wait_ge(sem("score_ready"), qt)
                nc.gpsimd.affine_select(out=v, in_=v, compare_op=ALU.is_ge, fill=MASKED, base=0,
                                        pattern=[[-1, P]], channel_multiplier=1).then_inc(sem("causal"), 1)

        @block.scalar
        def _(act):
            A = nc.scalar.activation
            split = [0]

            def split_hi(upto):
                while split[0] <= min(upto, NU - 1):
                    u = split[0]
                    split[0] += 1
                    nk = units[u][2]
                    act.wait_ge(w_arrived[u % 2], raw_count[u])
                    if u >= 2:
                        slot_used(act, u - 2)
                    A(w_hi[u % 2][:, 0:nk, :], w_raw[u % 2][:, 0:nk, :], ACT.Copy).then_inc(hi_ready, 1)

            roots = [0]

            def root():
                roots[0] += 1
                act.wait_ge(sem("var_ready"), roots[0])
                A(rs[:, :], rs[:, :], ACT.Sqrt).then_inc(sem("rs_ready"), 1)

            act.wait_ge(sem("pool_steps"), 1)
            for dst, src in par_dmas:
                act.dma_start(dst, src).then_inc(sem("par_loaded"), 16)
            for c in range(CH):
                b = take(act, ("xT", c))
                A(sq1[:, c, :], b[:, :], ACT.Square).then_inc(sem("sq_x"), 1)
                evac(A(x_res[:, c, :], b[:, :], ACT.Copy), ("xT", c))
            split_hi(1)
            root()
            filled(act, ("xT", CH - 1))
            filled(act, "ss_x")
            act.dma_start(lora[0:32, :], dram["w_up"][0]).then_inc(sem("lora_loaded"), 16)
            act.dma_start(lora[32:64, :], dram["a_up"][0]).then_inc(sem("lora_loaded"), 16)

            for m in range(2):
                evac(A(qd[:, m, :], take(act, ("qd", 0, m))[:, :], ACT.Copy), ("qd", 0, m))
            split_hi(2)
            evac(A(ckv[:, :], take(act, ("kvi", 0, 0))[:, :], ACT.Copy), ("kvi", 0, 0))
            evac(A(kidx[:, :], take(act, ("kvi", 0, 1))[:, :], ACT.Copy), ("kvi", 0, 1))
            split_hi(3)
            act.wait_ge(sem("derived"), 1)

            def unshifted(key, dst, col):
                A(dst, take(act, key)[:, :], ACT.Copy, scale=omm[:, col:col + 1]).then_inc(sem("unshifted"), 1)

            unshifted(("wa", 0, 0), tmp[2][:, 0:T], 12)
            split_hi(4)
            evacuated(act, ("wa", 0, 0))
            A(tmp[2][0:32, 0:T], tmp[2][0:32, 0:T], ACT.Tanh).then_inc(sem("tanh_ready"), 1)
            u = 3
            last = None
            for half in range(2):
                for w, dst in enumerate((lambda i: ar[:, i, 1, :], lambda i: kt[:, i, :], lambda i: vf[:, i, :])):
                    for m in range(2):
                        i = 2 * half + m
                        unshifted(("rkv"[w], half, m), dst(i), 4 * w + i)
                    u += 1
                    split_hi(u + 1)
                for m in range(2):
                    b = take(act, ("g", half, m))
                    if half:
                        evacuated(act, ("g", 0, m))
                    A(tmp[m][:, 0:T], b[:, :], ACT.Sigmoid).then_inc(sem("sig_g"), 1)
                u += 1
                split_hi(u + 1)
            for half in range(2):
                for m in range(2):
                    b = take(act, ("ga", half, m))
                    evacuated(act, ("ga", 0, m) if half else ("g", 1, m))
                    A(tmp[m][:, 0:T], b[:, :], ACT.Sigmoid).then_inc(sem("sig_g"), 1)
                u += 1
                split_hi(min(u + 1, first_phase2_unit - 1))

            for i in range(NI):
                if i:
                    act.wait_ge(sem("prep_ready"), i)
                evac(A(prep[0][:, 0:T], take(act, ("z", i))[:, :], ACT.Sigmoid, bias=pcol("w0", i)), ("z", i))
                evac(A(prep[1][:, 0:T], take(act, ("a", i))[:, :], ACT.Sigmoid, bias=pcol("a0", i)), ("a", i))
                if i:
                    filled(act, ("bonus", i - 1))
                else:
                    evacuated(act, ("k", 0, 0))
                A(prep[3][:, 0:T], kt[:, i, :], ACT.Square, scale=pcol("k_k", i)).then_inc(sem("kk_sq"), 1)
                evac(A(rs[:, :], take(act, ("kk", i))[:, :], ACT.Sqrt), ("kk", i))
                act.wait_ge(sem("cum_ready"), i + 1)
                A(tmp[0][:, 0:516], prep[2][:, 0:516], ACT.Exp, scale=-KAPPA).then_inc(sem("exps"), 1)
                A(tmp[1][:, 0:516], prep[2][:, 0:516], ACT.Exp, scale=KAPPA).then_inc(sem("exps"), 1)

            act.wait_ge(sem("prep_ready"), NI)
            for c in range(NT):
                for j in range(3):
                    evac(A(tok[c % 2][j][:, :], take(act, ("tok", c, j))[:, :], ACT.Copy), ("tok", c, j))
                for odd in range(2):
                    evac(A(xs_t[odd], take(act, ("scan_x", c, odd))[:, 0:256], ACT.Copy), ("scan_x", c, odd))
                for odd in range(2):
                    evac(A(us_t[odd], take(act, ("scan_u", c, odd))[:, 0:256], ACT.Copy), ("scan_u", c, odd))
                for odd in range(2):
                    rows = slice(HD * odd, HD * odd + HD)
                    b = take(act, ("yT", c, odd))
                    evac(A(y_scan[rows, :, c * P:c * P + P], b[rows, :].rearrange("p (i t) -> p i t", i=NI), ACT.Copy),
                         ("yT", c, odd))
            for i in range(NI):
                evacuated(act, ("gn_mean", i))
                A(tmp[1][:, 0:T], tmp[0][:, 0:T], ACT.Square).then_inc(sem("gn_sq"), 1)
                root()

            for m in range(2):
                slot_used(act, first_phase2_unit - 2 + m)
            for m in range(2):
                A(prob[m][:, :], qd[:, m, :], ACT.Square).then_inc(sem("sq_q"), 1)
            A(relu_t[0][:, :], ckv[:, :], ACT.Square).then_inc(sem("sq_kv"), 1)
            root()
            root()
            evacuated(act, "ki_mean")
            A(o_lat[0][:, :], kidx[:, :], ACT.Square).then_inc(sem("ki_sq"), 1)
            root()
            evac(A(wukT[:, :, :], take(act, "wukT")[:, :].rearrange("p (i r) -> p i r", i=NI), ACT.Copy), "wukT")
            for i in range(NI):
                evac(A(qT[:, i, :], take(act, ("q", i))[:, :], ACT.Copy), ("q", i))
            for i in range(2):
                evac(A(qiT[:, i, :], take(act, ("qi", i))[:, :], ACT.Copy), ("qi", i))
            evac(A(ckv_tok[:, :, :], take(act, "ckv_tok")[:, :].rearrange("p (i r) -> p i r", i=NT), ACT.Copy), "ckv_tok")
            n = 0
            for qt in range(1, NT):
                for h in range(4):
                    if n:
                        act.wait_ge(sem("relu_used"), n)
                    n += 1
                    w = P * (qt + 1)
                    evac(A(relu_t[0][:, 0:w], take(act, ("lg", qt, h))[:, 0:w], ACT.Relu), ("lg", qt, h))
            for h in range(NH):
                evac(A(q_abs[h % 2][:, :], take(act, ("qa", h))[:, :], ACT.Copy, scale=HD ** -0.5), ("qa", h))
                for qt in range(NT):
                    act.wait_ge(sem("max_ready"), NT * h + qt + 1)
                    p = prob[qt % 2][:, 0:P * (qt + 1)]
                    A(p, p, ACT.Exp, bias=negmax[:, qt:qt + 1], accum_out=sums[:, qt:qt + 1]).then_inc(sem("exp_ready"), 1)
                evac(A(o_lat[h % 2][:, :], take(act, ("ol", h))[:, :], ACT.Copy), ("ol", h))

            act.wait_ge(sem("mix_ready"), CH)
            u = first_phase2_unit
            split_hi(u + 1)

            def after_unit():
                nonlocal u
                split_hi(u + 2)
                u += 1

            for i in range(4):
                filled(act, ("wout", i, 1))
                after_unit()
            for c in range(CH):
                b = take(act, ("memT", c))
                A(sq2[:, c, 0:MEM], b[:, 0:MEM], ACT.Square).then_inc(sem("sq_mem"), 1)
                evac(A(memT[:, c, :], b[:, 0:MEM], ACT.Copy), ("memT", c))
            root()
            for i in range(4):
                for m in range(2):
                    evac(A(memK[:, 2 * i + m, :], take(act, ("kT", i, m))[:, 0:MEM], ACT.Copy), ("kT", i, m))
                after_unit()
            for i in range(4):
                b = take(act, ("vm", i))
                evac(A(memV[:, :, 256 * i:256 * i + 256], b[:, :].rearrange("p (t n) -> p t n", t=2), ACT.Copy), ("vm", i))
                after_unit()
            for i in range(4):
                for m in range(2):
                    evacuated(act, ("wout", i, m))
            for c in range(CH):
                A(sq2[:, c, :], x_res[:, c, :], ACT.Square).then_inc(sem("sq_y"), 1)
            root()
            for c in range(CH):
                act.wait_ge(sem("x1_ready"), c + 1)
                if c == 0:
                    filled(act, "ss_y")
                A(sq2[:, c, :], x_res[:, c, :], ACT.Square).then_inc(sem("sq_mix"), 1)
            root()
            for i in range(8):
                if i:
                    evacuated(act, ("u", i - 1, 0))
                evac(A(tmp[0][:, 0:T], take(act, ("u", i, 1))[:, :], ACT.Sigmoid), ("u", i, 1))
                after_unit()
            for i in range(4):
                for m in range(2):
                    evac(A(work[:, 2 * i + m, :], take(act, ("q2", i, m))[:, :], ACT.Copy), ("q2", i, m))
                after_unit()
            for h in range(MH):
                for qt in range(NT):
                    n = NT * h + qt
                    act.wait_ge(sem("max2_ready"), n + 1)
                    if n >= 2:
                        filled(act, ("p2T", (n - 2) // NT, (n - 2) % NT))
                    b = take(act, ("s2", h, qt))
                    evac2 = A(prob2[qt % 2][:, :], b[:, 0:MEM], ACT.Exp, scale=1.0 / 16, bias=negmax[:, qt:qt + 1],
                              accum_out=sums[:, qt:qt + 1])
                    evac(evac2, ("s2", h, qt))

            def gate_steps(branch, before):
                for i in range(4):
                    for m in range(2):
                        if i:
                            evacuated(act, ("y", branch, i - 1, m))
                        elif before is not None:
                            evacuated(act, ("y", before, 3, m))
                        evac(A(gates[m][:, :], take(act, ("pg", branch, i, m))[:, :], ACT.Sigmoid,
                               bias=pcol("b_gate_2", 8 * branch + 2 * i + m)), ("pg", branch, i, m))
                    after_unit()
                    filled(act, ("y", branch, i, 1))
                    after_unit()

            gate_steps(2, None)
            for i in range(4):
                for m in range(2):
                    evac(A(work[:, 2 * i + m, :], take(act, ("gb", i, m))[:, :], ACT.Copy), ("gb", i, m))
                after_unit()
            for i in range(8):
                if i:
                    evacuated(act, ("cv", i - 1, 1))
                evac(A(tmp[0][:, 0:T], take(act, ("cv", i, 0))[:, :], ACT.Copy), ("cv", i, 0))
                filled(act, ("cv", i, 1))
                after_unit()
            gate_steps(0, 2)
            evacuated(act, "ln_mean")
            for c in range(CH):
                A(sq2[:, c, :], conv_b[:, c, :], ACT.Square).then_inc(sem("sq_ln"), 1)
            root()
            for c in range(CH):
                act.wait_ge(sem("ln_scaled"), c + 1)
                A(tmp[1][:, 0:T], tmp[0][:, 0:T], ACT.Sigmoid, bias=pcol("ln_b_b_2", c)).then_inc(sem("ln_sig"), 1)
            gate_steps(1, 0)
            for i in range(4):
                filled(act, ("wo2", i, 1))
                after_unit()
            for c in range(CH):
                evacuated(act, ("wo2", c // 2, c % 2))
                A(sq2[:, c, :], x_res[:, c, :], ACT.Square).then_inc(sem("sq_ffn"), 1)
            root()
            for i in range(FC):
                for m in range(2):
                    if i:
                        act.wait_ge(sem("pad_used"), 2 * (i - 1) + m + 1)
                    evac(A(pads[m][:, KF - 1:KF - 1 + T], take(act, ("up", i, m))[:, :], ACT.Copy), ("up", i, m))
                after_unit()
                act.wait_ge(sem("cg_ready"), i + 1)
                A(rs[:, :], tmp[0][:, 0:T], ACT.Sigmoid).then_inc(sem("cg_sig"), 1)
            for n in range(12):
                slot_used(act, u)
                after_unit()
            for c in range(CH):
                evacuated(act, ("down", c // 2, c % 2))
                A(sq3[:, c, :], x_res[:, c, :], ACT.Square).then_inc(sem("sq_fin"), 1)
            root()
            for t in range(NT):
                b = take(act, ("out", t, 0))
                if t >= 2:
                    act.wait_ge(sem(f"stored{t % 2}"), 16 * (t // 2))
                evac(A(out_tok[t % 2][:, 0:T], b[:, :], ACT.Copy), ("out", t, 0))

        @block.vector
        def _(dve):
            V = nc.vector
            steps = [0]

            def link(ins):
                steps[0] += 1
                ins.then_inc(sem("dve_steps"), 1)
                dve.wait_ge(sem("dve_steps"), steps[0])

            split = [0]

            def split_lo(upto):
                while split[0] <= min(upto, NU - 1):
                    u = split[0]
                    split[0] += 1
                    nk = units[u][2]
                    dve.wait_ge(hi_ready, u + 1)
                    if u >= 2:
                        slot_used(dve, u - 2)
                    V.tensor_tensor(w_lo[u % 2][:, 0:nk, :], w_raw[u % 2][:, 0:nk, :],
                                    w_hi[u % 2][:, 0:nk, :].bitcast(F32), ALU.subtract).then_inc(lo_ready, 1)

            roots = [0]

            def variance(key, width, scale, eps):
                b = take(dve, key)
                evac(V.tensor_scalar(rs[:, 0:width], b[:, 0:width], scale, eps, ALU.mult, ALU.add), key)
                evacuated(dve, key)
                V.reciprocal(rs[:, 0:width], rs[:, 0:width]).then_inc(sem("var_ready"), 1)
                roots[0] += 1
                dve.wait_ge(sem("rs_ready"), roots[0])

            def parts(src, hi, lo, name):
                link(V.tensor_copy(hi, src))
                V.tensor_tensor(lo, src, hi.bitcast(F32), ALU.subtract).then_inc(sem(name), 1)

            def normed(src, gain, width, hi, lo, name):
                for c in range(CH):
                    t = tmp[c % 2][:, 0:width]
                    link(V.scalar_tensor_tensor(t, src[:, c, 0:width], pcol(gain, c), rs[:, 0:width], ALU.mult, ALU.mult))
                    parts(t, hi[:, c, 0:width], lo[:, c, 0:width], name)

            evac(V.tensor_copy(par[:, 0:T], take(dve, ("par", 0))[:, :]), ("par", 0))
            evac(V.tensor_copy(par[:, T:PARAM_TILES * P], take(dve, ("par", 1))[:, 0:PARAM_TILES * P - T]), ("par", 1))
            evacuated(dve, ("par", 0))
            evacuated(dve, ("par", 1))
            c0 = PARAM_AT["mu_r"]
            link(V.tensor_scalar(omm, par[:, c0:c0 + 13], -1.0, 1.0, ALU.mult, ALU.add))
            c0 = PARAM_AT["k_a"]
            V.tensor_scalar(omka, par[:, c0:c0 + 4], -1.0, 1.0, ALU.mult, ALU.add).then_inc(sem("derived"), 1)
            dve.wait_ge(sem("derived"), 1)
            split_lo(1)
            variance("ss_x", T, 1.0 / D, NORM_EPS)
            for c in range(CH):
                evacuated(dve, ("xT", c))
            normed(x_res, "norm_g", T, op_hi, op_lo, "xn_ready")

            sh = [0]

            def shift(key, dst, mu):
                sh[0] += 1
                b = take(dve, key)
                dve.wait_ge(sem("unshifted"), sh[0])
                evac(V.scalar_tensor_tensor(dst[:, 1:T], b[:, 0:T - 1], mu, dst[:, 1:T], ALU.mult, ALU.add), key)

            filled(dve, ("qd", 0, 1))
            split_lo(2)
            filled(dve, ("kvi", 0, 1))
            split_lo(3)
            shift(("wa", 0, 0), tmp[2], pcol("mu_wa"))
            split_lo(4)
            u = 3
            for half in range(2):
                for w, dst in enumerate((lambda i: ar[:, i, 1, :], lambda i: kt[:, i, :], lambda i: vf[:, i, :])):
                    for m in range(2):
                        i = 2 * half + m
                        shift(("rkv"[w], half, m), dst(i), pcol("mu_" + "rkv"[w], i))
                    u += 1
                    split_lo(u + 1)
                for m in range(2):
                    b = take(dve, ("g", half, m))
                    dve.wait_ge(sem("sig_g"), 2 * half + m + 1)
                    evac(V.tensor_tensor(gate_r[:, 2 * half + m, :], b[:, :], tmp[m][:, 0:T], ALU.mult), ("g", half, m))
                u += 1
                split_lo(u + 1)
            for half in range(2):
                for m in range(2):
                    b = take(dve, ("ga", half, m))
                    dve.wait_ge(sem("sig_g"), 4 + 2 * half + m + 1)
                    evac(V.tensor_tensor(gate_a[:, 2 * half + m, :], b[:, :], tmp[m][:, 0:T], ALU.mult), ("ga", half, m))
                u += 1
                split_lo(min(u + 1, first_phase2_unit - 1))

            b = take(dve, "w_idx")[:, :].rearrange("p (t n) -> p t n", t=NT)[:, :, HD:HD + 4]
            evac(V.tensor_scalar(w_idx.rearrange("p (t n) -> p t n", t=NT), b, 0.5, None, ALU.mult), "w_idx")
            cum = prep[2][:, 0:516].rearrange("p (c t) -> p c t", c=NT)
            link(V.memset(prep[2][:, 0:516], 0.0))
            e_down = tmp[0][:, 0:516].rearrange("p (c t) -> p c t", c=NT)
            e_up = tmp[1][:, 0:516].rearrange("p (c t) -> p c t", c=NT)

            def chunked(t):
                return t.rearrange("p (c t) -> p c t", c=NT)

            mid = negmax[:, 0:NT]
            for half in range(2):
                for m in range(2):
                    evacuated(dve, ("r", half, m))
                    evacuated(dve, ("k", half, m))
                    evacuated(dve, ("v", half, m))
                    evacuated(dve, ("ga", half, m))
            for i in range(NI):
                evacuated(dve, ("z", i))
                if i:
                    link(V.memset(cum[:, :, 0:1], 0.0))
                for c in range(NT):
                    ins = V.tensor_tensor_scan(cum[:, c, 1:P + 1], ones[:, :], prep[0][:, c * P:c * P + P], 0.0, ALU.mult, ALU.add)
                    link(ins)
                link(V.tensor_copy(mid, cum[:, :, HD]))
                V.tensor_tensor(cum, cum, mid.unsqueeze(2).to_broadcast([P, NT, P + 1]), ALU.subtract)\
                    .then_inc(sem("cum_ready"), 1)
                dve.wait_ge(sem("cum_ready"), i + 1)
                link(V.tensor_scalar(prep[0][:, 0:T], kt[:, i, :], pcol("k_k", i), None, ALU.mult))
                evacuated(dve, ("kk", i))
                link(V.tensor_scalar(rs[:, :], rs[:, :], 1e-12, None, ALU.max))
                link(V.reciprocal(rs[:, :], rs[:, :]))
                link(V.tensor_tensor(prep[0][:, 0:T], prep[0][:, 0:T], rs[:, :], ALU.mult))
                evacuated(dve, ("a", i))
                link(V.tensor_scalar(rs[:, :], prep[1][:, 0:T], pcol("k_a", i), omka[:, i:i + 1], ALU.mult, ALU.add))
                link(V.tensor_tensor(kt[:, i, :], kt[:, i, :], rs[:, :], ALU.mult))
                V.scalar_tensor_tensor(prep[3][:, 0:T], ar[:, i, 1, :], pcol("r_k", i), kt[:, i, :], ALU.mult, ALU.mult)\
                    .then_inc(sem("rk_ready"), 1)
                link(V.tensor_tensor(prep[1][:, 0:T], prep[0][:, 0:T], prep[1][:, 0:T], ALU.mult))
                dve.wait_ge(sem("exps"), 2 * i + 2)
                V.tensor_tensor(dec.rearrange("p (i c) -> p i c", i=NI)[:, i, 0:NT - 1], e_up[:, 1:NT, 0], e_down[:, 0:NT - 1, P],
                                ALU.mult)
                V.tensor_tensor(chunked(bt[:, i, :]), chunked(prep[1][:, 0:T]), e_up[:, :, 1:P + 1], ALU.mult)
                V.scalar_tensor_tensor(chunked(ar[:, i, 0, :]), chunked(prep[0][:, 0:T]), -1.0, e_down[:, :, 0:P], ALU.mult, ALU.mult)
                dve.wait_ge(sem("rk_ready"), i + 1)
                V.tensor_tensor(chunked(ar[:, i, 1, :]), chunked(ar[:, i, 1, :]), e_down[:, :, 1:P + 1], ALU.mult)
                b = take(dve, ("bonus", i))
                evac(V.tensor_tensor(bonus_v[:, i, :], b[:, :], vf[:, i, :], ALU.mult), ("bonus", i))
                V.tensor_tensor(chunked(kt[:, i, :]), chunked(kt[:, i, :]), e_up[:, :, 1:P + 1], ALU.mult).then_inc(sem("prep_ready"), 1)

            dve.wait_ge(sem("prep_ready"), NI)
            for c in range(NT):
                for odd in range(2):
                    hs = slice(NI * odd, NI * odd + NI)
                    for name, dst in (("gb", g_b), ("gk", g_k)):
                        for i2 in range(2):
                            h = NI * odd + 2 * i2
                            b = take(dve, (name, c, odd, i2))[:, :].rearrange("p (n a t) -> p n a t", n=2, a=2)
                            evac(V.tensor_tensor(dst[:, h:h + 2, :, :], b, mask_ar[:, :, :].unsqueeze(1).to_broadcast([P, 2, 2, P]),
                                                 ALU.mult), (name, c, odd, i2))
                    b = take(dve, ("low", c, odd))[:, :].rearrange("p (i t) -> p i t", i=NI)
                    evac(V.tensor_tensor(low[:, hs, :], b, mask_low[:, :].unsqueeze(1).to_broadcast([P, NI, P]), ALU.mult),
                         ("low", c, odd))
                    evacuated(dve, ("gb", c, odd, 0))
                    evacuated(dve, ("gb", c, odd, 1))
                    evacuated(dve, ("low", c, odd))
                    eye = ident[:, :].unsqueeze(1).to_broadcast([P, NI, P])
                    V.tensor_tensor(inv[:, hs, :], g_b[:, hs, 0, :], mask_lev[:, 0, :].unsqueeze(1).to_broadcast([P, NI, P]), ALU.mult)
                    link(V.tensor_tensor(invT[:, hs, :], low[:, hs, :], mask_lowT[:, :].unsqueeze(1).to_broadcast([P, NI, P]), ALU.mult))
                    link(V.tensor_tensor(inv[:, hs, :], inv[:, hs, :], eye, ALU.add))
                    V.tensor_tensor(invT[:, hs, :], invT[:, hs, :], eye, ALU.add).then_inc(sem(f"inv_init{odd}"), 1)
                    dve.wait_ge(sem(f"inv_init{odd}"), c + 1)
                for lev in range(1, 7):
                    for odd in range(2):
                        hs = slice(NI * odd, NI * odd + NI)
                        b = take(dve, ("w", c, lev, odd))[:, :].rearrange("p (i t) -> p i t", i=NI)
                        evac(V.tensor_tensor(wprod[:, hs, :], b, mask_lev[:, lev, :].unsqueeze(1).to_broadcast([P, NI, P]), ALU.mult),
                             ("w", c, lev, odd))
                    for odd in range(2):
                        hs = slice(NI * odd, NI * odd + NI)
                        for name, dst in (("dinv", inv), ("dinvT", invT))[0:2 if lev < 6 else 1]:
                            b = take(dve, (name, c, lev, odd))[:, :].rearrange("p (i t) -> p i t", i=NI)
                            if lev > 1:
                                evacuated(dve, (name, c, lev - 1, odd))
                            evac(V.tensor_tensor(dst[:, hs, :], b, dst[:, hs, :], ALU.add), (name, c, lev, odd))
                if c < NT - 1:
                    for odd in range(2):
                        rows = slice(HD * odd, HD * odd + HD)
                        b = take(dve, ("p", c, odd))[rows, 0:256].rearrange("p (i d) -> p i d", i=NI)
                        f = dec[rows, :].rearrange("p (i c) -> p i c", i=NI)[:, :, c]
                        evac(V.tensor_tensor(state[rows, :, :], b, f.unsqueeze(2).to_broadcast([HD, NI, HD]), ALU.mult), ("p", c, odd))

            for i in range(NI):
                b = take(dve, ("gn_mean", i))
                evac(V.scalar_tensor_tensor(tmp[0][:, 0:T], b[:, :], -1.0 / HD, y_scan[:, i, :], ALU.mult, ALU.add), ("gn_mean", i))
                variance(("gn_var", i), T, 1.0 / HD, GN_EPS)
                link(V.scalar_tensor_tensor(tmp[0][:, 0:T], tmp[0][:, 0:T], pcol("gn_g", i), rs[:, :], ALU.mult, ALU.mult))
                link(V.scalar_tensor_tensor(tmp[0][:, 0:T], tmp[0][:, 0:T], pcol("gn_b", i), bonus_v[:, i, :], ALU.add, ALU.add))
                link(V.tensor_tensor(gate_r[:, i, :], tmp[0][:, 0:T], gate_r[:, i, :], ALU.mult))

            variance("ss_q", T, 1.0 / 256, NORM_EPS)
            for m in range(2):
                V.scalar_tensor_tensor(qd[:, m, :], qd[:, m, :], pcol("q_norm_g", m), rs[:, :], ALU.mult, ALU.mult)\
                    .then_inc(sem("cq_ready"), 1)
            dve.wait_ge(sem("cq_ready"), 2)
            variance("ss_kv", T, 1.0 / P, NORM_EPS)
            V.scalar_tensor_tensor(ckv[:, :], ckv[:, :], pcol("kv_norm_g"), rs[:, :], ALU.mult, ALU.mult).then_inc(sem("ckv_ready"), 1)
            dve.wait_ge(sem("ckv_ready"), 1)
            b = take(dve, "ki_mean")
            evac(V.scalar_tensor_tensor(kidx[:, :], b[:, :], -1.0 / HD, kidx[:, :], ALU.mult, ALU.add), "ki_mean")
            variance("ki_var", T, 1.0 / HD, LN_EPS)
            link(V.scalar_tensor_tensor(kidx[:, :], kidx[:, :], pcol("kidx_g"), rs[:, :], ALU.mult, ALU.mult))
            V.tensor_scalar(kidx[:, :], kidx[:, :], pcol("kidx_b"), None, ALU.add).then_inc(sem("kidx_ready"), 1)
            evacuated(dve, "w_idx")
            for qt in range(1, NT):
                w = P * (qt + 1)
                s = score[:, qt, 0:w]
                for h in range(4):
                    evacuated(dve, ("lg", qt, h))
                    wi = w_idx[:, 4 * qt + h:4 * qt + h + 1]
                    if h:
                        ins = V.scalar_tensor_tensor(s, relu_t[0][:, 0:w], wi, s, ALU.mult, ALU.add)
                    else:
                        ins = V.tensor_scalar(s, relu_t[0][:, 0:w], wi, None, ALU.mult)
                    ins.then_inc(sem("relu_used"), 1)
                    dve.wait_ge(sem("relu_used"), 4 * (qt - 1) + h + 1)
                V.tensor_copy(top8, s[:, 0:8]).then_inc(sem("score_ready"), 1)
            for qt in range(1, NT):
                s = score[:, qt, 0:P * (qt + 1)]
                dve.wait_ge(sem("causal"), qt + 1)
                dve.wait_ge(sem("score_ready"), 3)
                for n in range(TOPK // 8):
                    link(V.max(top8, s))
                    link(V.match_replace(s, top8, s, TAKEN))
                link(V.tensor_scalar(s, s, -2.0e38, MASKED, ALU.is_gt, ALU.mult))
            dve.wait_ge(sem("causal"), 1)
            for h in range(NH):
                for n in range(NT + 2):
                    if n < NT:
                        w = P * (n + 1)
                        if n >= 2:
                            filled(dve, ("pT", h, n - 2))
                        p = prob[n % 2][:, 0:w]
                        b = take(dve, ("s", h, n))
                        evac(V.tensor_tensor(p, b[:, 0:w], score[:, n, 0:w], ALU.add), ("s", h, n))
                        evacuated(dve, ("s", h, n))
                        V.tensor_reduce(negmax[:, n:n + 1], p, X_AXIS, ALU.max, negate=True).then_inc(sem("max_ready"), 1)
                    if 0 <= n - 1 < NT:
                        q = n - 1
                        p = prob[q % 2][:, 0:P * (q + 1)]
                        dve.wait_ge(sem("exp_ready"), NT * h + q + 1)
                        link(V.reciprocal(rsum[:, q:q + 1], sums[:, q:q + 1]))
                        V.tensor_scalar(p, p, rsum[:, q:q + 1], None, ALU.mult).then_inc(sem("prob_ready"), 1)
                    if 0 <= n - 2:
                        q = n - 2
                        b = take(dve, ("pT", h, q))[:, 0:P * (q + 1)].rearrange("p (k t) -> p k t", t=P)
                        evac(V.tensor_copy(probT[:, 0:q + 1, q * P:q * P + P], b), ("pT", h, q))
                rows, i = slice(HD * (h % 2), HD * (h % 2) + HD), h // 2
                b = take(dve, ("o", h))
                evac(V.tensor_tensor(gate_a[rows, i, :], b[rows, :], gate_a[rows, i, :], ALU.mult), ("o", h))
            for h in range(NH):
                evacuated(dve, ("o", h))
            for c in range(CH):
                src = gate_r[:, c, :] if c < NI else gate_a[:, c - NI, :]
                parts(src, op_hi[:, c, :], op_lo[:, c, :], "mix_ready")
            u = first_phase2_unit
            split_lo(u + 1)

            def after_unit():
                nonlocal u
                split_lo(u + 2)
                u += 1

            def residual(what, i):
                for m in range(2):
                    b = take(dve, (what, i, m))
                    x = x_res[:, 2 * i + m, :]
                    evac(V.tensor_tensor(x, b[:, :], x, ALU.add), (what, i, m))

            for i in range(4):
                residual("wout", i)
                after_unit()
            for c in range(CH):
                evacuated(dve, ("memT", c))
            variance("ss_mem", MEM, 1.0 / D, EPS2)
            normed(memT, "norm_mem_g_2", MEM, op2_hi, op2_lo, "memn_ready")
            for i in range(4):
                filled(dve, ("kT", i, 1))
                after_unit()
            for i in range(4):
                filled(dve, ("vm", i))
                after_unit()
            for i in range(4):
                for m in range(2):
                    evacuated(dve, ("wout", i, m))
            variance("ss_y", T, 1.0 / D, NORM_EPS)
            for c in range(CH):
                V.scalar_tensor_tensor(x_res[:, c, :], x_res[:, c, :], pcol("final_g", c), rs[:, :], ALU.mult, ALU.mult)\
                    .then_inc(sem("x1_ready"), 1)
            dve.wait_ge(sem("x1_ready"), CH)
            variance("ss_mix", T, 1.0 / D, EPS2)
            normed(x_res, "norm_mix_g_2", T, op_hi, op_lo, "mixn_ready")

            for s_ in range(2):
                link(V.memset(pad_b[s_][:, 0:KB - 1], 0.0))
            for i in range(8):
                evacuated(dve, ("u", i, 1))
                b = take(dve, ("u", i, 0))
                pad = pad_b[i % 2]
                evac(V.tensor_tensor(pad[:, KB - 1:KB - 1 + T], b[:, :], tmp[0][:, 0:T], ALU.mult), ("u", i, 0))
                after_unit()
                evacuated(dve, ("u", i, 0))
                y = conv_b[:, i, :]
                link(V.tensor_scalar(y, pad[:, 0:T], pcol("conv_b_w_2", i), pcol("conv_b_bias_2", i), ALU.mult, ALU.add))
                for k in range(1, KB):
                    ins = V.scalar_tensor_tensor(y, pad[:, k:k + T], pcol("conv_b_w_2", 8 * k + i), y, ALU.mult, ALU.add)
                    if k < KB - 1:
                        link(ins)
                    else:
                        ins.then_inc(sem("conv_ready"), 1)
            for i in range(4):
                filled(dve, ("q2", i, 1))
                after_unit()
            for h in range(MH):
                for n in range(NT + 2):
                    if n < NT:
                        b = take(dve, ("s2", h, n))
                        link(V.tensor_reduce(negmax[:, n:n + 1], b[:, 0:MEM], X_AXIS, ALU.max, negate=True))
                        V.tensor_scalar(negmax[:, n:n + 1], negmax[:, n:n + 1], 1.0 / 16, None, ALU.mult).then_inc(sem("max2_ready"), 1)
                    if 0 <= n - 1 < NT:
                        q = n - 1
                        evacuated(dve, ("s2", h, q))
                        link(V.reciprocal(rsum[:, q:q + 1], sums[:, q:q + 1]))
                        V.tensor_scalar(prob2[q % 2][:, :], prob2[q % 2][:, :], rsum[:, q:q + 1], None, ALU.mult).then_inc(sem("prob2_ready"), 1)
                    if 0 <= n - 2:
                        q = n - 2
                        b = take(dve, ("p2T", h, q))[:, 0:MEM].rearrange("p (k t) -> p k t", t=P)
                        evac(V.tensor_copy(prob2T[:, :, q * P:q * P + P], b), ("p2T", h, q))
                for d in range(2):
                    b = take(dve, ("oc", h, d))
                    hi = op2_hi[:, 2 * h + d, :]
                    link(V.tensor_copy(hi, b[:, :]))
                    evac(V.tensor_tensor(op2_lo[:, 2 * h + d, :], b[:, :], hi.bitcast(F32), ALU.subtract), ("oc", h, d))

            def gate_steps(branch):
                for i in range(4):
                    filled(dve, ("pg", branch, i, 1))
                    after_unit()
                    for m in range(2):
                        evacuated(dve, ("pg", branch, i, m))
                        b = take(dve, ("y", branch, i, m))
                        mg = merged[:, 2 * i + m, :]
                        if branch == 2:
                            evac(V.tensor_tensor(mg, b[:, :], gates[m][:, :], ALU.mult), ("y", branch, i, m))
                        else:
                            evac(V.tensor_tensor(tmp[2][:, 0:T], b[:, :], gates[m][:, :], ALU.mult), ("y", branch, i, m))
                            evacuated(dve, ("y", branch, i, m))
                            link(V.tensor_tensor(mg, mg, tmp[2][:, 0:T], ALU.add))
                    after_unit()

            def conv3(dst, pad, weights, first, stride):
                link(V.tensor_scalar(dst, pad[:, 0:T], pcol(weights, first), None, ALU.mult))
                link(V.scalar_tensor_tensor(dst, pad[:, 1:1 + T], pcol(weights, first + stride), dst, ALU.mult, ALU.add))
                return V.scalar_tensor_tensor(dst, pad[:, 2:2 + T], pcol(weights, first + 2 * stride), dst, ALU.mult, ALU.add)

            gate_steps(2)
            for i in range(4):
                for m in range(2):
                    evacuated(dve, ("y", 2, i, m))
            for i in range(4):
                filled(dve, ("gb", i, 1))
                after_unit()
            dve.wait_ge(sem("conv_ready"), CH)
            for s_ in range(2):
                link(V.memset(pads[s_][:, 0:KF - 1], 0.0))
            for i in range(8):
                evacuated(dve, ("cv", i, 0))
                evac(V.tensor_tensor(pads[0][:, KF - 1:KF - 1 + T], take(dve, ("cv", i, 1))[:, :], tmp[0][:, 0:T], ALU.mult), ("cv", i, 1))
                after_unit()
                evacuated(dve, ("cv", i, 1))
                evacuated(dve, ("gb", i // 2, i % 2))
                link(conv3(tmp[1][:, 0:T], pads[0], "conv_a_w_2", i, 8))
                link(V.tensor_tensor(tmp[1][:, 0:T], tmp[1][:, 0:T], work[:, i, :], ALU.mult))
                parts(tmp[1][:, 0:T], op2_hi[:, i, :], op2_lo[:, i, :], "op2_ready0")
            gate_steps(0)
            b = take(dve, "ln_mean")
            for c in range(CH):
                ins = V.scalar_tensor_tensor(conv_b[:, c, :], b[:, :], -1.0 / D, conv_b[:, c, :], ALU.mult, ALU.add)
            evac(ins, "ln_mean")
            variance("ln_var", T, 1.0 / D, EPS2)
            for c in range(CH):
                V.scalar_tensor_tensor(tmp[0][:, 0:T], conv_b[:, c, :], pcol("ln_b_g_2", c), rs[:, :], ALU.mult, ALU.mult)\
                    .then_inc(sem("ln_scaled"), 1)
                dve.wait_ge(sem("ln_sig"), c + 1)
                link(V.scalar_tensor_tensor(tmp[2][:, 0:T], tmp[0][:, 0:T], pcol("ln_b_b_2", c), tmp[1][:, 0:T], ALU.add, ALU.mult))
                parts(tmp[2][:, 0:T], op2_hi[:, c, :], op2_lo[:, c, :], "op2_ready1")
            gate_steps(1)
            for c in range(CH):
                parts(merged[:, c, :], op_hi[:, c, :], op_lo[:, c, :], "merged_ready")
            for i in range(4):
                residual("wo2", i)
                after_unit()
            for i in range(4):
                for m in range(2):
                    evacuated(dve, ("wo2", i, m))
            variance("ss_ffn", T, 1.0 / D, EPS2)
            normed(x_res, "norm_ffn_g_2", T, op_hi, op_lo, "ffn_ready")

            for i in range(FC):
                evacuated(dve, ("up", i, 0))
                if i:
                    dve.wait_ge(sem("act_ready"), i)
                conv3(tmp[0][:, 0:T], pads[0], "conv_ffn_w_2", i, 2 * FC).then_inc(sem("pad_used"), 1)
                dve.wait_ge(sem("pad_used"), 2 * i + 1)
                V.tensor_copy(top8, tmp[0][:, 0:8]).then_inc(sem("cg_ready"), 1)
                evacuated(dve, ("up", i, 1))
                conv3(tmp[1][:, 0:T], pads[1], "conv_ffn_w_2", FC + i, 2 * FC).then_inc(sem("pad_used"), 1)
                dve.wait_ge(sem("pad_used"), 2 * i + 2)
                after_unit()
                dve.wait_ge(sem("cg_sig"), i + 1)
                link(V.tensor_tensor(tmp[0][:, 0:T], tmp[0][:, 0:T], rs[:, :], ALU.mult))
                link(V.tensor_tensor(tmp[0][:, 0:T], tmp[0][:, 0:T], tmp[1][:, 0:T], ALU.mult))
                lo = act_lo[:, i, :] if i < 16 else act_lo2[:, i - 16, :]
                parts(tmp[0][:, 0:T], act_hi[:, i, :], lo, "act_ready")
            for i in range(4):
                for n in range(2):
                    slot_used(dve, u)
                    after_unit()
                residual("down", i)
                after_unit()
            for i in range(4):
                for m in range(2):
                    evacuated(dve, ("down", i, m))
            variance("ss_fin", T, 1.0 / D, EPS2)
            for c in range(CH):
                V.scalar_tensor_tensor(x_res[:, c, :], x_res[:, c, :], pcol("norm_final_g_2", c), rs[:, :], ALU.mult, ALU.mult)\
                    .then_inc(sem("fin_ready"), 1)
            for t in range(NT):
                b = take(dve, ("out", t, 1))
                if t >= 2:
                    dve.wait_ge(sem(f"stored{t % 2}"), 16 * (t // 2))
                evac(V.tensor_copy(out_tok[t % 2][:, T:D], b[:, :]), ("out", t, 1))


NAMES = ["x", "norm_g", "w_in", "mu_shift", "w0", "w_up", "a0", "a_up", "k_k", "k_a", "r_k", "gn_g", "gn_b", "q_norm_g",
         "kv_norm_g", "w_uq", "w_uk", "w_uv", "w_qidx", "kidx_g", "kidx_b", "w_out", "final_g", "mem_2", "norm_mix_g_2",
         "norm_mem_g_2", "w_in_2", "b_gate_2", "conv_a_w_2", "w_a_out_2", "conv_b_w_2", "conv_b_bias_2", "ln_b_g_2",
         "ln_b_b_2", "w_b_out_2", "w_kv_2", "w_att_out_2", "w_o_2", "norm_ffn_g_2", "w_up_2", "conv_ffn_w_2", "w_down_2",
         "norm_final_g_2"]


def kernel(**inputs):
    import concourse.bacc as bacc
    from concourse.bass_utils import run_bass_kernel_spmd

    nc = bacc.Bacc("TRN2", target_bir_lowering=False, num_devices=1)
    arrays, dram = {}, {}
    for name in NAMES:
        a = np.ascontiguousarray(inputs[name])
        arrays["in_" + name] = a
        dram[name] = nc.dram_tensor("in_" + name, a.shape, mybir.dt.from_np(a.dtype), kind="ExternalInput").ap()
    out = nc.dram_tensor("out", (1, T, D), F32, kind="ExternalOutput").ap()
    build(nc, dram, out)
    r = run_bass_kernel_spmd(nc, [arrays], core_ids=[0])
    return r.results[0]["out"]
```

```python
from contextlib import ExitStack

import numpy as np

import concourse.bass as bass
from concourse import mybir

F32 = mybir.dt.float32
F32R = mybir.dt.float32r
ALU = mybir.AluOpType
ACT = mybir.ActivationFunctionType
X_AXIS = mybir.AxisListType.X

P = 128
D = 1024
T = 512
CH = D // P
NT = T // P
HD = 64
NH = 8
NI = NH // 2
MEM = 256
MH = 4
FF = 2816
FC = FF // P
TOPK = 128
KAPPA = float(np.exp(-0.5))
NORM_EPS, LN_EPS, GN_EPS, EPS2 = 1e-6, 1e-5, 64e-5, 1e-6
MASKED = -1.0e30
TAKEN = -3.0e38
KB, KA, KF = 31, 3, 3
BANKS = 8

C_R, C_K, C_V, C_WA, C_G, C_QD, C_KV, C_KI, C_WI, C_GA = 0, 512, 1024, 1536, 1600, 2112, 2368, 2496, 2560, 2564
C2_GB, C2_GC, C2_VA, C2_U, C2_UG, C2_Q, C2_PG = 0, 1024, 2048, 3072, 4096, 5120, 6144


def weight_units():
    units = []

    def add(what, i, pieces, nk=CH, k0=0):
        units.append((what, i, nk, [(at, w, col, n, k0) for at, w, col, n in pieces]))

    add("qd", 0, [(0, "w_in", C_QD, 256)])
    add("kvi", 0, [(0, "w_in", C_KV, 128), (128, "w_in", C_KI, 64), (192, "w_in", C_KI, 64)])
    add("wa", 0, [(0, "w_in", C_WA, 64), (64, "w_in", C_WI, 4), (68, "w_in", C_G + 4, 188)])
    for half in range(2):
        for what, col in (("r", C_R), ("k", C_K), ("v", C_V), ("g", C_G)):
            add(what, half, [(0, "w_in", col + 256 * half, 256)])
    for half in range(2):
        add("ga", half, [(0, "w_in", C_GA + 256 * half, 256)])
    for i in range(4):
        add("wout", i, [(0, "w_out", 256 * i, 256)])
    for i in range(4):
        add("kT", i, [(0, "w_kv_2", 256 * i, 256)])
    for i in range(4):
        add("vm", i, [(0, "w_kv_2", D + 256 * i, 256)])

    def add_u(i):
        add("u", i, [(0, "w_in_2", C2_U + P * i, P), (P, "w_in_2", C2_UG + P * i, P)])

    def gated(branch, w):
        for i in range(4):
            add("pg", i, [(0, "w_in_2", C2_PG + D * branch + 256 * i, 256)])
            if branch == 2 and i == 0:
                add_u(2)
            add("y", i, [(0, w, 256 * i, 256)])
            if branch == 2 and i:
                add_u(2 + i)

    add_u(0)
    for i in range(4):
        add("q2", i, [(0, "w_in_2", C2_Q + 256 * i, 256)])
    add_u(1)
    gated(2, "w_att_out_2")
    for i in range(4):
        add("gb", i, [(0, "w_in_2", C2_GB + 256 * i, 256)])
        if i % 2:
            add_u(6 + i // 2)
    for i in range(8):
        add("cv", i, [(0, "w_in_2", C2_GC + P * i, P), (P, "w_in_2", C2_VA + P * i, P)])
    gated(0, "w_a_out_2")
    gated(1, "w_b_out_2")
    for i in range(4):
        add("wo2", i, [(0, "w_o_2", 256 * i, 256)])
    for i in range(FC):
        add("up", i, [(0, "w_up_2", P * i, P), (P, "w_up_2", FF + P * i, P)])
    for i in range(4):
        for k0, nk in ((0, 8), (8, 8), (16, 6)):
            add("down", (i, k0), [(0, "w_down_2", 256 * i, 256)], nk, k0)
    return units


PARAM_ROWS = [("norm_g", 8), ("mu_r", 4), ("mu_k", 4), ("mu_v", 4), ("mu_wa", 1), ("w0", 4), ("a0", 4), ("k_k", 4),
              ("k_a", 4), ("r_k", 4), ("gn_g", 4), ("gn_b", 4), ("q_norm_g", 2), ("kv_norm_g", 1), ("kidx_g", 1),
              ("kidx_b", 1), ("final_g", 8), ("norm_mix_g_2", 8), ("norm_mem_g_2", 8), ("b_gate_2", 24),
              ("conv_b_bias_2", 8), ("ln_b_g_2", 8), ("ln_b_b_2", 8), ("norm_ffn_g_2", 8), ("norm_final_g_2", 8),
              ("conv_a_w_2", 24), ("conv_b_w_2", 248), ("conv_ffn_w_2", 132)]
PARAM_AT = {}
_at = 0
for _name, _rows in PARAM_ROWS:
    PARAM_AT[_name] = _at
    _at += _rows
PARAM_TILES = -(-_at // P)


def build(nc, dram, out):
    units = weight_units()
    NU = len(units)
    ctx = ExitStack()
    with ctx:
        base = -(-nc.sbuf_base // 32) * 32

        def at(name, offset, shape, dt=F32):
            return nc.alloc_sbuf_tensor_at(name, [P] + shape, dt, offset=base + offset)

        sems = {}

        def sem(name):
            if name not in sems:
                sems[name] = ctx.enter_context(nc.semaphore(name))
            return sems[name]

        w_raw = [at(f"w_raw{s}", 8192 * s, [CH, 256]) for s in range(2)]
        w_hi = [at(f"w_hi{s}", 16384 + 8192 * s, [CH, 256], F32R) for s in range(2)]
        w_lo = [at(f"w_lo{s}", 32768 + 8192 * s, [CH, 256], F32R) for s in range(2)]
        x_res = at("x_res", 49152, [CH, T])
        op_hi = at("op_hi", 81920, [CH, T], F32R)
        op_lo = at("op_lo", 98304, [CH, T], F32R)
        ident = at("ident", 114688, [P])
        ones = at("ones", 115200, [P])
        par = at("par", 115712, [PARAM_TILES * P])
        misc = at("misc", 118272, [128])
        S0 = 118784
        tmp = [at(f"tmp{i}", 124928 + 2176 * i, [544]) for i in range(3)]
        rs = at("rs", 131456, [T])
        R0 = 133504
        pair_ones = at("pair_ones", S0, [P])
        mask_ar = at("mask_ar", S0 + 512, [2, P])
        mask_lev = at("mask_lev", S0 + 1536, [7, P])
        mask_lowT = at("mask_lowT", S0 + 5120, [P])
        mask_low = at("mask_low", S0 + 5632, [P])
        x_tok = at("x_tok", R0, [NT, D])
        sq1 = at("sq1", R0 + 16384, [CH, T])
        par_rows = at("par_rows", R0 + 32768, [PARAM_TILES, P])
        ar = at("ar", R0, [NI, 2, T])
        bt = at("bt", R0 + 16384, [NI, T])
        kt = at("kt", R0 + 24576, [NI, T])
        vf = at("vf", R0 + 32768, [NI, T])
        gate_r = at("gate_r", R0 + 40960, [NI, T])
        gate_a = at("gate_a", R0 + 49152, [NI, T])
        tok = [[at(f"tok{j}_{s}", R0 + 57344 + 6144 * s + 2048 * j, [T]) for j in range(3)] for s in range(2)]
        lora = at("lora", R0 + 57344, [T])
        prep = [at(f"prep{j}", R0 + 59392 + 2080 * j, [4 * 129 + 4]) for j in range(4)]
        qd = at("qd", R0 + 69632, [2, T])
        ckv = at("ckv", R0 + 73728, [T])
        kidx = at("kidx", R0 + 75776, [T])
        bonus_v = at("bonus_v", 65536, [NI, T])
        y_scan = at("y_scan", 73728, [NI, T])
        g_b = at("g_b", 81920, [NH, 2, P])
        g_k = at("g_k", 90112, [NH, 2, P])
        low = at("low", 98304, [NH, P])
        inv = at("inv", 102400, [NH, P])
        invT = at("invT", 106496, [NH, P])
        wprod = at("wprod", 110592, [NH, P])
        state = at("state", R0 + 77824, [NI, HD])
        xs_t = [tmp[0][:, 0:256], tmp[0][:, 256:512]]
        us_t = [tmp[1][:, 0:256], tmp[1][:, 256:512]]
        wuq = at("wuq", 0, [2, 512])
        wqi = at("wqi", 4096, [2, 256])
        wuk = at("wuk", 6144, [512])
        probT = at("probT", 0, [NT, T])
        wukT = at("wukT", 8192, [NI, P])
        wuv = at("wuv", 10240, [512])
        qT = at("qT", 12288, [NI, T])
        qiT = at("qiT", 20480, [2, T])
        q_abs = [at(f"q_abs{s}", 24576 + 2048 * s, [T]) for s in range(2)]
        ckv_tok = at("ckv_tok", 28672, [NT, P])
        score = at("score", 30720, [NT, T])
        o_lat = [at(f"o_lat{s}", 38912 + 2048 * s, [T]) for s in range(2)]
        prob = [at(f"prob{s}", 43008 + 2048 * s, [T]) for s in range(2)]
        relu_t = [at(f"relu{s}", 47104, [T]) for s in range(1)]
        op2_hi = at("op2_hi", R0, [CH, T], F32R)
        op2_lo = at("op2_lo", R0 + 16384, [CH, T], F32R)
        mem_tok = at("mem_tok", R0, [2, D])
        memT = at("memT", R0 + 8192, [CH, MEM])
        memn_hi = at("memn_hi", R0 + 16384, [CH, MEM], F32R)
        memn_lo = at("memn_lo", R0 + 24576, [CH, MEM], F32R)
        sq_mem = at("sq_mem", R0 + 32768, [CH, MEM])
        sq_g = at("sq_g", R0 + 32768, [CH, T])
        conv_b = at("conv_b", R0 + 32768, [CH, T])
        work = at("work", R0 + 49152, [CH, T])
        sq2 = at("sq2", R0 + 49152, [CH, T])
        merged_hi = at("merged_hi", R0 + 32768, [CH, T], F32R)
        merged_lo = at("merged_lo", R0 + 49152, [CH, T], F32R)
        sq_f = at("sq_f", R0, [CH, T])
        pad_a = at("pad_a", R0 + 73728, [KA - 1 + T])
        rs_mix = tmp[2][:, 0:T]
        u_sig = tmp[2][:, 0:T]
        gates = [at(f"gate{m}", R0 + 65536 + 2048 * m, [T]) for m in range(2)]
        prob2T = at("prob2T", R0 + 69632, [2, T])
        prob2 = [at(f"prob2_{s}", R0 + 73728 + 1024 * s, [MEM]) for s in range(NT)]
        memK = at("memK", 65536, [CH, MEM])
        memV = at("memV", 73728, [2, D])
        merged = at("merged", 65536, [CH, T])
        pad_b = [at(f"pad_b{s}", S0 + 2304 * s, [KB - 1 + T]) for s in range(2)]
        conv_f = [[at("conv_f00", S0, [T]), at("conv_f01", S0 + 2048, [T])], [at("conv_f10", S0 + 4096, [T]), tmp[0]]]
        sig_f = [tmp[1], tmp[2]]
        act_hi = at("act_hi", R0, [FC, T], F32R)
        act_lo = at("act_lo", R0 + 45056, [16, T], F32R)
        act_lo2 = at("act_lo2", 65536, [FC - 16, T], F32R)
        sq3 = at("sq3", 81920, [CH, T])
        out_tok = [at(f"out_tok{s}", R0 + 4096 * s, [D]) for s in range(NT)]

        omm = misc[:, 0:13]
        omka = misc[:, 13:17]
        w_idx = misc[:, 17:33]
        top8 = misc[:, 33:41]
        negmax = misc[:, 41:49]
        sums = misc[:, 49:57]
        rsum = misc[:, 57:65]
        dec = misc[:, 65:81]
        ps = [ctx.enter_context(nc.psum_tensor(f"bank{b}", [P, T], F32)) for b in range(BANKS)]

        def pcol(name, i=0):
            c = PARAM_AT[name] + i
            return par[:, c:c + 1]

        full = [sem(f"bank_full{b}") for b in range(BANKS)]
        free = [sem(f"bank_free{b}") for b in range(BANKS)]
        seq = {}

        def take(eng, key):
            n = seq[key]
            eng.wait_ge(full[n % BANKS], n // BANKS + 1)
            return ps[n % BANKS]

        def evac(ins, key):
            ins.then_inc(free[seq[key] % BANKS], 1)

        def evacuated(eng, key):
            n = seq[key]
            eng.wait_ge(free[n % BANKS], n // BANKS + 1)

        def filled(eng, key):
            n = seq[key]
            eng.wait_ge(full[n % BANKS], n // BANKS + 1)

        raw_count, tot = [], [0, 0]
        for u, (_, _, _, pieces) in enumerate(units):
            tot[u % 2] += 16 * len(pieces)
            raw_count.append(tot[u % 2])
        w_arrived = [sem("w_arrived0"), sem("w_arrived1")]
        hi_ready, lo_ready = sem("w_hi_ready"), sem("w_lo_ready")
        unit_last = {}
        first_phase2_unit = next(n for n, u in enumerate(units) if u[0] == "wout")

        par_src = []
        for name, n in PARAM_ROWS:
            if name.startswith("mu_"):
                j = ("mu_r", "mu_k", "mu_v", "mu_wa").index(name)
                src = dram["mu_shift"][0, 512 * j:512 * j + (512 if j < 3 else 64)]
                par_src.append((name, 0, src.rearrange("(n q) -> n q", n=n)))
            elif name in ("kidx_g", "kidx_b"):
                par_src += [(name, HD * d, dram[name]) for d in range(2)]
            elif name in ("final_g", "norm_final_g_2"):
                par_src.append((name, 0, dram[name].rearrange("(n q) -> n q", q=P)))
            elif name in ("conv_a_w_2", "conv_b_w_2", "conv_ffn_w_2"):
                par_src.append((name, 0, dram[name][0].rearrange("k (n q) -> (k n) q", q=P)))
            elif name in ("k_k", "k_a", "r_k", "gn_g", "gn_b"):
                par_src.append((name, 0, dram[name][0].rearrange("(n a) d -> n (a d)", a=2)))
            else:
                par_src.append((name, 0, dram[name][0].rearrange("(n q) -> n q", q=P)))
        par_dmas = []
        for name, col, src in par_src:
            row, n, a = PARAM_AT[name], src.shape[0], 0
            while a < n:
                tl, r = divmod(row + a, P)
                m = min(n - a, P - r)
                par_dmas.append((par_rows[r:r + m, tl, col:col + src.shape[1]], src[a:a + m, :]))
                a += m
        n_par_dmas = len(par_dmas)

        block = ctx.enter_context(nc.Block())

        @block.tensor
        def _(pe):
            count = [0]

            def bank(key):
                n = count[0]
                count[0] += 1
                assert key not in seq, key
                seq[key] = n
                if n >= BANKS:
                    pe.wait_ge(free[n % BANKS], n // BANKS)
                return ps[n % BANKS]

            def done(ins, key):
                ins.then_inc(full[seq[key] % BANKS], 1)

            def transposes(key, blocks, rows=P):
                b = bank(key)
                for j, src in enumerate(blocks):
                    mm = nc.tensor.transpose(b[:, j * P:j * P + rows], src, ident[0:rows, 0:rows])
                done(mm, key)

            def sum_chunks(key, sq, n, width, ready):
                b = bank(key)
                for c in range(n):
                    pe.wait_ge(sem(ready), c + 1)
                    mm = nc.tensor.matmul(b[:, 0:width], ones[:, :], sq[:, c, 0:width], start=c == 0, stop=c == n - 1)
                done(mm, key)

            unit = [0]

            def next_unit(what):
                u = unit[0]
                unit[0] += 1
                assert units[u][0] == what, (units[u], what)
                pe.wait_ge(hi_ready, u + 1)
                pe.wait_ge(lo_ready, u + 1)
                return u

            def sum_some(key, sq, first, last):
                b = bank(key) if first == 0 else ps[seq[key] % BANKS]
                for c in range(first, last):
                    pe.wait_ge(sem("sq_" + key), c + 1)
                    mm = nc.tensor.matmul(b[:, :], ones[:, :], sq[:, c, :], start=c == 0, stop=c == CH - 1)
                if last == CH:
                    done(mm, key)

            def tile(b, u, col, width, xh, xl, x0=0, start=True, stop=True, ks=None):
                wh, wl, nk = w_hi[u % 2], w_lo[u % 2], units[u][2]
                for k in range(nk) if ks is None else ks:
                    h, l = wh[:, k, col:col + P], wl[:, k, col:col + P]
                    nc.tensor.matmul(b[:, 0:width], h, xh[:, x0 + k, 0:width], start=start and k == 0, stop=False)
                    nc.tensor.matmul(b[:, 0:width], h, xl(x0 + k, width), start=False, stop=False)
                    mm = nc.tensor.matmul(b[:, 0:width], l, xh[:, x0 + k, 0:width], start=False,
                                          stop=stop and k == nk - 1)
                return mm

            def plain(t):
                return lambda k, width: t[:, k, 0:width]

            def unit_tiles(what, i, xh, xl, width=T, tiles=2, ready=None, branch=None):
                u = next_unit(what)
                keys = [(what, i, m) if branch is None else (what, branch, i, m) for m in range(tiles)]
                if ready is None:
                    for m in range(tiles):
                        b = bank(keys[m])
                        done(tile(b, u, m * P, width, xh, xl), keys[m])
                else:
                    bs = [bank(key) for key in keys]
                    for k in range(CH):
                        pe.wait_ge(sem(ready), k + 1)
                        for m in range(tiles):
                            mm = tile(bs[m], u, m * P, width, xh, xl, ks=[k])
                            if k == CH - 1:
                                done(mm, keys[m])
                unit_last[u] = keys[-1]

            pe.wait_ge(sem("consts"), 2)
            pe.wait_ge(sem("par_loaded"), 16 * n_par_dmas)
            transposes(("par", 0), [par_rows[:, j, :] for j in range(4)])
            transposes(("par", 1), [par_rows[:, j, :] for j in range(4, PARAM_TILES)])
            pe.wait_ge(sem("x_loaded"), 16)
            for c in range(CH):
                transposes(("xT", c), [x_tok[:, t, c * P:c * P + P] for t in range(NT)])
            sum_chunks("ss_x", sq1, CH, T, "sq_x")

            oh, ol = op_hi, plain(op_lo)
            unit_tiles("qd", 0, oh, ol, ready="xn_ready")
            unit_tiles("kvi", 0, oh, ol)
            unit_tiles("wa", 0, oh, ol, tiles=1)
            for half in range(2):
                for what in "rkvg":
                    unit_tiles(what, half, oh, ol)
            for half in range(2):
                unit_tiles("ga", half, oh, ol)

            pe.wait_ge(sem("lora_loaded"), 32)
            pe.wait_ge(sem("tanh_ready"), 1)
            evacuated(pe, ("wa", 0, 0))
            pe.wait_ge(sem("consts"), 7)
            transposes("w_idx", [tmp[2][:, t * P:t * P + P] for t in range(NT)])
            for i in range(NI):
                b = bank(("z", i))
                done(nc.tensor.matmul(b[:, :], lora[0:32, i * P:i * P + P], tmp[2][0:32, 0:T], start=True, stop=True), ("z", i))
                b = bank(("a", i))
                done(nc.tensor.matmul(b[:, :], lora[32:64, i * P:i * P + P], tmp[2][32:64, 0:T], start=True, stop=True), ("a", i))
                b = bank(("kk", i))
                pe.wait_ge(sem("kk_sq"), i + 1)
                done(nc.tensor.matmul(b[:, :], pair_ones[:, :], prep[3][:, 0:T], start=True, stop=True), ("kk", i))
                b = bank(("bonus", i))
                pe.wait_ge(sem("rk_ready"), i + 1)
                done(nc.tensor.matmul(b[:, :], pair_ones[:, :], prep[3][:, 0:T], start=True, stop=True), ("bonus", i))

            pe.wait_ge(sem("prep_ready"), NI)
            for c in range(NT):
                cs = slice(c * P, c * P + P)
                for j, src in enumerate((vf, bt, kt)):
                    transposes(("tok", c, j), [src[:, i, cs] for i in range(NI)])
                for odd in range(2):
                    rows = slice(HD * odd, HD * odd + HD)
                    for name, stat in (("gb", bt), ("gk", kt)):
                        for i2 in range(2):
                            b = bank((name, c, odd, i2))
                            for n in range(2):
                                i = 2 * i2 + n
                                mm = nc.tensor.matmul(b[:, n * 256:n * 256 + 256], stat[rows, i, cs], ar[rows, i, :, cs],
                                                      start=True, stop=True)
                            done(mm, (name, c, odd, i2))
                    b = bank(("low", c, odd))
                    for i in range(NI):
                        mm = nc.tensor.matmul(b[:, i * P:i * P + P], ar[rows, i, 0, cs], bt[rows, i, cs], start=True, stop=True)
                    done(mm, ("low", c, odd))
                for lev in range(1, 7):
                    for odd in range(2):
                        hs = slice(NI * odd, NI * odd + NI)
                        if lev == 1:
                            pe.wait_ge(sem(f"inv_init{odd}"), c + 1)
                        else:
                            evacuated(pe, ("dinv", c, lev - 1, odd))
                            evacuated(pe, ("dinvT", c, lev - 1, odd))
                        b = bank(("w", c, lev, odd))
                        for i in range(NI):
                            h = NI * odd + i
                            mm = nc.tensor.matmul(b[:, i * P:i * P + P], low[:, h, :], inv[:, h, :], start=True, stop=True)
                        done(mm, ("w", c, lev, odd))
                    for odd in range(2):
                        evacuated(pe, ("w", c, lev, odd))
                        b = bank(("dinv", c, lev, odd))
                        for i in range(NI):
                            h = NI * odd + i
                            mm = nc.tensor.matmul(b[:, i * P:i * P + P], invT[:, h, :], wprod[:, h, :], start=True, stop=True)
                        done(mm, ("dinv", c, lev, odd))
                        if lev < 6:
                            b = bank(("dinvT", c, lev, odd))
                            for i in range(NI):
                                h = NI * odd + i
                                mm = nc.tensor.matmul(b[:, i * P:i * P + P], wprod[:, h, :], invT[:, h, :], start=True, stop=True)
                            done(mm, ("dinvT", c, lev, odd))
                V, B, K = tok[c % 2]
                for j in range(3):
                    evacuated(pe, ("tok", c, j))
                for odd in range(2):
                    for i2 in range(2):
                        evacuated(pe, ("gb", c, odd, i2))
                        evacuated(pe, ("gk", c, odd, i2))
                for odd in range(2):
                    rows = slice(HD * odd, HD * odd + HD)
                    if c > 0:
                        evacuated(pe, ("p", c - 1, odd))
                    b = bank(("scan_x", c, odd))
                    for i in range(NI):
                        h, f = NI * odd + i, P * i + HD * odd
                        if c > 0:
                            nc.tensor.matmul(b[:, i * HD:i * HD + HD], ar[rows, i, 0, cs], state[rows, i, :], start=True, stop=False)
                        mm = nc.tensor.matmul(b[:, i * HD:i * HD + HD], g_k[:, h, 0, :], V[:, f:f + HD], start=c == 0, stop=True)
                    done(mm, ("scan_x", c, odd))
                for odd in range(2):
                    evacuated(pe, ("dinv", c, 6, odd))
                    evacuated(pe, ("scan_x", c, odd))
                    b = bank(("scan_u", c, odd))
                    for i in range(NI):
                        h = NI * odd + i
                        mm = nc.tensor.matmul(b[:, i * HD:i * HD + HD], inv[:, h, :], xs_t[odd][:, i * HD:i * HD + HD], start=True, stop=True)
                    done(mm, ("scan_u", c, odd))
                for odd in range(2):
                    rows = slice(HD * odd, HD * odd + HD)
                    evacuated(pe, ("scan_u", c, odd))
                    b = bank(("yT", c, odd))
                    for i in range(NI):
                        h, f = NI * odd + i, P * i + HD * odd
                        o = b[rows, i * P:i * P + P]
                        if c > 0:
                            nc.tensor.matmul(o, state[rows, i, :], ar[rows, i, 1, cs], start=True, stop=False)
                        nc.tensor.matmul(o, us_t[odd][:, i * HD:i * HD + HD], g_b[:, h, 1, :], start=c == 0, stop=False)
                        mm = nc.tensor.matmul(o, V[:, f:f + HD], g_k[:, h, 1, :], start=False, stop=True)
                    done(mm, ("yT", c, odd))
                    if c < NT - 1:
                        b = bank(("p", c, odd))
                        for i in range(NI):
                            h, f = NI * odd + i, P * i + HD * odd
                            o = b[rows, i * HD:i * HD + HD]
                            if c > 0:
                                nc.tensor.matmul(o, ident[rows, rows], state[rows, i, :], start=True, stop=False)
                            nc.tensor.matmul(o, B[:, f:f + HD], us_t[odd][:, i * HD:i * HD + HD], start=c == 0, stop=False)
                            mm = nc.tensor.matmul(o, K[:, f:f + HD], V[:, f:f + HD], start=False, stop=True)
                        done(mm, ("p", c, odd))
            for i in range(NI):
                for odd in range(2):
                    evacuated(pe, ("yT", NT - 1, odd))
                b = bank(("gn_mean", i))
                done(nc.tensor.matmul(b[:, :], pair_ones[:, :], y_scan[:, i, :], start=True, stop=True), ("gn_mean", i))
                pe.wait_ge(sem("gn_sq"), i + 1)
                b = bank(("gn_var", i))
                done(nc.tensor.matmul(b[:, :], pair_ones[:, :], tmp[1][:, 0:T], start=True, stop=True), ("gn_var", i))

            pe.wait_ge(sem("sq_q"), 2)
            b = bank("ss_q")
            for m in range(2):
                mm = nc.tensor.matmul(b[:, :], ones[:, :], prob[m][:, :], start=m == 0, stop=m == 1)
            done(mm, "ss_q")
            pe.wait_ge(sem("sq_kv"), 1)
            b = bank("ss_kv")
            done(nc.tensor.matmul(b[:, :], ones[:, :], relu_t[0][:, :], start=True, stop=True), "ss_kv")
            b = bank("ki_mean")
            done(nc.tensor.matmul(b[:, :], pair_ones[:, :], kidx[:, :], start=True, stop=True), "ki_mean")
            pe.wait_ge(sem("ki_sq"), 1)
            b = bank("ki_var")
            done(nc.tensor.matmul(b[:, :], pair_ones[:, :], o_lat[0][:, :], start=True, stop=True), "ki_var")
            pe.wait_ge(sem("dsa_w"), 16 * 4)
            transposes("wukT", [wuk[:, i * P:i * P + P] for i in range(NI)])
            pe.wait_ge(sem("cq_ready"), 2)
            for i in range(NI):
                b = bank(("q", i))
                for m in range(2):
                    mm = nc.tensor.matmul(b[:, :], wuq[:, m, i * P:i * P + P], qd[:, m, :], start=m == 0, stop=m == 1)
                done(mm, ("q", i))
            for i in range(2):
                b = bank(("qi", i))
                for m in range(2):
                    mm = nc.tensor.matmul(b[:, :], wqi[:, m, i * P:i * P + P], qd[:, m, :], start=m == 0, stop=m == 1)
                done(mm, ("qi", i))
            pe.wait_ge(sem("ckv_ready"), 1)
            transposes("ckv_tok", [ckv[:, t * P:t * P + P] for t in range(NT)])
            pe.wait_ge(sem("kidx_ready"), 1)
            for i in range(2):
                evacuated(pe, ("qi", i))
            for qt in range(1, NT):
                for h in range(4):
                    rows = slice(HD * (h % 2), HD * (h % 2) + HD)
                    b = bank(("lg", qt, h))
                    done(nc.tensor.matmul(b[:, 0:P * (qt + 1)], qiT[rows, h // 2, qt * P:qt * P + P], kidx[rows, 0:P * (qt + 1)],
                                          start=True, stop=True), ("lg", qt, h))
            pe.wait_ge(sem("mem_loaded"), 16)
            for c in range(CH):
                transposes(("memT", c), [mem_tok[:, t, c * P:c * P + P] for t in range(2)])
            sum_chunks("ss_mem", sq_mem, CH, MEM, "sq_mem")
            for i in range(NI):
                evacuated(pe, ("q", i))
            evacuated(pe, "wukT")
            evacuated(pe, "ckv_tok")
            for h in range(NH):
                rows = slice(HD * (h % 2), HD * (h % 2) + HD)
                b = bank(("qa", h))
                done(nc.tensor.matmul(b[:, :], wukT[rows, h // 2, :], qT[rows, h // 2, :], start=True, stop=True), ("qa", h))
                evacuated(pe, ("qa", h))
                for qt in range(NT):
                    b = bank(("s", h, qt))
                    done(nc.tensor.matmul(b[:, 0:P * (qt + 1)], q_abs[h % 2][:, qt * P:qt * P + P], ckv[:, 0:P * (qt + 1)],
                                          start=True, stop=True), ("s", h, qt))
                for qt in range(NT):
                    pe.wait_ge(sem("prob_ready"), NT * h + qt + 1)
                    transposes(("pT", h, qt), [prob[qt % 2][:, k * P:k * P + P] for k in range(qt + 1)])
                for qt in range(NT):
                    evacuated(pe, ("pT", h, qt))
                b = bank(("ol", h))
                for k in range(NT):
                    mm = nc.tensor.matmul(b[:, k * P:T], ckv_tok[:, k, :], probT[:, k, k * P:T], start=k == 0, stop=k == NT - 1)
                done(mm, ("ol", h))
                evacuated(pe, ("ol", h))
                b = bank(("o", h))
                done(nc.tensor.matmul(b[rows, :], wuv[:, h * HD:h * HD + HD], o_lat[h % 2][:, :], start=True, stop=True), ("o", h))

            for i in range(4):
                unit_tiles("wout", i, oh, ol, ready=None if i else "mix_ready")
                if i:
                    sum_some("y", sq2, 2 * i - 2, 2 * i)
                    sum_some("yg", sq_g, 2 * i - 2, 2 * i)
            sum_some("y", sq2, CH - 2, CH)
            sum_some("yg", sq_g, CH - 2, CH)
            pe.wait_ge(sem("memn_ready"), CH)
            for i in range(4):
                unit_tiles("kT", i, memn_hi, plain(memn_lo), MEM)
            for i in range(4):
                u = next_unit("vm")
                b = bank(("vm", i))
                for t in range(2):
                    o = b[:, t * 256:t * 256 + 256]
                    for k in range(CH):
                        h, l = memn_hi[:, k, t * P:t * P + P], memn_lo[:, k, t * P:t * P + P]
                        nc.tensor.matmul(o, h, w_hi[u % 2][:, k, :], start=k == 0, stop=False)
                        nc.tensor.matmul(o, h, w_lo[u % 2][:, k, :], start=False, stop=False)
                        mm = nc.tensor.matmul(o, l, w_hi[u % 2][:, k, :], start=False, stop=k == CH - 1)
                done(mm, ("vm", i))
                unit_last[u] = ("vm", i)
            unit_tiles("u", 0, oh, ol, ready="mixn_ready")
            mh, ml = op2_hi, plain(op2_lo)

            def mem_scores(h):
                for m in range(2):
                    evacuated(pe, ("q2", h, m))
                    evacuated(pe, ("kT", h, m))
                for qt in range(NT):
                    b = bank(("s2", h, qt))
                    for k in range(2):
                        mm = nc.tensor.matmul(b[:, 0:MEM], work[:, 2 * h + k, qt * P:qt * P + P], memK[:, 2 * h + k, :],
                                              start=k == 0, stop=k == 1)
                    done(mm, ("s2", h, qt))

            def mem_probs(h):
                for qt in range(NT):
                    pe.wait_ge(sem("prob2_ready"), NT * h + qt + 1)
                    transposes(("p2T", h, qt), [prob2[qt][:, k * P:k * P + P] for k in range(2)])

            def mem_out(h):
                evacuated(pe, ("vm", h))
                for qt in range(NT):
                    evacuated(pe, ("p2T", h, qt))
                for d in range(2):
                    b = bank(("oc", h, d))
                    for k in range(2):
                        mm = nc.tensor.matmul(b[:, :], memV[:, k, 256 * h + P * d:256 * h + P * d + P], prob2T[:, k, :],
                                              start=k == 0, stop=k == 1)
                    done(mm, ("oc", h, d))

            unit_tiles("q2", 0, oh, ol)
            unit_tiles("q2", 1, oh, ol)
            mem_scores(0)
            unit_tiles("q2", 2, oh, ol)
            mem_probs(0)
            mem_scores(1)
            unit_tiles("q2", 3, oh, ol)
            mem_out(0)
            mem_probs(1)
            mem_scores(2)
            unit_tiles("u", 1, oh, ol)
            mem_out(1)
            mem_probs(2)
            mem_scores(3)
            unit_tiles("pg", 0, oh, ol, branch=2)
            mem_out(2)
            mem_probs(3)
            unit_tiles("u", 2, oh, ol)
            mem_out(3)

            def gated(branch):
                if branch == 2:
                    for h in range(MH):
                        for d in range(2):
                            evacuated(pe, ("oc", h, d))
                for i in range(4):
                    if branch < 2 or i:
                        unit_tiles("pg", i, oh, ol, branch=branch)
                    unit_tiles("y", i, mh, ml, branch=branch, ready=None if i or branch == 2 else f"op2_ready{branch}")
                    if branch == 2 and i:
                        unit_tiles("u", 2 + i, oh, ol)
                    if branch == 0 and i == 1:
                        sum_chunks("ln_mean", conv_b, CH, T, "conv_ready")
                    if branch == 0 and i == 2:
                        sum_chunks("ln_var", sq2, CH, T, "sq_ln")

            gated(2)
            for i in range(4):
                unit_tiles("gb", i, oh, ol)
                if i % 2:
                    unit_tiles("u", 6 + i // 2, oh, ol)
            for i in range(8):
                unit_tiles("cv", i, oh, ol)
            gated(0)
            gated(1)
            for i in range(4):
                unit_tiles("wo2", i, merged_hi, plain(merged_lo), ready=None if i else "merged_ready")
                if i:
                    sum_some("f", sq_f, 2 * i - 2, 2 * i)
            sum_some("f", sq_f, CH - 2, CH)
            for i in range(FC):
                unit_tiles("up", i, oh, ol, ready=None if i else "ffn_ready")
            for i in range(4):
                bs = None
                for k0 in (0, 8, 16):
                    u = next_unit("down")
                    if bs is None:
                        bs = [bank(("down", i, m)) for m in range(2)]
                    if i == 0:
                        pe.wait_ge(sem("act_ready"), k0 + units[u][2])
                    for m in range(2):
                        mm = tile(bs[m], u, m * P, T, act_hi,
                                  lambda k, w: act_lo[:, k, 0:w] if k < 16 else act_lo2[:, k - 16, 0:w],
                                  x0=k0, start=k0 == 0, stop=k0 == 16)
                        if k0 == 16:
                            done(mm, ("down", i, m))
                    if k0 < 16:
                        mm.then_inc(sem("down_used"), 1)
                        unit_last[u] = ("down_used", 2 * i + k0 // 8 + 1)
                    else:
                        unit_last[u] = ("down", i, 1)
                if i:
                    sum_some("fin", sq3, 2 * i - 2, 2 * i)
            sum_some("fin", sq3, CH - 2, CH)
            for g in range(2):
                pe.wait_ge(sem("fin_ready"), 4 * g + 4)
                for t in range(NT):
                    transposes(("out", t, g), [x_res[:, 4 * g + j, t * P:t * P + P] for j in range(4)])
            assert unit[0] == NU

        def slot_used(eng, u):
            key = unit_last[u]
            if key[0] == "down_used":
                eng.wait_ge(sem("down_used"), key[1])
            else:
                filled(eng, key)

        @block.sync
        def _(sp):
            x_d = dram["x"][0].rearrange("(t p) d -> p t d", p=P)
            sp.dma_start(x_tok[:, :, :], x_d).then_inc(sem("x_loaded"), 16)

            def load(u):
                _, _, nk, pieces = units[u]
                if u >= 2:
                    sp.wait_ge(hi_ready, u - 1)
                    sp.wait_ge(lo_ready, u - 1)
                for at_, w, col, n, k0 in pieces:
                    src = dram[w][0, k0 * P:(k0 + nk) * P, col:col + n].rearrange("(k p) n -> p k n", p=P)
                    sp.dma_start(w_raw[u % 2][:, 0:nk, at_:at_ + n], src).then_inc(w_arrived[u % 2], 16)

            for u in range(first_phase2_unit):
                load(u)
            for u in (first_phase2_unit - 2, first_phase2_unit - 1):
                sp.wait_ge(hi_ready, u + 1)
                sp.wait_ge(lo_ready, u + 1)
                slot_used(sp, u)
            dw = sem("dsa_w")
            sp.dma_start(wuq[:, :, :], dram["w_uq"][0].rearrange("(m p) n -> p m n", p=P)).then_inc(dw, 16)
            sp.dma_start(wqi[:, :, :], dram["w_qidx"][0].rearrange("(m p) n -> p m n", p=P)).then_inc(dw, 16)
            sp.dma_start(wuk[:, :].rearrange("p (h d) -> p h d", d=HD), dram["w_uk"][0].rearrange("h r d -> r h d")).then_inc(dw, 16)
            sp.dma_start(wuv[:, :].rearrange("p (h d) -> p h d", d=HD), dram["w_uv"][0].rearrange("h r d -> r h d")).then_inc(dw, 16)
            filled(sp, ("gn_mean", 0))
            sp.dma_start(mem_tok[:, :, :], dram["mem_2"][0].rearrange("(t p) d -> p t d", p=P)).then_inc(sem("mem_loaded"), 16)
            evacuated(sp, ("o", NH - 1))
            for u in range(first_phase2_unit, NU):
                load(u)
            for g in range(2):
                for t in range(NT):
                    evacuated(sp, ("out", t, g))
                    sp.dma_start(out[0, t * P:t * P + P, g * T:g * T + T], out_tok[t][:, g * T:g * T + T]).then_inc(sem("stored"), 16)
            sp.wait_ge(sem("stored"), 16 * 2 * NT)

        @block.gpsimd
        def _(pool):
            steps = [0]

            def step(ins):
                steps[0] += 1
                ins.then_inc(sem("pool_steps"), 1)
                pool.wait_ge(sem("pool_steps"), steps[0])

            step(nc.gpsimd.memset(par_rows[:, :, :], 0.0))
            nc.gpsimd.memset(ones[:, :], 1.0).then_inc(sem("consts"), 1)
            pool.wait_ge(sem("consts"), 1)
            nc.gpsimd.affine_select(out=ident[:, :], in_=ones[:, :], compare_op=ALU.is_equal, fill=0.0, base=0,
                                    pattern=[[-1, P]], channel_multiplier=1).then_inc(sem("consts"), 1)
            pool.wait_ge(sem("consts"), 2)
            step(nc.gpsimd.memset(pair_ones[:, :], 0.0))
            step(nc.gpsimd.memset(pair_ones[0:HD, 0:HD], 1.0))
            nc.gpsimd.memset(pair_ones[HD:P, HD:P], 1.0).then_inc(sem("consts"), 1)
            pool.wait_ge(sem("consts"), 3)
            nc.gpsimd.affine_select(out=mask_ar[:, 0, :], in_=ones[:, :], compare_op=ALU.is_gt, fill=0.0, base=0,
                                    pattern=[[1, P]], channel_multiplier=-1).then_inc(sem("consts"), 1)
            pool.wait_ge(sem("consts"), 4)
            nc.gpsimd.affine_select(out=mask_ar[:, 1, :], in_=ones[:, :], compare_op=ALU.is_ge, fill=0.0, base=0,
                                    pattern=[[1, P]], channel_multiplier=-1).then_inc(sem("consts"), 1)
            pool.wait_ge(sem("consts"), 5)
            nc.gpsimd.affine_select(out=mask_low[:, :], in_=ones[:, :], compare_op=ALU.is_gt, fill=0.0, base=0,
                                    pattern=[[-1, P]], channel_multiplier=1).then_inc(sem("consts"), 1)
            pool.wait_ge(sem("consts"), 6)
            step(nc.gpsimd.memset(mask_lev[:, :, :], 0.0))
            for n in range(7):
                b = 1 << n
                v = mask_lev[:, n, :].rearrange("p (k h c) -> p k h c", h=2, c=b)[:, :, 1, :]
                step(nc.gpsimd.memset(v, 1.0))
                step(nc.gpsimd.affine_select(out=v, in_=v, compare_op=ALU.is_ge, fill=0.0, base=0,
                                             pattern=[[-2 * b, P // (2 * b)], [0, b]], channel_multiplier=1))
                step(nc.gpsimd.affine_select(out=v, in_=v, compare_op=ALU.is_ge, fill=0.0, base=b - 1,
                                             pattern=[[2 * b, P // (2 * b)], [0, b]], channel_multiplier=-1))
            step(nc.gpsimd.memset(mask_lowT[:, :], 0.0))
            v = mask_lowT[:, :].rearrange("p (k h) -> p k h", h=2)[:, :, 0]
            step(nc.gpsimd.memset(v, 1.0))
            nc.gpsimd.affine_select(out=v, in_=v, compare_op=ALU.is_equal, fill=0.0, base=-1,
                                    pattern=[[-2, P // 2]], channel_multiplier=1).then_inc(sem("consts"), 1)
            pool.wait_ge(sem("consts"), 7)
            v = score[:, 0, 0:P]
            slot_used(pool, first_phase2_unit - 2)
            slot_used(pool, first_phase2_unit - 1)
            step(nc.gpsimd.memset(v, 0.0))
            nc.gpsimd.affine_select(out=v, in_=v, compare_op=ALU.is_ge, fill=MASKED, base=0,
                                    pattern=[[-1, P]], channel_multiplier=1).then_inc(sem("causal"), 1)
            pool.wait_ge(sem("causal"), 1)
            for qt in range(1, NT):
                v = score[:, qt, qt * P:qt * P + P]
                pool.wait_ge(sem("score_ready"), qt)
                nc.gpsimd.affine_select(out=v, in_=v, compare_op=ALU.is_ge, fill=MASKED, base=0,
                                        pattern=[[-1, P]], channel_multiplier=1).then_inc(sem("causal"), 1)

        @block.scalar
        def _(act):
            A = nc.scalar.activation
            split = [0]

            def split_hi(upto):
                while split[0] <= min(upto, NU - 1):
                    u = split[0]
                    split[0] += 1
                    nk = units[u][2]
                    act.wait_ge(w_arrived[u % 2], raw_count[u])
                    if u >= 2:
                        slot_used(act, u - 2)
                    A(w_hi[u % 2][:, 0:nk, :], w_raw[u % 2][:, 0:nk, :], ACT.Copy).then_inc(hi_ready, 1)

            roots = [0]

            def root(t=rs[:, :]):
                roots[0] += 1
                act.wait_ge(sem("var_ready"), roots[0])
                A(t, t, ACT.Sqrt).then_inc(sem("rs_ready"), 1)

            act.wait_ge(sem("pool_steps"), 1)
            for dst, src in par_dmas:
                act.dma_start(dst, src).then_inc(sem("par_loaded"), 16)
            for c in range(CH):
                b = take(act, ("xT", c))
                A(sq1[:, c, :], b[:, :], ACT.Square).then_inc(sem("sq_x"), 1)
                evac(A(x_res[:, c, :], b[:, :], ACT.Copy), ("xT", c))
            split_hi(1)
            root()
            filled(act, ("xT", CH - 1))
            filled(act, "ss_x")
            act.dma_start(lora[0:32, :], dram["w_up"][0]).then_inc(sem("lora_loaded"), 16)
            act.dma_start(lora[32:64, :], dram["a_up"][0]).then_inc(sem("lora_loaded"), 16)

            for m in range(2):
                evac(A(qd[:, m, :], take(act, ("qd", 0, m))[:, :], ACT.Copy), ("qd", 0, m))
            split_hi(2)
            evac(A(ckv[:, :], take(act, ("kvi", 0, 0))[:, :], ACT.Copy), ("kvi", 0, 0))
            evac(A(kidx[:, :], take(act, ("kvi", 0, 1))[:, :], ACT.Copy), ("kvi", 0, 1))
            split_hi(3)
            act.wait_ge(sem("derived"), 1)

            def unshifted(key, dst, col):
                A(dst, take(act, key)[:, :], ACT.Copy, scale=omm[:, col:col + 1]).then_inc(sem("unshifted"), 1)

            unshifted(("wa", 0, 0), tmp[2][:, 0:T], 12)
            split_hi(4)
            evacuated(act, ("wa", 0, 0))
            A(tmp[2][0:32, 0:T], tmp[2][0:32, 0:T], ACT.Tanh).then_inc(sem("tanh_ready"), 1)
            u = 3
            last = None
            for half in range(2):
                for w, dst in enumerate((lambda i: ar[:, i, 1, :], lambda i: kt[:, i, :], lambda i: vf[:, i, :])):
                    for m in range(2):
                        i = 2 * half + m
                        unshifted(("rkv"[w], half, m), dst(i), 4 * w + i)
                    u += 1
                    split_hi(u + 1)
                for m in range(2):
                    b = take(act, ("g", half, m))
                    if half:
                        evacuated(act, ("g", 0, m))
                    A(tmp[m][:, 0:T], b[:, :], ACT.Sigmoid).then_inc(sem("sig_g"), 1)
                u += 1
                split_hi(u + 1)
            for half in range(2):
                for m in range(2):
                    b = take(act, ("ga", half, m))
                    evacuated(act, ("ga", 0, m) if half else ("g", 1, m))
                    A(tmp[m][:, 0:T], b[:, :], ACT.Sigmoid).then_inc(sem("sig_g"), 1)
                u += 1
                split_hi(min(u + 1, first_phase2_unit - 1))

            for i in range(NI):
                if i:
                    act.wait_ge(sem("prep_ready"), i)
                evac(A(prep[0][:, 0:T], take(act, ("z", i))[:, :], ACT.Sigmoid, bias=pcol("w0", i)), ("z", i))
                evac(A(prep[1][:, 0:T], take(act, ("a", i))[:, :], ACT.Sigmoid, bias=pcol("a0", i)), ("a", i))
                if i:
                    filled(act, ("bonus", i - 1))
                else:
                    evacuated(act, ("k", 0, 0))
                A(prep[3][:, 0:T], kt[:, i, :], ACT.Square, scale=pcol("k_k", i)).then_inc(sem("kk_sq"), 1)
                evac(A(rs[:, :], take(act, ("kk", i))[:, :], ACT.Sqrt), ("kk", i))
                act.wait_ge(sem("cum_ready"), i + 1)
                A(tmp[0][:, 0:516], prep[2][:, 0:516], ACT.Exp, scale=-KAPPA).then_inc(sem("exps"), 1)
                A(tmp[1][:, 0:516], prep[2][:, 0:516], ACT.Exp, scale=KAPPA).then_inc(sem("exps"), 1)

            act.wait_ge(sem("prep_ready"), NI)
            for c in range(NT):
                for j in range(3):
                    evac(A(tok[c % 2][j][:, :], take(act, ("tok", c, j))[:, :], ACT.Copy), ("tok", c, j))
                for odd in range(2):
                    evac(A(xs_t[odd], take(act, ("scan_x", c, odd))[:, 0:256], ACT.Copy), ("scan_x", c, odd))
                for odd in range(2):
                    evac(A(us_t[odd], take(act, ("scan_u", c, odd))[:, 0:256], ACT.Copy), ("scan_u", c, odd))
                for odd in range(2):
                    rows = slice(HD * odd, HD * odd + HD)
                    b = take(act, ("yT", c, odd))
                    evac(A(y_scan[rows, :, c * P:c * P + P], b[rows, :].rearrange("p (i t) -> p i t", i=NI), ACT.Copy),
                         ("yT", c, odd))
            for i in range(NI):
                evacuated(act, ("gn_mean", i))
                A(tmp[1][:, 0:T], tmp[0][:, 0:T], ACT.Square).then_inc(sem("gn_sq"), 1)
                root()

            for m in range(2):
                slot_used(act, first_phase2_unit - 2 + m)
            for m in range(2):
                A(prob[m][:, :], qd[:, m, :], ACT.Square).then_inc(sem("sq_q"), 1)
            A(relu_t[0][:, :], ckv[:, :], ACT.Square).then_inc(sem("sq_kv"), 1)
            root()
            root()
            evacuated(act, "ki_mean")
            A(o_lat[0][:, :], kidx[:, :], ACT.Square).then_inc(sem("ki_sq"), 1)
            root()
            evac(A(wukT[:, :, :], take(act, "wukT")[:, :].rearrange("p (i r) -> p i r", i=NI), ACT.Copy), "wukT")
            for i in range(NI):
                evac(A(qT[:, i, :], take(act, ("q", i))[:, :], ACT.Copy), ("q", i))
            for i in range(2):
                evac(A(qiT[:, i, :], take(act, ("qi", i))[:, :], ACT.Copy), ("qi", i))
            evac(A(ckv_tok[:, :, :], take(act, "ckv_tok")[:, :].rearrange("p (i r) -> p i r", i=NT), ACT.Copy), "ckv_tok")
            n = 0
            for qt in range(1, NT):
                for h in range(4):
                    if n:
                        act.wait_ge(sem("relu_used"), n)
                    n += 1
                    w = P * (qt + 1)
                    evac(A(relu_t[0][:, 0:w], take(act, ("lg", qt, h))[:, 0:w], ACT.Relu), ("lg", qt, h))
            for c in range(CH):
                b = take(act, ("memT", c))
                A(sq_mem[:, c, :], b[:, 0:MEM], ACT.Square).then_inc(sem("sq_mem"), 1)
                evac(A(memT[:, c, :], b[:, 0:MEM], ACT.Copy), ("memT", c))
            root()
            for h in range(NH):
                evac(A(q_abs[h % 2][:, :], take(act, ("qa", h))[:, :], ACT.Copy, scale=HD ** -0.5), ("qa", h))
                for qt in range(NT):
                    act.wait_ge(sem("max_ready"), NT * h + qt + 1)
                    p = prob[qt % 2][:, 0:P * (qt + 1)]
                    A(p, p, ACT.Exp, bias=negmax[:, qt:qt + 1], accum_out=sums[:, qt:qt + 1]).then_inc(sem("exp_ready"), 1)
                evac(A(o_lat[h % 2][:, :], take(act, ("ol", h))[:, :], ACT.Copy), ("ol", h))

            act.wait_ge(sem("mix_ready"), CH)
            u = first_phase2_unit
            split_hi(u + 1)

            def after_unit():
                nonlocal u
                split_hi(u + 2)
                u += 1

            for i in range(4):
                filled(act, ("wout", i, 1))
                after_unit()
                for c in (2 * i, 2 * i + 1):
                    evacuated(act, ("wout", i, c % 2))
                    A(sq2[:, c, :], x_res[:, c, :], ACT.Square).then_inc(sem("sq_y"), 1)
                    A(sq_g[:, c, :], x_res[:, c, :], ACT.Square, scale=pcol("final_g", c)).then_inc(sem("sq_yg"), 1)
            root()
            root(rs_mix)
            for i in range(4):
                for m in range(2):
                    evac(A(memK[:, 2 * i + m, :], take(act, ("kT", i, m))[:, 0:MEM], ACT.Copy), ("kT", i, m))
                after_unit()
            for i in range(4):
                b = take(act, ("vm", i))
                evac(A(memV[:, :, 256 * i:256 * i + 256], b[:, :].rearrange("p (t n) -> p t n", t=2), ACT.Copy), ("vm", i))
                after_unit()

            def u_gate(i):
                if i:
                    evacuated(act, ("u", i - 1, 0))
                evac(A(u_sig, take(act, ("u", i, 1))[:, :], ACT.Sigmoid), ("u", i, 1))
                after_unit()

            def mem_query(i):
                for m in range(2):
                    evac(A(work[:, 2 * i + m, :], take(act, ("q2", i, m))[:, :], ACT.Copy), ("q2", i, m))
                after_unit()

            def mem_exp(h):
                for qt in range(NT):
                    act.wait_ge(sem("max2_ready"), NT * h + qt + 1)
                    if h:
                        filled(act, ("p2T", h - 1, qt))
                    b = take(act, ("s2", h, qt))
                    evac(A(prob2[qt][:, :], b[:, 0:MEM], ACT.Exp, scale=1.0 / 16, bias=negmax[:, qt:qt + 1],
                           accum_out=sums[:, qt:qt + 1]), ("s2", h, qt))

            def gate(branch, i, before):
                for m in range(2):
                    if before is not None:
                        evacuated(act, ("y", *before, m))
                    evac(A(gates[m][:, :], take(act, ("pg", branch, i, m))[:, :], ACT.Sigmoid,
                           bias=pcol("b_gate_2", 8 * branch + 2 * i + m)), ("pg", branch, i, m))
                after_unit()

            u_gate(0)
            mem_query(0)
            mem_query(1)
            mem_exp(0)
            mem_query(2)
            mem_exp(1)
            mem_query(3)
            mem_exp(2)
            u_gate(1)
            mem_exp(3)
            gate(2, 0, None)
            u_gate(2)

            def gate_steps(branch, before):
                for i in range(4):
                    if branch < 2 or i:
                        gate(branch, i, (branch, i - 1) if i else before)
                    filled(act, ("y", branch, i, 1))
                    after_unit()
                    if branch == 2 and i:
                        u_gate(2 + i)
                    if branch == 0 and i == 1:
                        evacuated(act, "ln_mean")
                        for c in range(CH):
                            A(sq2[:, c, :], conv_b[:, c, :], ACT.Square).then_inc(sem("sq_ln"), 1)
                    if branch == 0 and i == 2:
                        root()
                        for c in range(CH):
                            act.wait_ge(sem("ln_scaled"), c + 1)
                            A(tmp[1][:, 0:T], tmp[0][:, 0:T], ACT.Sigmoid, bias=pcol("ln_b_b_2", c)).then_inc(sem("ln_sig"), 1)

            gate_steps(2, None)
            for i in range(4):
                for m in range(2):
                    evac(A(work[:, 2 * i + m, :], take(act, ("gb", i, m))[:, :], ACT.Copy), ("gb", i, m))
                after_unit()
                if i % 2:
                    u_gate(6 + i // 2)
            for i in range(8):
                if i:
                    evacuated(act, ("cv", i - 1, 1))
                evac(A(tmp[0][:, 0:T], take(act, ("cv", i, 0))[:, :], ACT.Copy), ("cv", i, 0))
                filled(act, ("cv", i, 1))
                after_unit()
            gate_steps(0, (2, 3))
            gate_steps(1, (0, 3))
            for i in range(4):
                filled(act, ("wo2", i, 1))
                after_unit()
                for c in (2 * i, 2 * i + 1):
                    evacuated(act, ("wo2", i, c % 2))
                    A(sq_f[:, c, :], x_res[:, c, :], ACT.Square).then_inc(sem("sq_f"), 1)
            root()
            for i in range(FC):
                for m in range(2):
                    if i >= 2:
                        act.wait_ge(sem("act_ready"), i - 1)
                    A(conv_f[i % 2][m][:, 0:T], take(act, ("up", i, m))[:, :], ACT.Copy,
                      scale=pcol("conv_ffn_w_2", 4 * FC + FC * m + i)).then_inc(sem("tap_ready"), 1)
                after_unit()
                evacuated(act, ("up", i, 0))
                A(sig_f[i % 2][:, 0:T], conv_f[i % 2][0][:, 0:T], ACT.Sigmoid).then_inc(sem("cg_sig"), 1)
            for i in range(4):
                for n in range(3):
                    slot_used(act, u)
                    after_unit()
                for c in (2 * i, 2 * i + 1):
                    evacuated(act, ("down", i, c % 2))
                    A(sq3[:, c, :], x_res[:, c, :], ACT.Square).then_inc(sem("sq_fin"), 1)
            root()
            for g in range(2):
                for t in range(0, NT, 2):
                    evac(A(out_tok[t][:, g * T:g * T + T], take(act, ("out", t, g))[:, :], ACT.Copy), ("out", t, g))

        @block.vector
        def _(dve):
            V = nc.vector
            steps = [0]

            def link(ins):
                steps[0] += 1
                ins.then_inc(sem("dve_steps"), 1)
                dve.wait_ge(sem("dve_steps"), steps[0])

            split = [0]

            def split_lo(upto):
                while split[0] <= min(upto, NU - 1):
                    u = split[0]
                    split[0] += 1
                    nk = units[u][2]
                    dve.wait_ge(hi_ready, u + 1)
                    if u >= 2:
                        slot_used(dve, u - 2)
                    V.tensor_tensor(w_lo[u % 2][:, 0:nk, :], w_raw[u % 2][:, 0:nk, :],
                                    w_hi[u % 2][:, 0:nk, :].bitcast(F32), ALU.subtract).then_inc(lo_ready, 1)

            roots = [0]

            def variance(key, width, scale, eps):
                b = take(dve, key)
                evac(V.tensor_scalar(rs[:, 0:width], b[:, 0:width], scale, eps, ALU.mult, ALU.add), key)
                evacuated(dve, key)
                V.reciprocal(rs[:, 0:width], rs[:, 0:width]).then_inc(sem("var_ready"), 1)
                roots[0] += 1
                dve.wait_ge(sem("rs_ready"), roots[0])

            def parts(src, hi, lo, name):
                link(V.tensor_copy(hi, src))
                V.tensor_tensor(lo, src, hi.bitcast(F32), ALU.subtract).then_inc(sem(name), 1)

            def normed_chunk(src, gain, c, width, r, hi, lo, name):
                t = tmp[c % 2][:, 0:width]
                link(V.scalar_tensor_tensor(t, src[:, c, 0:width], pcol(gain, c), r[:, 0:width], ALU.mult, ALU.mult))
                parts(t, hi[:, c, 0:width], lo[:, c, 0:width], name)

            def normed(src, gain, width, hi, lo, name):
                for c in range(CH):
                    normed_chunk(src, gain, c, width, rs, hi, lo, name)

            evac(V.tensor_copy(par[:, 0:T], take(dve, ("par", 0))[:, :]), ("par", 0))
            evac(V.tensor_copy(par[:, T:PARAM_TILES * P], take(dve, ("par", 1))[:, 0:PARAM_TILES * P - T]), ("par", 1))
            evacuated(dve, ("par", 0))
            evacuated(dve, ("par", 1))
            c0 = PARAM_AT["mu_r"]
            link(V.tensor_scalar(omm, par[:, c0:c0 + 13], -1.0, 1.0, ALU.mult, ALU.add))
            c0 = PARAM_AT["k_a"]
            V.tensor_scalar(omka, par[:, c0:c0 + 4], -1.0, 1.0, ALU.mult, ALU.add).then_inc(sem("derived"), 1)
            dve.wait_ge(sem("derived"), 1)
            split_lo(1)
            variance("ss_x", T, 1.0 / D, NORM_EPS)
            for c in range(CH):
                evacuated(dve, ("xT", c))
            normed(x_res, "norm_g", T, op_hi, op_lo, "xn_ready")

            sh = [0]

            def shift(key, dst, mu):
                sh[0] += 1
                b = take(dve, key)
                dve.wait_ge(sem("unshifted"), sh[0])
                evac(V.scalar_tensor_tensor(dst[:, 1:T], b[:, 0:T - 1], mu, dst[:, 1:T], ALU.mult, ALU.add), key)

            filled(dve, ("qd", 0, 1))
            split_lo(2)
            filled(dve, ("kvi", 0, 1))
            split_lo(3)
            shift(("wa", 0, 0), tmp[2], pcol("mu_wa"))
            split_lo(4)
            u = 3
            for half in range(2):
                for w, dst in enumerate((lambda i: ar[:, i, 1, :], lambda i: kt[:, i, :], lambda i: vf[:, i, :])):
                    for m in range(2):
                        i = 2 * half + m
                        shift(("rkv"[w], half, m), dst(i), pcol("mu_" + "rkv"[w], i))
                    u += 1
                    split_lo(u + 1)
                for m in range(2):
                    b = take(dve, ("g", half, m))
                    dve.wait_ge(sem("sig_g"), 2 * half + m + 1)
                    evac(V.tensor_tensor(gate_r[:, 2 * half + m, :], b[:, :], tmp[m][:, 0:T], ALU.mult), ("g", half, m))
                u += 1
                split_lo(u + 1)
            for half in range(2):
                for m in range(2):
                    b = take(dve, ("ga", half, m))
                    dve.wait_ge(sem("sig_g"), 4 + 2 * half + m + 1)
                    evac(V.tensor_tensor(gate_a[:, 2 * half + m, :], b[:, :], tmp[m][:, 0:T], ALU.mult), ("ga", half, m))
                u += 1
                split_lo(min(u + 1, first_phase2_unit - 1))

            b = take(dve, "w_idx")[:, :].rearrange("p (t n) -> p t n", t=NT)[:, :, HD:HD + 4]
            evac(V.tensor_scalar(w_idx.rearrange("p (t n) -> p t n", t=NT), b, 0.5, None, ALU.mult), "w_idx")
            cum = prep[2][:, 0:516].rearrange("p (c t) -> p c t", c=NT)
            link(V.memset(prep[2][:, 0:516], 0.0))
            e_down = tmp[0][:, 0:516].rearrange("p (c t) -> p c t", c=NT)
            e_up = tmp[1][:, 0:516].rearrange("p (c t) -> p c t", c=NT)

            def chunked(t):
                return t.rearrange("p (c t) -> p c t", c=NT)

            mid = negmax[:, 0:NT]
            for half in range(2):
                for m in range(2):
                    evacuated(dve, ("r", half, m))
                    evacuated(dve, ("k", half, m))
                    evacuated(dve, ("v", half, m))
                    evacuated(dve, ("ga", half, m))
            for i in range(NI):
                evacuated(dve, ("z", i))
                if i:
                    link(V.memset(cum[:, :, 0:1], 0.0))
                for c in range(NT):
                    ins = V.tensor_tensor_scan(cum[:, c, 1:P + 1], ones[:, :], prep[0][:, c * P:c * P + P], 0.0, ALU.mult, ALU.add)
                    link(ins)
                link(V.tensor_copy(mid, cum[:, :, HD]))
                V.tensor_tensor(cum, cum, mid.unsqueeze(2).to_broadcast([P, NT, P + 1]), ALU.subtract)\
                    .then_inc(sem("cum_ready"), 1)
                dve.wait_ge(sem("cum_ready"), i + 1)
                link(V.tensor_scalar(prep[0][:, 0:T], kt[:, i, :], pcol("k_k", i), None, ALU.mult))
                evacuated(dve, ("kk", i))
                link(V.tensor_scalar(rs[:, :], rs[:, :], 1e-12, None, ALU.max))
                link(V.reciprocal(rs[:, :], rs[:, :]))
                link(V.tensor_tensor(prep[0][:, 0:T], prep[0][:, 0:T], rs[:, :], ALU.mult))
                evacuated(dve, ("a", i))
                link(V.tensor_scalar(rs[:, :], prep[1][:, 0:T], pcol("k_a", i), omka[:, i:i + 1], ALU.mult, ALU.add))
                link(V.tensor_tensor(kt[:, i, :], kt[:, i, :], rs[:, :], ALU.mult))
                V.scalar_tensor_tensor(prep[3][:, 0:T], ar[:, i, 1, :], pcol("r_k", i), kt[:, i, :], ALU.mult, ALU.mult)\
                    .then_inc(sem("rk_ready"), 1)
                link(V.tensor_tensor(prep[1][:, 0:T], prep[0][:, 0:T], prep[1][:, 0:T], ALU.mult))
                dve.wait_ge(sem("exps"), 2 * i + 2)
                V.tensor_tensor(dec.rearrange("p (i c) -> p i c", i=NI)[:, i, 0:NT - 1], e_up[:, 1:NT, 0], e_down[:, 0:NT - 1, P],
                                ALU.mult)
                V.tensor_tensor(chunked(bt[:, i, :]), chunked(prep[1][:, 0:T]), e_up[:, :, 1:P + 1], ALU.mult)
                V.scalar_tensor_tensor(chunked(ar[:, i, 0, :]), chunked(prep[0][:, 0:T]), -1.0, e_down[:, :, 0:P], ALU.mult, ALU.mult)
                dve.wait_ge(sem("rk_ready"), i + 1)
                V.tensor_tensor(chunked(ar[:, i, 1, :]), chunked(ar[:, i, 1, :]), e_down[:, :, 1:P + 1], ALU.mult)
                b = take(dve, ("bonus", i))
                evac(V.tensor_tensor(bonus_v[:, i, :], b[:, :], vf[:, i, :], ALU.mult), ("bonus", i))
                V.tensor_tensor(chunked(kt[:, i, :]), chunked(kt[:, i, :]), e_up[:, :, 1:P + 1], ALU.mult).then_inc(sem("prep_ready"), 1)

            dve.wait_ge(sem("prep_ready"), NI)
            for c in range(NT):
                for odd in range(2):
                    hs = slice(NI * odd, NI * odd + NI)
                    for name, dst in (("gb", g_b), ("gk", g_k)):
                        for i2 in range(2):
                            h = NI * odd + 2 * i2
                            b = take(dve, (name, c, odd, i2))[:, :].rearrange("p (n a t) -> p n a t", n=2, a=2)
                            evac(V.tensor_tensor(dst[:, h:h + 2, :, :], b, mask_ar[:, :, :].unsqueeze(1).to_broadcast([P, 2, 2, P]),
                                                 ALU.mult), (name, c, odd, i2))
                    b = take(dve, ("low", c, odd))[:, :].rearrange("p (i t) -> p i t", i=NI)
                    evac(V.tensor_tensor(low[:, hs, :], b, mask_low[:, :].unsqueeze(1).to_broadcast([P, NI, P]), ALU.mult),
                         ("low", c, odd))
                    evacuated(dve, ("gb", c, odd, 0))
                    evacuated(dve, ("gb", c, odd, 1))
                    evacuated(dve, ("low", c, odd))
                    eye = ident[:, :].unsqueeze(1).to_broadcast([P, NI, P])
                    V.tensor_tensor(inv[:, hs, :], g_b[:, hs, 0, :], mask_lev[:, 0, :].unsqueeze(1).to_broadcast([P, NI, P]), ALU.mult)
                    link(V.tensor_tensor(invT[:, hs, :], low[:, hs, :], mask_lowT[:, :].unsqueeze(1).to_broadcast([P, NI, P]), ALU.mult))
                    link(V.tensor_tensor(inv[:, hs, :], inv[:, hs, :], eye, ALU.add))
                    V.tensor_tensor(invT[:, hs, :], invT[:, hs, :], eye, ALU.add).then_inc(sem(f"inv_init{odd}"), 1)
                    dve.wait_ge(sem(f"inv_init{odd}"), c + 1)
                for lev in range(1, 7):
                    for odd in range(2):
                        hs = slice(NI * odd, NI * odd + NI)
                        b = take(dve, ("w", c, lev, odd))[:, :].rearrange("p (i t) -> p i t", i=NI)
                        evac(V.tensor_tensor(wprod[:, hs, :], b, mask_lev[:, lev, :].unsqueeze(1).to_broadcast([P, NI, P]), ALU.mult),
                             ("w", c, lev, odd))
                    for odd in range(2):
                        hs = slice(NI * odd, NI * odd + NI)
                        for name, dst in (("dinv", inv), ("dinvT", invT))[0:2 if lev < 6 else 1]:
                            b = take(dve, (name, c, lev, odd))[:, :].rearrange("p (i t) -> p i t", i=NI)
                            if lev > 1:
                                evacuated(dve, (name, c, lev - 1, odd))
                            evac(V.tensor_tensor(dst[:, hs, :], b, dst[:, hs, :], ALU.add), (name, c, lev, odd))
                if c < NT - 1:
                    for odd in range(2):
                        rows = slice(HD * odd, HD * odd + HD)
                        b = take(dve, ("p", c, odd))[rows, 0:256].rearrange("p (i d) -> p i d", i=NI)
                        f = dec[rows, :].rearrange("p (i c) -> p i c", i=NI)[:, :, c]
                        evac(V.tensor_tensor(state[rows, :, :], b, f.unsqueeze(2).to_broadcast([HD, NI, HD]), ALU.mult), ("p", c, odd))

            for i in range(NI):
                b = take(dve, ("gn_mean", i))
                evac(V.scalar_tensor_tensor(tmp[0][:, 0:T], b[:, :], -1.0 / HD, y_scan[:, i, :], ALU.mult, ALU.add), ("gn_mean", i))
                variance(("gn_var", i), T, 1.0 / HD, GN_EPS)
                link(V.scalar_tensor_tensor(tmp[0][:, 0:T], tmp[0][:, 0:T], pcol("gn_g", i), rs[:, :], ALU.mult, ALU.mult))
                link(V.scalar_tensor_tensor(tmp[0][:, 0:T], tmp[0][:, 0:T], pcol("gn_b", i), bonus_v[:, i, :], ALU.add, ALU.add))
                link(V.tensor_tensor(gate_r[:, i, :], tmp[0][:, 0:T], gate_r[:, i, :], ALU.mult))

            variance("ss_q", T, 1.0 / 256, NORM_EPS)
            for m in range(2):
                V.scalar_tensor_tensor(qd[:, m, :], qd[:, m, :], pcol("q_norm_g", m), rs[:, :], ALU.mult, ALU.mult)\
                    .then_inc(sem("cq_ready"), 1)
            dve.wait_ge(sem("cq_ready"), 2)
            variance("ss_kv", T, 1.0 / P, NORM_EPS)
            V.scalar_tensor_tensor(ckv[:, :], ckv[:, :], pcol("kv_norm_g"), rs[:, :], ALU.mult, ALU.mult).then_inc(sem("ckv_ready"), 1)
            dve.wait_ge(sem("ckv_ready"), 1)
            b = take(dve, "ki_mean")
            evac(V.scalar_tensor_tensor(kidx[:, :], b[:, :], -1.0 / HD, kidx[:, :], ALU.mult, ALU.add), "ki_mean")
            variance("ki_var", T, 1.0 / HD, LN_EPS)
            link(V.scalar_tensor_tensor(kidx[:, :], kidx[:, :], pcol("kidx_g"), rs[:, :], ALU.mult, ALU.mult))
            V.tensor_scalar(kidx[:, :], kidx[:, :], pcol("kidx_b"), None, ALU.add).then_inc(sem("kidx_ready"), 1)
            evacuated(dve, "w_idx")
            for qt in range(1, NT):
                w = P * (qt + 1)
                s = score[:, qt, 0:w]
                for h in range(4):
                    evacuated(dve, ("lg", qt, h))
                    wi = w_idx[:, 4 * qt + h:4 * qt + h + 1]
                    if h:
                        ins = V.scalar_tensor_tensor(s, relu_t[0][:, 0:w], wi, s, ALU.mult, ALU.add)
                    else:
                        ins = V.tensor_scalar(s, relu_t[0][:, 0:w], wi, None, ALU.mult)
                    ins.then_inc(sem("relu_used"), 1)
                    dve.wait_ge(sem("relu_used"), 4 * (qt - 1) + h + 1)
                V.tensor_copy(top8, s[:, 0:8]).then_inc(sem("score_ready"), 1)
            for qt in range(1, NT):
                s = score[:, qt, 0:P * (qt + 1)]
                dve.wait_ge(sem("causal"), qt + 1)
                dve.wait_ge(sem("score_ready"), 3)
                for n in range(TOPK // 8):
                    link(V.max(top8, s))
                    link(V.match_replace(s, top8, s, TAKEN))
                link(V.tensor_scalar(s, s, -2.0e38, MASKED, ALU.is_gt, ALU.mult))
            dve.wait_ge(sem("causal"), 1)
            for c in range(CH):
                evacuated(dve, ("memT", c))
            variance("ss_mem", MEM, 1.0 / D, EPS2)
            for h in range(NH):
                for n in range(NT + 2):
                    if n < NT:
                        w = P * (n + 1)
                        if n >= 2:
                            filled(dve, ("pT", h, n - 2))
                        p = prob[n % 2][:, 0:w]
                        b = take(dve, ("s", h, n))
                        evac(V.tensor_tensor(p, b[:, 0:w], score[:, n, 0:w], ALU.add), ("s", h, n))
                        evacuated(dve, ("s", h, n))
                        V.tensor_reduce(negmax[:, n:n + 1], p, X_AXIS, ALU.max, negate=True).then_inc(sem("max_ready"), 1)
                    if 0 <= n - 1 < NT:
                        q = n - 1
                        p = prob[q % 2][:, 0:P * (q + 1)]
                        dve.wait_ge(sem("exp_ready"), NT * h + q + 1)
                        link(V.reciprocal(rsum[:, q:q + 1], sums[:, q:q + 1]))
                        V.tensor_scalar(p, p, rsum[:, q:q + 1], None, ALU.mult).then_inc(sem("prob_ready"), 1)
                    if 0 <= n - 2:
                        q = n - 2
                        b = take(dve, ("pT", h, q))[:, 0:P * (q + 1)].rearrange("p (k t) -> p k t", t=P)
                        evac(V.tensor_copy(probT[:, 0:q + 1, q * P:q * P + P], b), ("pT", h, q))
                rows, i = slice(HD * (h % 2), HD * (h % 2) + HD), h // 2
                b = take(dve, ("o", h))
                evac(V.tensor_tensor(gate_a[rows, i, :], b[rows, :], gate_a[rows, i, :], ALU.mult), ("o", h))
                normed_chunk(memT, "norm_mem_g_2", h, MEM, rs, memn_hi, memn_lo, "memn_ready")
            for h in range(NH):
                evacuated(dve, ("o", h))
            for c in range(CH):
                src = gate_r[:, c, :] if c < NI else gate_a[:, c - NI, :]
                parts(src, op_hi[:, c, :], op_lo[:, c, :], "mix_ready")
            u = first_phase2_unit
            split_lo(u + 1)

            def after_unit():
                nonlocal u
                split_lo(u + 2)
                u += 1

            def residual(what, i):
                for m in range(2):
                    b = take(dve, (what, i, m))
                    x = x_res[:, 2 * i + m, :]
                    evac(V.tensor_tensor(x, b[:, :], x, ALU.add), (what, i, m))

            for i in range(4):
                residual("wout", i)
                after_unit()
            for i in range(4):
                for m in range(2):
                    evacuated(dve, ("wout", i, m))
            variance("y", T, 1.0 / D, NORM_EPS)
            evac(V.tensor_tensor(rs_mix, take(dve, "yg")[:, :], rs[:, :], ALU.mult), "yg")
            evacuated(dve, "yg")
            link(V.tensor_tensor(rs_mix, rs_mix, rs[:, :], ALU.mult))
            link(V.tensor_scalar(rs_mix, rs_mix, 1.0 / D, EPS2, ALU.mult, ALU.add))
            V.reciprocal(rs_mix, rs_mix).then_inc(sem("var_ready"), 1)
            roots[0] += 1

            def mix_norm(c):
                x = x_res[:, c, :]
                link(V.scalar_tensor_tensor(x, x, pcol("final_g", c), rs[:, :], ALU.mult, ALU.mult))
                if c == 0:
                    dve.wait_ge(sem("rs_ready"), roots[0])
                normed_chunk(x_res, "norm_mix_g_2", c, T, rs_mix, op_hi, op_lo, "mixn_ready")

            for i in range(4):
                mix_norm(i)
                filled(dve, ("kT", i, 1))
                after_unit()
            for i in range(4):
                mix_norm(4 + i)
                filled(dve, ("vm", i))
                after_unit()

            for s_ in range(2):
                link(V.memset(pad_b[s_][:, 0:KB - 1], 0.0))
            taps = [0]

            def conv_taps(n):
                for _ in range(n):
                    i, k = divmod(taps[0], KB)
                    if i == CH:
                        return
                    taps[0] += 1
                    pad, y = pad_b[i % 2], conv_b[:, i, :]
                    if k == 0:
                        evacuated(dve, ("u", i, 0))
                        ins = V.tensor_scalar(y, pad[:, 0:T], pcol("conv_b_w_2", i), pcol("conv_b_bias_2", i), ALU.mult, ALU.add)
                    else:
                        ins = V.scalar_tensor_tensor(y, pad[:, k:k + T], pcol("conv_b_w_2", 8 * k + i), y, ALU.mult, ALU.add)
                    if k < KB - 1:
                        link(ins)
                    else:
                        ins.then_inc(sem("conv_ready"), 1)

            def u_input(i):
                if taps[0] < KB * (i - 1):
                    conv_taps(KB * (i - 1) - taps[0])
                evacuated(dve, ("u", i, 1))
                b = take(dve, ("u", i, 0))
                if i >= 2:
                    dve.wait_ge(sem("conv_ready"), i - 1)
                evac(V.tensor_tensor(pad_b[i % 2][:, KB - 1:KB - 1 + T], b[:, :], u_sig, ALU.mult), ("u", i, 0))
                after_unit()

            def mem_softmax(h):
                for n in range(NT + 1):
                    if n < NT:
                        b = take(dve, ("s2", h, n))
                        link(V.tensor_reduce(negmax[:, n:n + 1], b[:, 0:MEM], X_AXIS, ALU.max, negate=True))
                        V.tensor_scalar(negmax[:, n:n + 1], negmax[:, n:n + 1], 1.0 / 16, None, ALU.mult).then_inc(sem("max2_ready"), 1)
                    if n:
                        q = n - 1
                        evacuated(dve, ("s2", h, q))
                        link(V.reciprocal(rsum[:, q:q + 1], sums[:, q:q + 1]))
                        V.tensor_scalar(prob2[q][:, :], prob2[q][:, :], rsum[:, q:q + 1], None, ALU.mult).then_inc(sem("prob2_ready"), 1)

            def mem_probs(h):
                for q in range(NT):
                    b = take(dve, ("p2T", h, q))[:, 0:MEM].rearrange("p (k t) -> p k t", t=P)
                    evac(V.tensor_copy(prob2T[:, :, q * P:q * P + P], b), ("p2T", h, q))

            def mem_out(h):
                for d in range(2):
                    b = take(dve, ("oc", h, d))
                    hi = op2_hi[:, 2 * h + d, :]
                    link(V.tensor_copy(hi, b[:, :]))
                    ins = V.tensor_tensor(op2_lo[:, 2 * h + d, :], b[:, :], hi.bitcast(F32), ALU.subtract)
                    evac(ins, ("oc", h, d))

            def after_query(i):
                filled(dve, ("q2", i, 1))
                after_unit()

            u_input(0)
            conv_taps(5)
            after_query(0)
            conv_taps(5)
            after_query(1)
            mem_softmax(0)
            after_query(2)
            mem_probs(0)
            mem_softmax(1)
            conv_taps(5)
            after_query(3)
            mem_out(0)
            mem_probs(1)
            mem_softmax(2)
            u_input(1)
            mem_out(1)
            mem_probs(2)
            mem_softmax(3)
            conv_taps(6)
            filled(dve, ("pg", 2, 0, 1))
            after_unit()
            mem_out(2)
            mem_probs(3)
            conv_taps(10)
            u_input(2)
            mem_out(3)

            def gate_steps(branch):
                for i in range(4):
                    if branch < 2 or i:
                        filled(dve, ("pg", branch, i, 1))
                        after_unit()
                    for m in range(2):
                        evacuated(dve, ("pg", branch, i, m))
                        b = take(dve, ("y", branch, i, m))
                        mg = merged[:, 2 * i + m, :]
                        if branch == 2:
                            evac(V.tensor_tensor(mg, b[:, :], gates[m][:, :], ALU.mult), ("y", branch, i, m))
                        else:
                            evac(V.tensor_tensor(tmp[2][:, 0:T], b[:, :], gates[m][:, :], ALU.mult), ("y", branch, i, m))
                            evacuated(dve, ("y", branch, i, m))
                            link(V.tensor_tensor(mg, mg, tmp[2][:, 0:T], ALU.add))
                        if branch == 1:
                            parts(mg, merged_hi[:, 2 * i + m, :], merged_lo[:, 2 * i + m, :], "merged_ready")
                    after_unit()
                    if branch == 2:
                        conv_taps(10)
                        if i:
                            u_input(2 + i)
                        conv_taps(8)
                    if branch == 0 and i == 0:
                        conv_taps(KB * CH)
                    if branch == 0 and i == 1:
                        b = take(dve, "ln_mean")
                        for c in range(CH):
                            ins = V.scalar_tensor_tensor(conv_b[:, c, :], b[:, :], -1.0 / D, conv_b[:, c, :], ALU.mult, ALU.add)
                        evac(ins, "ln_mean")
                    if branch == 0 and i == 2:
                        variance("ln_var", T, 1.0 / D, EPS2)
                        for c in range(CH):
                            V.scalar_tensor_tensor(tmp[0][:, 0:T], conv_b[:, c, :], pcol("ln_b_g_2", c), rs[:, :], ALU.mult, ALU.mult)\
                                .then_inc(sem("ln_scaled"), 1)
                            dve.wait_ge(sem("ln_sig"), c + 1)
                            link(V.scalar_tensor_tensor(conv_b[:, c, :], tmp[0][:, 0:T], pcol("ln_b_b_2", c), tmp[1][:, 0:T],
                                                        ALU.add, ALU.mult))

            def conv3(dst, pad, weights, first, stride):
                link(V.tensor_scalar(dst, pad[:, 0:T], pcol(weights, first), None, ALU.mult))
                link(V.scalar_tensor_tensor(dst, pad[:, 1:1 + T], pcol(weights, first + stride), dst, ALU.mult, ALU.add))
                return V.scalar_tensor_tensor(dst, pad[:, 2:2 + T], pcol(weights, first + 2 * stride), dst, ALU.mult, ALU.add)

            gate_steps(2)
            for i in range(4):
                for m in range(2):
                    evacuated(dve, ("y", 2, i, m))
            for i in range(4):
                conv_taps(10)
                filled(dve, ("gb", i, 1))
                after_unit()
                if i % 2:
                    u_input(6 + i // 2)
            link(V.memset(pad_a[:, 0:KA - 1], 0.0))
            for i in range(8):
                evacuated(dve, ("cv", i, 0))
                evac(V.tensor_tensor(pad_a[:, KA - 1:KA - 1 + T], take(dve, ("cv", i, 1))[:, :], tmp[0][:, 0:T], ALU.mult), ("cv", i, 1))
                after_unit()
                evacuated(dve, ("cv", i, 1))
                evacuated(dve, ("gb", i // 2, i % 2))
                link(conv3(tmp[1][:, 0:T], pad_a, "conv_a_w_2", i, 8))
                link(V.tensor_tensor(tmp[1][:, 0:T], tmp[1][:, 0:T], work[:, i, :], ALU.mult))
                parts(tmp[1][:, 0:T], op2_hi[:, i, :], op2_lo[:, i, :], "op2_ready0")
                conv_taps(6)
            gate_steps(0)
            for c in range(CH):
                parts(conv_b[:, c, :], op2_hi[:, c, :], op2_lo[:, c, :], "op2_ready1")
            gate_steps(1)
            for i in range(4):
                residual("wo2", i)
                after_unit()
            for i in range(4):
                for m in range(2):
                    evacuated(dve, ("wo2", i, m))
            variance("f", T, 1.0 / D, EPS2)
            normed(x_res, "norm_ffn_g_2", T, op_hi, op_lo, "ffn_ready")

            for i in range(FC):
                for m in range(2):
                    b, y = take(dve, ("up", i, m)), conv_f[i % 2][m]
                    dve.wait_ge(sem("tap_ready"), 2 * i + m + 1)
                    for back in (1, 2):
                        w = pcol("conv_ffn_w_2", 2 * FC * (2 - back) + FC * m + i)
                        ins = V.scalar_tensor_tensor(y[:, back:T], b[:, 0:T - back], w, y[:, back:T], ALU.mult, ALU.add)
                        if back == 1:
                            link(ins)
                    evac(ins, ("up", i, m))
                    if m == 1:
                        after_unit()
                g, y = sig_f[i % 2][:, 0:T], conv_f[i % 2]
                dve.wait_ge(sem("cg_sig"), i + 1)
                link(V.tensor_tensor(g, g, y[0][:, 0:T], ALU.mult))
                evacuated(dve, ("up", i, 1))
                link(V.tensor_tensor(g, g, y[1][:, 0:T], ALU.mult))
                lo = act_lo[:, i, :] if i < 16 else act_lo2[:, i - 16, :]
                parts(g, act_hi[:, i, :], lo, "act_ready")
            for i in range(4):
                for n in range(2):
                    slot_used(dve, u)
                    after_unit()
                residual("down", i)
                after_unit()
            for i in range(4):
                for m in range(2):
                    evacuated(dve, ("down", i, m))
            variance("fin", T, 1.0 / D, EPS2)
            for c in range(CH):
                V.scalar_tensor_tensor(x_res[:, c, :], x_res[:, c, :], pcol("norm_final_g_2", c), rs[:, :], ALU.mult, ALU.mult)\
                    .then_inc(sem("fin_ready"), 1)
            for g in range(2):
                for t in range(1, NT, 2):
                    evac(V.tensor_copy(out_tok[t][:, g * T:g * T + T], take(dve, ("out", t, g))[:, :]), ("out", t, g))



NAMES = ["x", "norm_g", "w_in", "mu_shift", "w0", "w_up", "a0", "a_up", "k_k", "k_a", "r_k", "gn_g", "gn_b", "q_norm_g",
         "kv_norm_g", "w_uq", "w_uk", "w_uv", "w_qidx", "kidx_g", "kidx_b", "w_out", "final_g", "mem_2", "norm_mix_g_2",
         "norm_mem_g_2", "w_in_2", "b_gate_2", "conv_a_w_2", "w_a_out_2", "conv_b_w_2", "conv_b_bias_2", "ln_b_g_2",
         "ln_b_b_2", "w_b_out_2", "w_kv_2", "w_att_out_2", "w_o_2", "norm_ffn_g_2", "w_up_2", "conv_ffn_w_2", "w_down_2",
         "norm_final_g_2"]


def kernel(**inputs):
    import concourse.bacc as bacc
    from concourse.bass_utils import run_bass_kernel_spmd

    nc = bacc.Bacc("TRN2", target_bir_lowering=False, num_devices=1)
    arrays, dram = {}, {}
    for name in NAMES:
        a = np.ascontiguousarray(inputs[name])
        arrays["in_" + name] = a
        dram[name] = nc.dram_tensor("in_" + name, a.shape, mybir.dt.from_np(a.dtype), kind="ExternalInput").ap()
    out = nc.dram_tensor("out", (1, T, D), F32, kind="ExternalOutput").ap()
    build(nc, dram, out)
    r = run_bass_kernel_spmd(nc, [arrays], core_ids=[0])
    return r.results[0]["out"]
```

```python
from contextlib import ExitStack

import numpy as np

import concourse.bass as bass
from concourse import mybir

F32 = mybir.dt.float32
F32R = mybir.dt.float32r
ALU = mybir.AluOpType
ACT = mybir.ActivationFunctionType
X_AXIS = mybir.AxisListType.X

P = 128
D = 1024
T = 512
CH = D // P
NT = T // P
HD = 64
NH = 8
NI = NH // 2
MEM = 256
MH = 4
FF = 2816
FC = FF // P
TOPK = 128
KAPPA = float(np.exp(-0.5))
NORM_EPS, LN_EPS, GN_EPS, EPS2 = 1e-6, 1e-5, 64e-5, 1e-6
MASKED = -1.0e30
TAKEN = -3.0e38
KB, KA, KF = 31, 3, 3
BANKS = 8

C_R, C_K, C_V, C_WA, C_G, C_QD, C_KV, C_KI, C_WI, C_GA = 0, 512, 1024, 1536, 1600, 2112, 2368, 2496, 2560, 2564
C2_GB, C2_GC, C2_VA, C2_U, C2_UG, C2_Q, C2_PG = 0, 1024, 2048, 3072, 4096, 5120, 6144


def weight_units():
    units = []

    def add(what, i, pieces, nk=CH, k0=0):
        units.append((what, i, nk, [(at, w, col, n, k0) for at, w, col, n in pieces]))

    add("qd", 0, [(0, "w_in", C_QD, 256)])
    add("kvi", 0, [(0, "w_in", C_KV, 128), (128, "w_in", C_KI, 64), (192, "w_in", C_KI, 64)])
    add("wa", 0, [(0, "w_in", C_WA, 64), (64, "w_in", C_WI, 4), (68, "w_in", C_G + 4, 188)])
    for half in range(2):
        for what, col in (("r", C_R), ("k", C_K), ("v", C_V), ("g", C_G)):
            add(what, half, [(0, "w_in", col + 256 * half, 256)])
    for half in range(2):
        add("ga", half, [(0, "w_in", C_GA + 256 * half, 256)])
    for i in range(4):
        add("vm", i, [(0, "w_kv_2", D + 256 * i, 256)])
    for i in range(4):
        add("wout", i, [(0, "w_out", 256 * i, 256)])
    for i in range(4):
        add("kT", i, [(0, "w_kv_2", 256 * i, 256)])

    def add_u(i):
        add("u", i, [(0, "w_in_2", C2_U + P * i, P), (P, "w_in_2", C2_UG + P * i, P)])

    def gated(branch, w):
        for i in range(4):
            add("pg", i, [(0, "w_in_2", C2_PG + D * branch + 256 * i, 256)])
            if branch == 2 and i == 0:
                add_u(2)
            add("y", i, [(0, w, 256 * i, 256)])
            if branch == 2 and i:
                add_u(2 + i)

    add_u(0)
    for i in range(4):
        add("q2", i, [(0, "w_in_2", C2_Q + 256 * i, 256)])
    add_u(1)
    gated(2, "w_att_out_2")
    for i in range(4):
        add("gb", i, [(0, "w_in_2", C2_GB + 256 * i, 256)])
        if i % 2:
            add_u(6 + i // 2)
    for i in range(8):
        add("cv", i, [(0, "w_in_2", C2_GC + P * i, P), (P, "w_in_2", C2_VA + P * i, P)])
    gated(0, "w_a_out_2")
    gated(1, "w_b_out_2")
    for i in range(4):
        add("wo2", i, [(0, "w_o_2", 256 * i, 256)])
    for i in range(FC):
        add("up", i, [(0, "w_up_2", P * i, P), (P, "w_up_2", FF + P * i, P)])
    for i in range(4):
        for k0, nk in ((0, 8), (8, 8), (16, 6)):
            add("down", (i, k0), [(0, "w_down_2", 256 * i, 256)], nk, k0)
    return units


PARAM_ROWS = [("norm_g", 8), ("mu_r", 4), ("mu_k", 4), ("mu_v", 4), ("mu_wa", 1), ("w0", 4), ("a0", 4), ("k_k", 4),
              ("k_a", 4), ("r_k", 4), ("gn_g", 4), ("gn_b", 4), ("q_norm_g", 2), ("kv_norm_g", 1), ("kidx_g", 1),
              ("kidx_b", 1), ("final_g", 8), ("norm_mix_g_2", 8), ("norm_mem_g_2", 8), ("b_gate_2", 24),
              ("conv_b_bias_2", 8), ("ln_b_g_2", 8), ("ln_b_b_2", 8), ("norm_ffn_g_2", 8), ("norm_final_g_2", 8),
              ("conv_a_w_2", 24), ("conv_b_w_2", 248), ("conv_ffn_w_2", 132)]
PARAM_AT = {}
_at = 0
for _name, _rows in PARAM_ROWS:
    PARAM_AT[_name] = _at
    _at += _rows
PARAM_TILES = -(-_at // P)
FIRST_POOL_UNIT = 9
MIX_ORDER = [*range(NI, CH), *range(NI)]


def build(nc, dram, out):
    units = weight_units()
    NU = len(units)
    ctx = ExitStack()
    with ctx:
        base = -(-nc.sbuf_base // 32) * 32

        def at(name, offset, shape, dt=F32):
            return nc.alloc_sbuf_tensor_at(name, [P] + shape, dt, offset=base + offset)

        sems = {}

        def sem(name):
            if name not in sems:
                sems[name] = ctx.enter_context(nc.semaphore(name))
            return sems[name]

        w_raw = [at(f"w_raw{s}", 8192 * s, [CH, 256]) for s in range(2)]
        w_hi = [at(f"w_hi{s}", 16384 + 8192 * s, [CH, 256], F32R) for s in range(2)]
        w_lo = [at(f"w_lo{s}", 32768 + 8192 * s, [CH, 256], F32R) for s in range(2)]
        x_res = at("x_res", 49152, [CH, T])
        op_hi = at("op_hi", 81920, [CH, T], F32R)
        op_lo = at("op_lo", 98304, [CH, T], F32R)
        ident = at("ident", 114688, [P])
        ones = at("ones", 115200, [P])
        par = at("par", 115712, [PARAM_TILES * P])
        misc = at("misc", 118272, [128])
        S0 = 118784
        tmp = [at(f"tmp{i}", 124928 + 2176 * i, [544]) for i in range(3)]
        rs = at("rs", 131456, [T])
        R0 = 133504
        pair_ones = at("pair_ones", S0, [P])
        mask_ar = at("mask_ar", S0 + 512, [2, P])
        mask_lev = at("mask_lev", S0 + 1536, [7, P])
        mask_lowT = at("mask_lowT", S0 + 5120, [P])
        mask_low = at("mask_low", S0 + 5632, [P])
        x_tok = at("x_tok", R0, [NT, D])
        x_scaled = at("x_scaled", R0 + 16384, [NT, D])
        par_rows = at("par_rows", R0 + 32768, [PARAM_TILES, P])
        gain_rows = at("gain_rows", R0 + 36864, [P])
        sq_row = at("sq_row", 67584, [D])
        ar = at("ar", R0, [NI, 2, T])
        bt = at("bt", R0 + 16384, [NI, T])
        kt = at("kt", R0 + 24576, [NI, T])
        vf = at("vf", R0 + 32768, [NI, T])
        gate_r = at("gate_r", R0 + 40960, [NI, T])
        gate_a = at("gate_a", R0 + 49152, [NI, T])
        tok = [[at(f"tok{j}_{s}", R0 + 57344 + 6144 * s + 2048 * j, [T]) for j in range(3)] for s in range(2)]
        lora = at("lora", R0 + 57344, [T])
        prep = [at(f"prep{j}", R0 + 59392 + 2080 * j, [4 * 129 + 4]) for j in range(4)]
        qd = at("qd", R0 + 69632, [2, T])
        ckv = at("ckv", R0 + 73728, [T])
        kidx = at("kidx", R0 + 75776, [T])
        bonus_v = at("bonus_v", 65536, [NI, T])
        y_scan = at("y_scan", 73728, [NI, T])
        g_b = at("g_b", 81920, [NH, 2, P])
        g_k = at("g_k", 90112, [NH, 2, P])
        low = at("low", 98304, [NH, P])
        inv = at("inv", 102400, [NH, P])
        invT = at("invT", 106496, [NH, P])
        wprod = at("wprod", 110592, [NH, P])
        state = at("state", R0 + 77824, [NI, HD])
        xs_t = [tmp[0][:, 0:256], tmp[0][:, 256:512]]
        us_t = [tmp[1][:, 0:256], tmp[1][:, 256:512]]
        wqi = at("wqi", 65536, [2, 256])
        qiT = at("qiT", 67584, [2, T])
        score = at("score", 73728, [NT, T])
        probT = at("probT", 0, [NT, T])
        wuq = at("wuq", 8192, [2, 512])
        wuk = at("wuk", 12288, [512])
        wuv = at("wuv", 14336, [512])
        wukT = at("wukT", 16384, [NI, P])
        qT = at("qT", 18432, [NI, T])
        q_abs = [at(f"q_abs{s}", 26624 + 2048 * s, [T]) for s in range(2)]
        ckv_tok = at("ckv_tok", 45056, [NT, P])
        prob = [[at(f"prob{s}_{q}", 30720 + 5120 * s + 256 * q * (q + 1), [P * (q + 1)]) for q in range(NT)] for s in range(2)]
        o_lat = [at(f"o_lat{s}", 40960 + 2048 * s, [T]) for s in range(2)]
        rs_gn = at("rs_gn", R0, [NI, T])
        sq_gn = at("sq_gn", R0 + 57344, [NI, T])
        op2_hi = at("op2_hi", R0, [CH, T], F32R)
        op2_lo = at("op2_lo", R0 + 16384, [CH, T], F32R)
        mem_tok = at("mem_tok", 16384, [2, D])
        memT = at("memT", 24576, [CH, MEM])
        sq_mem = at("sq_mem", 32768, [CH, MEM])
        memn = at("memn", R0 + 69632, [CH, MEM])
        memn_hi = at("memn_hi", R0 + 16384, [CH, MEM], F32R)
        memn_lo = at("memn_lo", R0 + 24576, [CH, MEM], F32R)
        sq_g = at("sq_g", R0 + 32768, [CH, T])
        conv_b = at("conv_b", R0 + 32768, [CH, T])
        work = at("work", R0 + 49152, [CH, T])
        sq2 = at("sq2", R0 + 49152, [CH, T])
        merged_hi = at("merged_hi", R0 + 32768, [CH, T], F32R)
        merged_lo = at("merged_lo", R0 + 49152, [CH, T], F32R)
        sq_f = at("sq_f", R0, [CH, T])
        pad_a = at("pad_a", R0 + 73728, [KA - 1 + T])
        rs_mix = tmp[2][:, 0:T]
        u_sig = tmp[2][:, 0:T]
        gates = [at(f"gate{m}", R0 + 65536 + 2048 * m, [T]) for m in range(2)]
        prob2T = at("prob2T", 73728, [2, T])
        prob2 = [at(f"prob2_{s}", 77824 + 1024 * s, [MEM]) for s in range(NT)]
        memK = at("memK", 65536, [CH, MEM])
        memV = at("memV", R0 + 69632, [2, D])
        merged = at("merged", 65536, [CH, T])
        pad_b = [at(f"pad_b{s}", S0 + 2304 * s, [KB - 1 + T]) for s in range(2)]
        conv_f = [[at("conv_f00", S0, [T]), at("conv_f01", S0 + 2048, [T])], [at("conv_f10", S0 + 4096, [T]), tmp[0]]]
        sig_f = [tmp[1], tmp[2]]
        act_hi = at("act_hi", R0, [FC, T], F32R)
        act_lo = at("act_lo", R0 + 45056, [16, T], F32R)
        act_lo2 = at("act_lo2", 65536, [FC - 16, T], F32R)
        sq3 = at("sq3", 81920, [CH, T])
        out_tok = [at(f"out_tok{s}", R0 + 4096 * s, [D]) for s in range(NT)]

        omm = misc[:, 0:13]
        omka = misc[:, 13:17]
        w_idx = misc[:, 17:33]
        top8 = misc[:, 33:41]
        negmax = misc[:, 41:49]
        sums = misc[:, 49:57]
        rsum = misc[:, 57:65]
        mid = misc[:, 81:85]
        gain = misc[:, 85:93]
        rs_x = misc[:, 93:97]
        dec = misc[:, 65:81]
        ps = [ctx.enter_context(nc.psum_tensor(f"bank{b}", [P, T], F32)) for b in range(BANKS)]

        def pcol(name, i=0):
            c = PARAM_AT[name] + i
            return par[:, c:c + 1]

        full = [sem(f"bank_full{b}") for b in range(BANKS)]
        free = [sem(f"bank_free{b}") for b in range(BANKS)]
        seq = {}

        def take(eng, key):
            n = seq[key]
            eng.wait_ge(full[n % BANKS], n // BANKS + 1)
            return ps[n % BANKS]

        def evac(ins, key):
            ins.then_inc(free[seq[key] % BANKS], 1)

        def evacuated(eng, key):
            n = seq[key]
            eng.wait_ge(free[n % BANKS], n // BANKS + 1)

        def filled(eng, key):
            n = seq[key]
            eng.wait_ge(full[n % BANKS], n // BANKS + 1)

        raw_count, tot = [], [0, 0]
        for u, (_, _, _, pieces) in enumerate(units):
            tot[u % 2] += 16 * len(pieces)
            raw_count.append(tot[u % 2])
        w_arrived = [sem("w_arrived0"), sem("w_arrived1")]
        hi_ready, lo_ready = sem("w_hi_ready"), sem("w_lo_ready")
        unit_last = {}
        first_phase2_unit = next(n for n, u in enumerate(units) if u[0] == "vm")

        par_src = []
        for name, n in PARAM_ROWS:
            if name.startswith("mu_"):
                j = ("mu_r", "mu_k", "mu_v", "mu_wa").index(name)
                src = dram["mu_shift"][0, 512 * j:512 * j + (512 if j < 3 else 64)]
                par_src.append((name, 0, src.rearrange("(n q) -> n q", n=n)))
            elif name in ("kidx_g", "kidx_b"):
                par_src += [(name, HD * d, dram[name]) for d in range(2)]
            elif name in ("final_g", "norm_final_g_2"):
                par_src.append((name, 0, dram[name].rearrange("(n q) -> n q", q=P)))
            elif name in ("conv_a_w_2", "conv_b_w_2", "conv_ffn_w_2"):
                par_src.append((name, 0, dram[name][0].rearrange("k (n q) -> (k n) q", q=P)))
            elif name in ("k_k", "k_a", "r_k", "gn_g", "gn_b"):
                par_src.append((name, 0, dram[name][0].rearrange("(n a) d -> n (a d)", a=2)))
            else:
                par_src.append((name, 0, dram[name][0].rearrange("(n q) -> n q", q=P)))
        par_dmas = []
        for name, col, src in par_src:
            row, n, a = PARAM_AT[name], src.shape[0], 0
            while a < n:
                tl, r = divmod(row + a, P)
                m = min(n - a, P - r)
                par_dmas.append((par_rows[r:r + m, tl, col:col + src.shape[1]], src[a:a + m, :]))
                a += m
        n_par_dmas = len(par_dmas)

        block = ctx.enter_context(nc.Block())

        @block.tensor
        def _(pe):
            count = [0]

            def bank(key):
                n = count[0]
                count[0] += 1
                assert key not in seq, key
                seq[key] = n
                if n >= BANKS:
                    pe.wait_ge(free[n % BANKS], n // BANKS)
                return ps[n % BANKS]

            def done(ins, key):
                ins.then_inc(full[seq[key] % BANKS], 1)

            def transposes(key, blocks, rows=P):
                b = bank(key)
                for j, src in enumerate(blocks):
                    mm = nc.tensor.transpose(b[:, j * P:j * P + rows], src, ident[0:rows, 0:rows])
                done(mm, key)

            def sum_chunks(key, sq, n, width, ready):
                b = bank(key)
                for c in range(n):
                    pe.wait_ge(sem(ready), c + 1)
                    mm = nc.tensor.matmul(b[:, 0:width], ones[:, :], sq[:, c, 0:width], start=c == 0, stop=c == n - 1)
                done(mm, key)

            unit = [0]

            def next_unit(what):
                u = unit[0]
                unit[0] += 1
                assert units[u][0] == what, (units[u], what)
                pe.wait_ge(hi_ready, u + 1)
                pe.wait_ge(lo_ready, u + 1)
                return u

            def sum_some(key, sq, first, last):
                b = bank(key) if first == 0 else ps[seq[key] % BANKS]
                if last < CH:
                    pe.wait_ge(sem("paired_" + key), last // 2)
                    nc.tensor.matmul(b[:, :], ones[:, :], sq[:, first, :], start=first == 0, stop=False)
                else:
                    for c in range(first, last):
                        pe.wait_ge(sem("sq_" + key), c + 1)
                        mm = nc.tensor.matmul(b[:, :], ones[:, :], sq[:, c, :], start=False, stop=c == CH - 1)
                    done(mm, key)

            def tile(b, u, col, width, xh, xl, x0=0, start=True, stop=True, ks=None):
                wh, wl, nk = w_hi[u % 2], w_lo[u % 2], units[u][2]
                ks = range(nk) if ks is None else ks
                for k in ks:
                    h, l = wh[:, k, col:col + P], wl[:, k, col:col + P]
                    nc.tensor.matmul(b[:, 0:width], h, xh[:, x0 + k, 0:width], start=start and k == ks[0], stop=False)
                    nc.tensor.matmul(b[:, 0:width], h, xl(x0 + k, width), start=False, stop=False)
                    mm = nc.tensor.matmul(b[:, 0:width], l, xh[:, x0 + k, 0:width], start=False,
                                          stop=stop and k == ks[-1])
                return mm

            def plain(t):
                return lambda k, width: t[:, k, 0:width]

            def unit_tiles(what, i, xh, xl, width=T, tiles=2, ready=None, branch=None, order=range(CH)):
                u = next_unit(what)
                keys = [(what, i, m) if branch is None else (what, branch, i, m) for m in range(tiles)]
                if ready is None:
                    for m in range(tiles):
                        b = bank(keys[m])
                        done(tile(b, u, m * P, width, xh, xl), keys[m])
                else:
                    bs = [bank(key) for key in keys]
                    for n, k in enumerate(order):
                        if callable(ready):
                            ready(k)
                        else:
                            pe.wait_ge(sem(ready), n + 1)
                        for m in range(tiles):
                            mm = tile(bs[m], u, m * P, width, xh, xl, start=n == 0, stop=n == CH - 1, ks=[k])
                            if n == CH - 1:
                                done(mm, keys[m])
                unit_last[u] = keys[-1]

            pe.wait_ge(sem("consts"), 2)
            pe.wait_ge(sem("gain_loaded"), 16)
            b = bank("gain")
            done(nc.tensor.transpose(b[:, 0:CH], gain_rows[0:CH, :], ident[0:CH, 0:CH]), "gain")
            for t in range(2):
                pe.wait_ge(sem(f"x_scaled{t}"), NT // 2)
            for c in range(CH):
                transposes(("xnT", c), [x_scaled[:, t, c * P:c * P + P] for t in range(NT)])

            oh, ol = op_hi, plain(op_lo)
            unit_tiles("qd", 0, oh, ol, ready=lambda k: evacuated(pe, ("xnT", k)))
            unit_tiles("kvi", 0, oh, ol)
            pe.wait_ge(sem("par_loaded"), 16 * n_par_dmas)
            transposes(("par", 0), [par_rows[:, j, :] for j in range(4)])
            transposes(("par", 1), [par_rows[:, j, :] for j in range(4, PARAM_TILES)])
            for c in range(CH):
                transposes(("xT", c), [x_tok[:, t, c * P:c * P + P] for t in range(NT)])
            unit_tiles("wa", 0, oh, ol, tiles=1)
            pe.wait_ge(sem("sq_q"), 2)
            b = bank("ss_q")
            for m in range(2):
                mm = nc.tensor.matmul(b[:, :], ones[:, :], prep[m][:, 0:T], start=m == 0, stop=m == 1)
            done(mm, "ss_q")
            pe.wait_ge(sem("sq_kv"), 1)
            pe.wait_ge(sem("consts"), 7)
            b = bank("ss_kv")
            done(nc.tensor.matmul(b[:, :], ones[:, :], prep[2][:, 0:T], start=True, stop=True), "ss_kv")
            evacuated(pe, ("kvi", 0, 1))
            b = bank("ki_mean")
            done(nc.tensor.matmul(b[:, :], pair_ones[:, :], kidx[:, :], start=True, stop=True), "ki_mean")
            unit_tiles("r", 0, oh, ol)
            unit_tiles("k", 0, oh, ol)
            pe.wait_ge(sem("ki_sq"), 1)
            b = bank("ki_var")
            done(nc.tensor.matmul(b[:, :], pair_ones[:, :], prep[3][:, 0:T], start=True, stop=True), "ki_var")
            pe.wait_ge(sem("tanh_ready"), 1)
            evacuated(pe, ("wa", 0, 0))
            transposes("w_idx", [tmp[2][:, t * P:t * P + P] for t in range(NT)])
            pe.wait_ge(sem("wqi_loaded"), 16)
            pe.wait_ge(sem("cq_ready"), 2)
            for i in range(2):
                b = bank(("qi", i))
                for m in range(2):
                    mm = nc.tensor.matmul(b[:, :], wqi[:, m, i * P:i * P + P], qd[:, m, :], start=m == 0, stop=m == 1)
                done(mm, ("qi", i))

            def index_logits(qt):
                for h in range(4):
                    rows = slice(HD * (h % 2), HD * (h % 2) + HD)
                    b = bank(("lg", qt, h))
                    done(nc.tensor.matmul(b[:, 0:P * (qt + 1)], qiT[rows, h // 2, qt * P:qt * P + P], kidx[rows, 0:P * (qt + 1)],
                                          start=True, stop=True), ("lg", qt, h))

            unit_tiles("v", 0, oh, ol)
            pe.wait_ge(sem("kidx_ready"), 1)
            for i in range(2):
                evacuated(pe, ("qi", i))
            index_logits(1)
            unit_tiles("g", 0, oh, ol)
            index_logits(2)
            unit_tiles("r", 1, oh, ol)
            index_logits(3)
            for what in "kvg":
                unit_tiles(what, 1, oh, ol)
            for half in range(2):
                unit_tiles("ga", half, oh, ol)

            def absorbed_query(h):
                rows = slice(HD * (h % 2), HD * (h % 2) + HD)
                b = bank(("qa", h))
                done(nc.tensor.matmul(b[:, :], wukT[rows, h // 2, :], qT[rows, h // 2, :], start=True, stop=True), ("qa", h))

            def scores(h):
                evacuated(pe, ("qa", h))
                for qt in range(NT):
                    b = bank(("s", h, qt))
                    done(nc.tensor.matmul(b[:, 0:P * (qt + 1)], q_abs[h % 2][:, qt * P:qt * P + P], ckv[:, 0:P * (qt + 1)],
                                          start=True, stop=True), ("s", h, qt))

            def head_out(h):
                rows = slice(HD * (h % 2), HD * (h % 2) + HD)
                evacuated(pe, ("ol", h))
                b = bank(("o", h))
                done(nc.tensor.matmul(b[rows, :], wuv[:, h * HD:h * HD + HD], o_lat[h % 2][:, :], start=True, stop=True), ("o", h))

            def attention_start():
                pe.wait_ge(sem("dsa_w"), 16 * 3)
                transposes("wukT", [wuk[:, i * P:i * P + P] for i in range(NI)])
                for i in range(NI):
                    b = bank(("q", i))
                    for m in range(2):
                        mm = nc.tensor.matmul(b[:, :], wuq[:, m, i * P:i * P + P], qd[:, m, :], start=m == 0, stop=m == 1)
                    done(mm, ("q", i))
                pe.wait_ge(sem("ckv_ready"), 1)
                transposes("ckv_tok", [ckv[:, t * P:t * P + P] for t in range(NT)])
                for i in range(NI):
                    evacuated(pe, ("q", i))
                evacuated(pe, "wukT")
                absorbed_query(0)
                absorbed_query(1)
                scores(0)

            def attention_step(h):
                if h + 1 < NH:
                    scores(h + 1)
                if h + 2 < NH:
                    absorbed_query(h + 2)
                for qt in range(NT):
                    pe.wait_ge(sem("prob_ready"), NT * h + qt + 1)
                    transposes(("pT", h, qt), [prob[h % 2][qt][:, k * P:k * P + P] for k in range(qt + 1)])
                if h:
                    head_out(h - 1)
                else:
                    evacuated(pe, "ckv_tok")
                for qt in range(NT):
                    evacuated(pe, ("pT", h, qt))
                b = bank(("ol", h))
                for k in range(NT):
                    mm = nc.tensor.matmul(b[:, k * P:T], ckv_tok[:, k, :], probT[:, k, k * P:T], start=k == 0, stop=k == NT - 1)
                done(mm, ("ol", h))

            pe.wait_ge(sem("lora_loaded"), 32)
            for i in range(NI):
                b = bank(("z", i))
                done(nc.tensor.matmul(b[:, :], lora[0:32, i * P:i * P + P], tmp[2][0:32, 0:T], start=True, stop=True), ("z", i))
                b = bank(("a", i))
                done(nc.tensor.matmul(b[:, :], lora[32:64, i * P:i * P + P], tmp[2][32:64, 0:T], start=True, stop=True), ("a", i))
                b = bank(("kk", i))
                pe.wait_ge(sem("kk_sq"), i + 1)
                done(nc.tensor.matmul(b[:, :], pair_ones[:, :], prep[3][:, 0:T], start=True, stop=True), ("kk", i))
                if i == 0:
                    attention_start()
                attention_step(2 * i)
                b = bank(("bonus", i))
                pe.wait_ge(sem("rk_ready"), i + 1)
                done(nc.tensor.matmul(b[:, :], pair_ones[:, :], prep[3][:, 0:T], start=True, stop=True), ("bonus", i))
                attention_step(2 * i + 1)
            head_out(NH - 1)
            pe.wait_ge(sem("prep_ready"), NI)
            pe.wait_ge(sem("bk_decayed"), 2 * NI)
            for c in range(NT):
                cs = slice(c * P, c * P + P)
                for j, src in enumerate((vf, bt, kt)):
                    transposes(("tok", c, j), [src[:, i, cs] for i in range(NI)])
                for odd in range(2):
                    rows = slice(HD * odd, HD * odd + HD)
                    for name, stat in (("gb", bt), ("gk", kt)):
                        for i2 in range(2):
                            b = bank((name, c, odd, i2))
                            for n in range(2):
                                i = 2 * i2 + n
                                mm = nc.tensor.matmul(b[:, n * 256:n * 256 + 256], stat[rows, i, cs], ar[rows, i, :, cs],
                                                      start=True, stop=True)
                            done(mm, (name, c, odd, i2))
                    b = bank(("low", c, odd))
                    for i in range(NI):
                        mm = nc.tensor.matmul(b[:, i * P:i * P + P], ar[rows, i, 0, cs], bt[rows, i, cs], start=True, stop=True)
                    done(mm, ("low", c, odd))
                if c == 0:
                    pe.wait_ge(sem("mem_loaded"), 16)
                    for k in range(CH):
                        transposes(("memT", k), [mem_tok[:, t, k * P:k * P + P] for t in range(2)])
                for lev in range(1, 7):
                    for odd in range(2):
                        hs = slice(NI * odd, NI * odd + NI)
                        if lev == 1:
                            pe.wait_ge(sem(f"inv_init{odd}"), c + 1)
                        else:
                            evacuated(pe, ("dinv", c, lev - 1, odd))
                            evacuated(pe, ("dinvT", c, lev - 1, odd))
                        b = bank(("w", c, lev, odd))
                        for i in range(NI):
                            h = NI * odd + i
                            mm = nc.tensor.matmul(b[:, i * P:i * P + P], low[:, h, :], inv[:, h, :], start=True, stop=True)
                        done(mm, ("w", c, lev, odd))
                    if c == 0 and lev == 2:
                        sum_chunks("ss_mem", sq_mem, CH, MEM, "sq_mem")
                    for odd in range(2):
                        evacuated(pe, ("w", c, lev, odd))
                        b = bank(("dinv", c, lev, odd))
                        for i in range(NI):
                            h = NI * odd + i
                            mm = nc.tensor.matmul(b[:, i * P:i * P + P], invT[:, h, :], wprod[:, h, :], start=True, stop=True)
                        done(mm, ("dinv", c, lev, odd))
                        if lev < 6:
                            b = bank(("dinvT", c, lev, odd))
                            for i in range(NI):
                                h = NI * odd + i
                                mm = nc.tensor.matmul(b[:, i * P:i * P + P], wprod[:, h, :], invT[:, h, :], start=True, stop=True)
                            done(mm, ("dinvT", c, lev, odd))
                V, B, K = tok[c % 2]
                for j in range(3):
                    evacuated(pe, ("tok", c, j))
                for odd in range(2):
                    for i2 in range(2):
                        evacuated(pe, ("gb", c, odd, i2))
                        evacuated(pe, ("gk", c, odd, i2))
                for odd in range(2):
                    rows = slice(HD * odd, HD * odd + HD)
                    if c > 0:
                        evacuated(pe, ("p", c - 1, odd))
                    b = bank(("scan_x", c, odd))
                    for i in range(NI):
                        h, f = NI * odd + i, P * i + HD * odd
                        if c > 0:
                            nc.tensor.matmul(b[:, i * HD:i * HD + HD], ar[rows, i, 0, cs], state[rows, i, :], start=True, stop=False)
                        mm = nc.tensor.matmul(b[:, i * HD:i * HD + HD], g_k[:, h, 0, :], V[:, f:f + HD], start=c == 0, stop=True)
                    done(mm, ("scan_x", c, odd))
                for odd in range(2):
                    evacuated(pe, ("dinv", c, 6, odd))
                    evacuated(pe, ("scan_x", c, odd))
                    b = bank(("scan_u", c, odd))
                    for i in range(NI):
                        h = NI * odd + i
                        mm = nc.tensor.matmul(b[:, i * HD:i * HD + HD], inv[:, h, :], xs_t[odd][:, i * HD:i * HD + HD], start=True, stop=True)
                    done(mm, ("scan_u", c, odd))
                for odd in range(2):
                    rows = slice(HD * odd, HD * odd + HD)
                    evacuated(pe, ("scan_u", c, odd))
                    b = bank(("yT", c, odd))
                    for i in range(NI):
                        h, f = NI * odd + i, P * i + HD * odd
                        o = b[rows, i * P:i * P + P]
                        if c > 0:
                            nc.tensor.matmul(o, state[rows, i, :], ar[rows, i, 1, cs], start=True, stop=False)
                        nc.tensor.matmul(o, us_t[odd][:, i * HD:i * HD + HD], g_b[:, h, 1, :], start=c == 0, stop=False)
                        mm = nc.tensor.matmul(o, V[:, f:f + HD], g_k[:, h, 1, :], start=False, stop=True)
                    done(mm, ("yT", c, odd))
                    if c < NT - 1:
                        b = bank(("p", c, odd))
                        for i in range(NI):
                            h, f = NI * odd + i, P * i + HD * odd
                            o = b[rows, i * HD:i * HD + HD]
                            if c > 0:
                                nc.tensor.matmul(o, ident[rows, rows], state[rows, i, :], start=True, stop=False)
                            nc.tensor.matmul(o, B[:, f:f + HD], us_t[odd][:, i * HD:i * HD + HD], start=c == 0, stop=False)
                            mm = nc.tensor.matmul(o, K[:, f:f + HD], V[:, f:f + HD], start=False, stop=True)
                        done(mm, ("p", c, odd))
            for odd in range(2):
                evacuated(pe, ("yT", NT - 1, odd))
            for i in range(NI):
                b = bank(("gn_mean", i))
                done(nc.tensor.matmul(b[:, :], pair_ones[:, :], y_scan[:, i, :], start=True, stop=True), ("gn_mean", i))
            for i in range(NI):
                pe.wait_ge(sem("gn_sq"), i + 1)
                b = bank(("gn_var", i))
                done(nc.tensor.matmul(b[:, :], pair_ones[:, :], sq_gn[:, i, :], start=True, stop=True), ("gn_var", i))

            pe.wait_ge(sem("memn_ready"), 1)
            for i in range(4):
                u = next_unit("vm")
                b = bank(("vm", i))
                for t in range(2):
                    o = b[:, t * 256:t * 256 + 256]
                    for k in range(CH):
                        h, l = memn_hi[:, k, t * P:t * P + P], memn_lo[:, k, t * P:t * P + P]
                        nc.tensor.matmul(o, h, w_hi[u % 2][:, k, :], start=k == 0, stop=False)
                        nc.tensor.matmul(o, h, w_lo[u % 2][:, k, :], start=False, stop=False)
                        mm = nc.tensor.matmul(o, l, w_hi[u % 2][:, k, :], start=False, stop=k == CH - 1)
                done(mm, ("vm", i))
                unit_last[u] = ("vm", i)
            for i in range(4):
                unit_tiles("wout", i, oh, ol, ready=None if i else "mix_ready", order=MIX_ORDER)
                if i:
                    sum_some("y", sq2, 2 * i - 2, 2 * i)
                    sum_some("yg", sq_g, 2 * i - 2, 2 * i)
            sum_some("y", sq2, CH - 2, CH)
            sum_some("yg", sq_g, CH - 2, CH)
            for i in range(4):
                unit_tiles("kT", i, memn_hi, plain(memn_lo), MEM)
            unit_tiles("u", 0, oh, ol, ready="mixn_ready")
            mh, ml = op2_hi, plain(op2_lo)

            def mem_scores(h):
                for m in range(2):
                    evacuated(pe, ("q2", h, m))
                    evacuated(pe, ("kT", h, m))
                for qt in range(NT):
                    b = bank(("s2", h, qt))
                    for k in range(2):
                        mm = nc.tensor.matmul(b[:, 0:MEM], work[:, 2 * h + k, qt * P:qt * P + P], memK[:, 2 * h + k, :],
                                              start=k == 0, stop=k == 1)
                    done(mm, ("s2", h, qt))

            def mem_probs(h):
                for qt in range(NT):
                    pe.wait_ge(sem("prob2_ready"), NT * h + qt + 1)
                    transposes(("p2T", h, qt), [prob2[qt][:, k * P:k * P + P] for k in range(2)])

            def mem_out(h):
                evacuated(pe, ("vm", h))
                for qt in range(NT):
                    evacuated(pe, ("p2T", h, qt))
                for d in range(2):
                    b = bank(("oc", h, d))
                    for k in range(2):
                        mm = nc.tensor.matmul(b[:, :], memV[:, k, 256 * h + P * d:256 * h + P * d + P], prob2T[:, k, :],
                                              start=k == 0, stop=k == 1)
                    done(mm, ("oc", h, d))

            unit_tiles("q2", 0, oh, ol)
            unit_tiles("q2", 1, oh, ol)
            mem_scores(0)
            unit_tiles("q2", 2, oh, ol)
            mem_probs(0)
            mem_scores(1)
            unit_tiles("q2", 3, oh, ol)
            mem_out(0)
            mem_probs(1)
            mem_scores(2)
            unit_tiles("u", 1, oh, ol)
            mem_out(1)
            mem_probs(2)
            mem_scores(3)
            unit_tiles("pg", 0, oh, ol, branch=2)
            mem_out(2)
            mem_probs(3)
            unit_tiles("u", 2, oh, ol)
            mem_out(3)

            def gated(branch):
                operand = f"op2_ready{branch}" if branch < 2 else lambda k: evacuated(pe, ("oc", k // 2, k % 2))
                for i in range(4):
                    if branch < 2 or i:
                        unit_tiles("pg", i, oh, ol, branch=branch)
                    unit_tiles("y", i, mh, ml, branch=branch, ready=None if i else operand)
                    if branch == 2 and i:
                        unit_tiles("u", 2 + i, oh, ol)
                    if branch == 0 and i == 1:
                        sum_chunks("ln_mean", conv_b, CH, T, "conv_ready")
                    if branch == 0 and i == 2:
                        b = bank("ln_var")
                        for c in range(0, CH, 2):
                            pe.wait_ge(sem("paired_ln"), c // 2 + 1)
                            mm = nc.tensor.matmul(b[:, :], ones[:, :], sq2[:, c, :], start=c == 0, stop=c == CH - 2)
                        done(mm, "ln_var")

            gated(2)
            for i in range(4):
                unit_tiles("gb", i, oh, ol)
                if i % 2:
                    unit_tiles("u", 6 + i // 2, oh, ol)
            for i in range(8):
                unit_tiles("cv", i, oh, ol)
            gated(0)
            gated(1)
            for i in range(4):
                unit_tiles("wo2", i, merged_hi, plain(merged_lo), ready=None if i else "merged_ready")
                if i:
                    sum_some("f", sq_f, 2 * i - 2, 2 * i)
            sum_some("f", sq_f, CH - 2, CH)
            for i in range(FC):
                unit_tiles("up", i, oh, ol, ready=None if i else "ffn_ready")
            for i in range(4):
                bs = None
                for k0 in (0, 8, 16):
                    u = next_unit("down")
                    if bs is None:
                        bs = [bank(("down", i, m)) for m in range(2)]
                    if i == 0:
                        pe.wait_ge(sem("act_ready"), k0 + units[u][2])
                    for m in range(2):
                        mm = tile(bs[m], u, m * P, T, act_hi,
                                  lambda k, w: act_lo[:, k, 0:w] if k < 16 else act_lo2[:, k - 16, 0:w],
                                  x0=k0, start=k0 == 0, stop=k0 == 16)
                        if k0 == 16:
                            done(mm, ("down", i, m))
                    if k0 < 16:
                        mm.then_inc(sem("down_used"), 1)
                        unit_last[u] = ("down_used", 2 * i + k0 // 8 + 1)
                    else:
                        unit_last[u] = ("down", i, 1)
                if i:
                    sum_some("fin", sq3, 2 * i - 2, 2 * i)
            sum_some("fin", sq3, CH - 2, CH)
            for g in range(2):
                pe.wait_ge(sem("fin_ready"), 4 * g + 4)
                for t in range(NT):
                    transposes(("out", t, g), [x_res[:, 4 * g + j, t * P:t * P + P] for j in range(4)])
            assert unit[0] == NU

        def slot_used(eng, u):
            key = unit_last[u]
            if key[0] == "down_used":
                eng.wait_ge(sem("down_used"), key[1])
            else:
                filled(eng, key)

        @block.sync
        def _(sp):
            x_d = dram["x"][0].rearrange("(t p) d -> p t d", p=P)
            for t in range(NT):
                sp.dma_start(x_tok[:, t, :], x_d[:, t, :]).then_inc(sem(f"x_loaded{t}"), 16)
                if t == 0:
                    sp.dma_start(gain_rows[0:CH, :], dram["norm_g"][0].rearrange("(n q) -> n q", q=P)).then_inc(sem("gain_loaded"), 16)

            def load(u):
                _, _, nk, pieces = units[u]
                if u >= 2:
                    sp.wait_ge(hi_ready, u - 1)
                    sp.wait_ge(lo_ready, u - 1)
                for at_, w, col, n, k0 in pieces:
                    src = dram[w][0, k0 * P:(k0 + nk) * P, col:col + n].rearrange("(k p) n -> p k n", p=P)
                    sp.dma_start(w_raw[u % 2][:, 0:nk, at_:at_ + n], src).then_inc(w_arrived[u % 2], 16)

            for u in range(first_phase2_unit):
                load(u)
                if u == 1:
                    sp.wait_ge(sem("pool_steps"), 1)
                    for dst, src in par_dmas:
                        sp.dma_start(dst, src).then_inc(sem("par_loaded"), 16)
                    sp.dma_start(wqi[:, :, :], dram["w_qidx"][0].rearrange("(m p) n -> p m n", p=P)).then_inc(sem("wqi_loaded"), 16)
            sp.wait_ge(hi_ready, first_phase2_unit - 1)
            sp.wait_ge(lo_ready, first_phase2_unit - 1)
            dw = sem("dsa_w")
            sp.dma_start(wuk[:, :].rearrange("p (h d) -> p h d", d=HD), dram["w_uk"][0].rearrange("h r d -> r h d")).then_inc(dw, 16)
            sp.dma_start(wuq[:, :, :], dram["w_uq"][0].rearrange("(m p) n -> p m n", p=P)).then_inc(dw, 16)
            sp.dma_start(wuv[:, :].rearrange("p (h d) -> p h d", d=HD), dram["w_uv"][0].rearrange("h r d -> r h d")).then_inc(dw, 16)
            evacuated(sp, ("o", NH - 1))
            sp.dma_start(mem_tok[:, :, :], dram["mem_2"][0].rearrange("(t p) d -> p t d", p=P)).then_inc(sem("mem_loaded"), 16)
            for u in range(first_phase2_unit, NU):
                load(u)
            for g in range(2):
                for t in range(NT):
                    evacuated(sp, ("out", t, g))
                    sp.dma_start(out[0, t * P:t * P + P, g * T:g * T + T], out_tok[t][:, g * T:g * T + T]).then_inc(sem("stored"), 16)
            sp.wait_ge(sem("stored"), 16 * 2 * NT)

        @block.gpsimd
        def _(pool):
            steps = [0]

            def step(ins):
                steps[0] += 1
                ins.then_inc(sem("pool_steps"), 1)
                pool.wait_ge(sem("pool_steps"), steps[0])

            step(nc.gpsimd.memset(par_rows[:, :, :], 0.0))
            nc.gpsimd.memset(ones[:, :], 1.0).then_inc(sem("consts"), 1)
            pool.wait_ge(sem("consts"), 1)
            nc.gpsimd.affine_select(out=ident[:, :], in_=ones[:, :], compare_op=ALU.is_equal, fill=0.0, base=0,
                                    pattern=[[-1, P]], channel_multiplier=1).then_inc(sem("consts"), 1)
            pool.wait_ge(sem("consts"), 2)
            step(nc.gpsimd.memset(pair_ones[:, :], 0.0))
            step(nc.gpsimd.memset(pair_ones[0:HD, 0:HD], 1.0))
            nc.gpsimd.memset(pair_ones[HD:P, HD:P], 1.0).then_inc(sem("consts"), 1)
            pool.wait_ge(sem("consts"), 3)
            nc.gpsimd.affine_select(out=mask_ar[:, 0, :], in_=ones[:, :], compare_op=ALU.is_gt, fill=0.0, base=0,
                                    pattern=[[1, P]], channel_multiplier=-1).then_inc(sem("consts"), 1)
            pool.wait_ge(sem("consts"), 4)
            nc.gpsimd.affine_select(out=mask_ar[:, 1, :], in_=ones[:, :], compare_op=ALU.is_ge, fill=0.0, base=0,
                                    pattern=[[1, P]], channel_multiplier=-1).then_inc(sem("consts"), 1)
            pool.wait_ge(sem("consts"), 5)
            nc.gpsimd.affine_select(out=mask_low[:, :], in_=ones[:, :], compare_op=ALU.is_gt, fill=0.0, base=0,
                                    pattern=[[-1, P]], channel_multiplier=1).then_inc(sem("consts"), 1)
            pool.wait_ge(sem("consts"), 6)
            step(nc.gpsimd.memset(mask_lev[:, :, :], 0.0))
            for n in range(7):
                b = 1 << n
                v = mask_lev[:, n, :].rearrange("p (k h c) -> p k h c", h=2, c=b)[:, :, 1, :]
                step(nc.gpsimd.memset(v, 1.0))
                step(nc.gpsimd.affine_select(out=v, in_=v, compare_op=ALU.is_ge, fill=0.0, base=0,
                                             pattern=[[-2 * b, P // (2 * b)], [0, b]], channel_multiplier=1))
                step(nc.gpsimd.affine_select(out=v, in_=v, compare_op=ALU.is_ge, fill=0.0, base=b - 1,
                                             pattern=[[2 * b, P // (2 * b)], [0, b]], channel_multiplier=-1))
            step(nc.gpsimd.memset(mask_lowT[:, :], 0.0))
            v = mask_lowT[:, :].rearrange("p (k h) -> p k h", h=2)[:, :, 0]
            step(nc.gpsimd.memset(v, 1.0))
            nc.gpsimd.affine_select(out=v, in_=v, compare_op=ALU.is_equal, fill=0.0, base=-1,
                                    pattern=[[-2, P // 2]], channel_multiplier=1).then_inc(sem("consts"), 1)
            pool.wait_ge(sem("consts"), 7)
            v = score[:, 0, 0:P]
            step(nc.gpsimd.memset(v, 0.0))
            nc.gpsimd.affine_select(out=v, in_=v, compare_op=ALU.is_ge, fill=MASKED, base=0,
                                    pattern=[[-1, P]], channel_multiplier=1).then_inc(sem("causal"), 1)
            pool.wait_ge(sem("causal"), 1)
            for qt in range(1, NT):
                v = score[:, qt, qt * P:qt * P + P]
                pool.wait_ge(sem("score_ready"), qt)
                nc.gpsimd.affine_select(out=v, in_=v, compare_op=ALU.is_ge, fill=MASKED, base=0,
                                        pattern=[[-1, P]], channel_multiplier=1).then_inc(sem("causal"), 1)

            def split_lo(u):
                nk = units[u][2]
                pool.wait_ge(hi_ready, u + 1)
                slot_used(pool, u - 2)
                pool.wait_ge(lo_ready, u)
                nc.gpsimd.tensor_tensor(w_lo[u % 2][:, 0:nk, :], w_raw[u % 2][:, 0:nk, :],
                                        w_hi[u % 2][:, 0:nk, :].bitcast(F32), ALU.subtract).then_inc(lo_ready, 1)

            for u in range(FIRST_POOL_UNIT, first_phase2_unit):
                split_lo(u)
            for i in range(NI):
                e_up = tmp[1][:, 0:516].rearrange("p (c t) -> p c t", c=NT)[:, :, 1:P + 1]
                pool.wait_ge(sem("exps"), 2 * i + 2)
                pool.wait_ge(sem("b_ready"), i + 1)
                nc.gpsimd.tensor_tensor(bt[:, i, :].rearrange("p (c t) -> p c t", c=NT),
                                        prep[1][:, 0:T].rearrange("p (c t) -> p c t", c=NT), e_up, ALU.mult)\
                    .then_inc(sem("bk_decayed"), 1)
                k = kt[:, i, :].rearrange("p (c t) -> p c t", c=NT)
                filled(pool, ("bonus", i))
                nc.gpsimd.tensor_tensor(k, k, e_up, ALU.mult).then_inc(sem("bk_decayed"), 1)
            pool.wait_ge(sem("memn_scaled"), 1)
            for u in range(first_phase2_unit, NU):
                split_lo(u)

        @block.scalar
        def _(act):
            A = nc.scalar.activation
            split = [0]

            def split_hi(upto):
                while split[0] <= min(upto, NU - 1):
                    u = split[0]
                    split[0] += 1
                    nk = units[u][2]
                    act.wait_ge(w_arrived[u % 2], raw_count[u])
                    if u >= 2:
                        slot_used(act, u - 2)
                    A(w_hi[u % 2][:, 0:nk, :], w_raw[u % 2][:, 0:nk, :], ACT.Copy).then_inc(hi_ready, 1)

            roots = [0]

            def root(t=rs[:, :]):
                roots[0] += 1
                act.wait_ge(sem("var_ready"), roots[0])
                A(t, t, ACT.Sqrt).then_inc(sem("rs_ready"), 1)

            for t in range(NT):
                act.wait_ge(sem(f"x_loaded{t}"), 16)
                A(sq_row[:, :], x_tok[:, t, :], ACT.Square, accum_out=rs_x[:, t:t + 1]).then_inc(sem("sq_x"), 1)
                act.wait_ge(sem("sq_x"), t + 1)
            root(rs_x)
            act.wait_ge(sem("rs_ready"), 1)
            for t in range(1, NT, 2):
                A(x_scaled[:, t, :], x_tok[:, t, :], ACT.Copy, scale=rs_x[:, t:t + 1]).then_inc(sem("x_scaled1"), 1)
            split_hi(0)
            evacuated(act, "gain")
            for c in range(CH):
                A(op_hi[:, c, :], take(act, ("xnT", c))[:, :], ACT.Copy, scale=gain[:, c:c + 1]).then_inc(sem("xn_hi"), 1)
            split_hi(1)
            act.dma_start(lora[0:32, :], dram["w_up"][0]).then_inc(sem("lora_loaded"), 16)
            act.dma_start(lora[32:64, :], dram["a_up"][0]).then_inc(sem("lora_loaded"), 16)

            for m in range(2):
                b = take(act, ("qd", 0, m))
                A(prep[m][:, 0:T], b[:, :], ACT.Square).then_inc(sem("sq_q"), 1)
                evac(A(qd[:, m, :], b[:, :], ACT.Copy), ("qd", 0, m))
            split_hi(2)
            b = take(act, ("kvi", 0, 0))
            A(prep[2][:, 0:T], b[:, :], ACT.Square).then_inc(sem("sq_kv"), 1)
            evac(A(ckv[:, :], b[:, :], ACT.Copy), ("kvi", 0, 0))
            evac(A(kidx[:, :], take(act, ("kvi", 0, 1))[:, :], ACT.Copy), ("kvi", 0, 1))
            split_hi(3)
            for c in range(CH):
                evac(A(x_res[:, c, :], take(act, ("xT", c))[:, :], ACT.Copy), ("xT", c))
            act.wait_ge(sem("derived"), 1)

            def unshifted(key, dst, col):
                A(dst, take(act, key)[:, :], ACT.Copy, scale=omm[:, col:col + 1]).then_inc(sem("unshifted"), 1)

            unshifted(("wa", 0, 0), tmp[2][:, 0:T], 12)
            split_hi(4)
            evacuated(act, ("wa", 0, 0))
            A(tmp[2][0:32, 0:T], tmp[2][0:32, 0:T], ACT.Tanh).then_inc(sem("tanh_ready"), 1)
            root()
            root()
            evacuated(act, "ki_mean")
            A(prep[3][:, 0:T], kidx[:, :], ACT.Square).then_inc(sem("ki_sq"), 1)

            logits = [0]

            def relus(qt):
                for h in range(4):
                    n = logits[0]
                    logits[0] += 1
                    if n >= 4:
                        act.wait_ge(sem("relu_used"), n - 3)
                    w = P * (qt + 1)
                    evac(A(prep[n % 4][:, 0:w], take(act, ("lg", qt, h))[:, 0:w], ACT.Relu), ("lg", qt, h))

            u = 3
            for half in range(2):
                for w, dst in enumerate((lambda i: ar[:, i, 1, :], lambda i: kt[:, i, :], lambda i: vf[:, i, :])):
                    for m in range(2):
                        i = 2 * half + m
                        unshifted(("rkv"[w], half, m), dst(i), 4 * w + i)
                    u += 1
                    split_hi(u + 1)
                    if half == 0 and w == 1:
                        root()
                        for i in range(2):
                            evac(A(qiT[:, i, :], take(act, ("qi", i))[:, :], ACT.Copy), ("qi", i))
                    elif half == 0 and w == 2:
                        relus(1)
                    elif half == 1 and w == 0:
                        relus(3)
                for m in range(2):
                    b = take(act, ("g", half, m))
                    if half:
                        evacuated(act, ("g", 0, m))
                    A(tmp[m][:, 0:T], b[:, :], ACT.Sigmoid).then_inc(sem("sig_g"), 1)
                u += 1
                split_hi(u + 1)
                if half == 0:
                    relus(2)
            for half in range(2):
                for m in range(2):
                    b = take(act, ("ga", half, m))
                    evacuated(act, ("ga", 0, m) if half else ("g", 1, m))
                    A(tmp[m][:, 0:T], b[:, :], ACT.Sigmoid).then_inc(sem("sig_g"), 1)
                u += 1
                split_hi(min(u + 1, first_phase2_unit - 1))

            def absorbed_query(h):
                evac(A(q_abs[h % 2][:, :], take(act, ("qa", h))[:, :], ACT.Copy, scale=HD ** -0.5), ("qa", h))

            def exps(h):
                for qt in range(NT):
                    act.wait_ge(sem("max_ready"), NT * h + qt + 1)
                    p, n = prob[h % 2][qt][:, :], NT * (h % 2) + qt
                    A(p, p, ACT.Exp, bias=negmax[:, n:n + 1], accum_out=sums[:, n:n + 1]).then_inc(sem("exp_ready"), 1)

            def attention_start():
                evac(A(wukT[:, :, :], take(act, "wukT")[:, :].rearrange("p (i r) -> p i r", i=NI), ACT.Copy), "wukT")
                for i in range(NI):
                    evac(A(qT[:, i, :], take(act, ("q", i))[:, :], ACT.Copy), ("q", i))
                evac(A(ckv_tok[:, :, :], take(act, "ckv_tok")[:, :].rearrange("p (i r) -> p i r", i=NT), ACT.Copy), "ckv_tok")
                absorbed_query(0)
                absorbed_query(1)
                exps(0)

            def attention_step(h):
                if h + 2 < NH:
                    absorbed_query(h + 2)
                for q in range(NT):
                    b = take(act, ("pT", h, q))[:, 0:P * (q + 1)].rearrange("p (k t) -> p k t", t=P)
                    evac(A(probT[:, 0:q + 1, q * P:q * P + P], b, ACT.Copy), ("pT", h, q))
                if h + 1 < NH:
                    exps(h + 1)
                evac(A(o_lat[h % 2][:, :], take(act, ("ol", h))[:, :], ACT.Copy), ("ol", h))

            act.wait_ge(sem("relu_used"), 12)
            for i in range(NI):
                if i:
                    act.wait_ge(sem("prep_ready"), i)
                    act.wait_ge(sem("bk_decayed"), 2 * i)
                evac(A(prep[0][:, 0:T], take(act, ("z", i))[:, :], ACT.Sigmoid, bias=pcol("w0", i)), ("z", i))
                evac(A(prep[1][:, 0:T], take(act, ("a", i))[:, :], ACT.Sigmoid, bias=pcol("a0", i)), ("a", i))
                if i:
                    filled(act, ("bonus", i - 1))
                else:
                    evacuated(act, ("k", 0, 0))
                A(prep[3][:, 0:T], kt[:, i, :], ACT.Square, scale=pcol("k_k", i)).then_inc(sem("kk_sq"), 1)
                evac(A(rs[:, :], take(act, ("kk", i))[:, :], ACT.Sqrt), ("kk", i))
                if i == 0:
                    attention_start()
                attention_step(2 * i)
                act.wait_ge(sem("cum_ready"), i + 1)
                A(tmp[0][:, 0:516], prep[2][:, 0:516], ACT.Exp, scale=-KAPPA).then_inc(sem("exps"), 1)
                A(tmp[1][:, 0:516], prep[2][:, 0:516], ACT.Exp, scale=KAPPA).then_inc(sem("exps"), 1)
                attention_step(2 * i + 1)

            act.wait_ge(sem("prep_ready"), NI)
            for c in range(NT):
                for j in range(3):
                    evac(A(tok[c % 2][j][:, :], take(act, ("tok", c, j))[:, :], ACT.Copy), ("tok", c, j))
                if c == 0:
                    for k in range(CH):
                        b = take(act, ("memT", k))
                        A(sq_mem[:, k, :], b[:, 0:MEM], ACT.Square).then_inc(sem("sq_mem"), 1)
                        evac(A(memT[:, k, :], b[:, 0:MEM], ACT.Copy), ("memT", k))
                    root()
                    act.wait_ge(sem("memn_scaled"), 1)
                    u = first_phase2_unit
                    split_hi(u + 1)
                for odd in range(2):
                    evac(A(xs_t[odd], take(act, ("scan_x", c, odd))[:, 0:256], ACT.Copy), ("scan_x", c, odd))
                for odd in range(2):
                    evac(A(us_t[odd], take(act, ("scan_u", c, odd))[:, 0:256], ACT.Copy), ("scan_u", c, odd))
                for odd in range(2):
                    rows = slice(HD * odd, HD * odd + HD)
                    b = take(act, ("yT", c, odd))
                    evac(A(y_scan[rows, :, c * P:c * P + P], b[rows, :].rearrange("p (i t) -> p i t", i=NI), ACT.Copy),
                         ("yT", c, odd))
            for i in range(NI):
                evacuated(act, ("gn_mean", i))
                A(sq_gn[:, i, :], y_scan[:, i, :], ACT.Square).then_inc(sem("gn_sq"), 1)
            for i in range(NI):
                A(op_hi[:, NI + i, :], gate_a[:, i, :], ACT.Copy).then_inc(sem("mix_hi"), 1)
            def after_unit():
                nonlocal u
                split_hi(u + 2)
                u += 1

            def mem_values(i):
                b = take(act, ("vm", i))
                evac(A(memV[:, :, 256 * i:256 * i + 256], b[:, :].rearrange("p (t n) -> p t n", t=2), ACT.Copy), ("vm", i))
                after_unit()

            def rwkv_hi(i):
                act.wait_ge(sem("gn_ready"), i + 1)
                A(op_hi[:, i, :], gate_r[:, i, :], ACT.Copy).then_inc(sem("mix_hi"), 1)

            root(rs_gn[:, 0, :])
            mem_values(0)
            root(rs_gn[:, 1, :])
            root(rs_gn[:, 2, :])
            mem_values(1)
            root(rs_gn[:, 3, :])
            mem_values(2)
            rwkv_hi(0)
            rwkv_hi(1)
            mem_values(3)
            rwkv_hi(2)
            rwkv_hi(3)
            for i in range(4):
                filled(act, ("wout", i, 1))
                after_unit()
                for c in (2 * i, 2 * i + 1):
                    evacuated(act, ("wout", i, c % 2))
                    A(sq2[:, c, :], x_res[:, c, :], ACT.Square).then_inc(sem("sq_y"), 1)
                    A(sq_g[:, c, :], x_res[:, c, :], ACT.Square, scale=pcol("final_g", c)).then_inc(sem("sq_yg"), 1)
            root()

            def hi_chunks(which, name):
                for c in range(*which):
                    act.wait_ge(sem(name + "_scaled"), c + 1)
                    A(op_hi[:, c, :], tmp[c % 2][:, 0:T], ACT.Copy).then_inc(sem(name + "_hi"), 1)

            for i in range(4):
                for m in range(2):
                    evac(A(memK[:, 2 * i + m, :], take(act, ("kT", i, m))[:, 0:MEM], ACT.Copy), ("kT", i, m))
                after_unit()
                if i == 0:
                    root(rs_mix)
                else:
                    hi_chunks(((0, 1), (1, 3), (3, 5))[i - 1], "mixn")
            hi_chunks((5, CH), "mixn")
            def u_gate(i):
                if i:
                    evacuated(act, ("u", i - 1, 0))
                evac(A(u_sig, take(act, ("u", i, 1))[:, :], ACT.Sigmoid), ("u", i, 1))
                after_unit()

            def mem_query(i):
                for m in range(2):
                    evac(A(work[:, 2 * i + m, :], take(act, ("q2", i, m))[:, :], ACT.Copy), ("q2", i, m))
                after_unit()

            def mem_exp(h):
                for qt in range(NT):
                    act.wait_ge(sem("max2_ready"), NT * h + qt + 1)
                    if h:
                        filled(act, ("p2T", h - 1, qt))
                    b = take(act, ("s2", h, qt))
                    evac(A(prob2[qt][:, :], b[:, 0:MEM], ACT.Exp, scale=1.0 / 16, bias=negmax[:, qt:qt + 1],
                           accum_out=sums[:, qt:qt + 1]), ("s2", h, qt))

            def gate(branch, i, before):
                for m in range(2):
                    if before is not None:
                        evacuated(act, ("y", *before, m))
                    evac(A(gates[m][:, :], take(act, ("pg", branch, i, m))[:, :], ACT.Sigmoid,
                           bias=pcol("b_gate_2", 8 * branch + 2 * i + m)), ("pg", branch, i, m))
                after_unit()

            u_gate(0)
            mem_query(0)
            mem_query(1)
            mem_exp(0)
            mem_query(2)
            mem_exp(1)
            mem_query(3)
            mem_exp(2)
            u_gate(1)
            mem_exp(3)
            gate(2, 0, None)
            u_gate(2)

            def gate_steps(branch, before):
                for i in range(4):
                    if branch < 2 or i:
                        gate(branch, i, (branch, i - 1) if i else before)
                    if branch == 0 and i == 3:
                        ln_sigmoids(2, 5)
                    filled(act, ("y", branch, i, 1))
                    after_unit()
                    if branch == 0 and i == 3:
                        ln_sigmoids(5, CH)
                    if branch == 2 and i:
                        u_gate(2 + i)
                    if branch == 0 and i == 1:
                        evacuated(act, "ln_mean")
                        for c in range(CH):
                            A(sq2[:, c, :], conv_b[:, c, :], ACT.Square).then_inc(sem("sq_ln"), 1)
                    if branch == 0 and i == 2:
                        root()
                        ln_sigmoids(0, 2)

            def ln_sigmoids(first, last):
                for c in range(first, last):
                    act.wait_ge(sem("ln_scaled"), c + 1)
                    A(tmp[1][:, 0:T], tmp[0][:, 0:T], ACT.Sigmoid, bias=pcol("ln_b_b_2", c)).then_inc(sem("ln_sig"), 1)

            gate_steps(2, None)
            for i in range(4):
                for m in range(2):
                    evac(A(work[:, 2 * i + m, :], take(act, ("gb", i, m))[:, :], ACT.Copy), ("gb", i, m))
                after_unit()
                if i % 2:
                    u_gate(6 + i // 2)
            for i in range(8):
                if i:
                    evacuated(act, ("cv", i - 1, 1))
                evac(A(tmp[0][:, 0:T], take(act, ("cv", i, 0))[:, :], ACT.Copy), ("cv", i, 0))
                filled(act, ("cv", i, 1))
                after_unit()
            gate_steps(0, (2, 3))
            gate_steps(1, (0, 3))
            for i in range(4):
                filled(act, ("wo2", i, 1))
                after_unit()
                for c in (2 * i, 2 * i + 1):
                    evacuated(act, ("wo2", i, c % 2))
                    A(sq_f[:, c, :], x_res[:, c, :], ACT.Square).then_inc(sem("sq_f"), 1)
            root()
            hi_chunks((0, CH), "ffn")
            for i in range(FC):
                for m in range(2):
                    if i >= 2:
                        act.wait_ge(sem("act_ready"), i - 1)
                    A(conv_f[i % 2][m][:, 0:T], take(act, ("up", i, m))[:, :], ACT.Copy,
                      scale=pcol("conv_ffn_w_2", 4 * FC + FC * m + i)).then_inc(sem("tap_ready"), 1)
                after_unit()
                evacuated(act, ("up", i, 0))
                A(sig_f[i % 2][:, 0:T], conv_f[i % 2][0][:, 0:T], ACT.Sigmoid).then_inc(sem("cg_sig"), 1)
            for i in range(4):
                for n in range(3):
                    slot_used(act, u)
                    after_unit()
                for c in (2 * i, 2 * i + 1):
                    evacuated(act, ("down", i, c % 2))
                    A(sq3[:, c, :], x_res[:, c, :], ACT.Square).then_inc(sem("sq_fin"), 1)
            root()
            for g in range(2):
                for t in range(0, NT, 2):
                    evac(A(out_tok[t][:, g * T:g * T + T], take(act, ("out", t, g))[:, :], ACT.Copy), ("out", t, g))

        @block.vector
        def _(dve):
            V = nc.vector
            steps = [0]

            def link(ins):
                steps[0] += 1
                ins.then_inc(sem("dve_steps"), 1)
                dve.wait_ge(sem("dve_steps"), steps[0])

            split = [0]

            def split_lo(upto):
                while split[0] <= min(upto, FIRST_POOL_UNIT - 1):
                    u = split[0]
                    split[0] += 1
                    nk = units[u][2]
                    dve.wait_ge(hi_ready, u + 1)
                    if u >= 2:
                        slot_used(dve, u - 2)
                    V.tensor_tensor(w_lo[u % 2][:, 0:nk, :], w_raw[u % 2][:, 0:nk, :],
                                    w_hi[u % 2][:, 0:nk, :].bitcast(F32), ALU.subtract).then_inc(lo_ready, 1)

            roots = [0]

            def variance(key, width, scale, eps):
                b = take(dve, key)
                evac(V.tensor_scalar(rs[:, 0:width], b[:, 0:width], scale, eps, ALU.mult, ALU.add), key)
                evacuated(dve, key)
                V.reciprocal(rs[:, 0:width], rs[:, 0:width]).then_inc(sem("var_ready"), 1)
                roots[0] += 1
                dve.wait_ge(sem("rs_ready"), roots[0])

            def parts(src, hi, lo, name):
                link(V.tensor_copy(hi, src))
                V.tensor_tensor(lo, src, hi.bitcast(F32), ALU.subtract).then_inc(sem(name), 1)

            def scaled_chunk(gain, c, r, name):
                V.scalar_tensor_tensor(tmp[c % 2][:, 0:T], x_res[:, c, :], pcol(gain, c), r[:, 0:T], ALU.mult, ALU.mult)\
                    .then_inc(sem(name + "_scaled"), 1)

            def lo_chunk(c, name):
                dve.wait_ge(sem(name + "_hi"), c + 1)
                V.tensor_tensor(op_lo[:, c, :], tmp[c % 2][:, 0:T], op_hi[:, c, :].bitcast(F32), ALU.subtract)\
                    .then_inc(sem(name + "_ready"), 1)
                dve.wait_ge(sem(name + "_ready"), c + 1)

            dve.wait_ge(sem("sq_x"), NT)
            link(V.tensor_scalar(rs_x, rs_x, 1.0 / D, NORM_EPS, ALU.mult, ALU.add))
            V.reciprocal(rs_x, rs_x).then_inc(sem("var_ready"), 1)
            roots[0] += 1
            evac(V.tensor_copy(gain, take(dve, "gain")[:, 0:CH]), "gain")
            dve.wait_ge(sem("rs_ready"), roots[0])
            for t in range(0, NT, 2):
                V.tensor_scalar(x_scaled[:, t, :], x_tok[:, t, :], rs_x[:, t:t + 1], None, ALU.mult).then_inc(sem("x_scaled0"), 1)
            split_lo(0)
            evacuated(dve, "gain")
            for c in range(CH):
                b = take(dve, ("xnT", c))
                dve.wait_ge(sem("xn_hi"), c + 1)
                evac(V.scalar_tensor_tensor(op_lo[:, c, :], b[:, :], gain[:, c:c + 1], op_hi[:, c, :].bitcast(F32), ALU.mult,
                                            ALU.subtract), ("xnT", c))
            split_lo(1)

            sh = [0]

            def shift(key, dst, mu):
                sh[0] += 1
                b = take(dve, key)
                dve.wait_ge(sem("unshifted"), sh[0])
                evac(V.scalar_tensor_tensor(dst[:, 1:T], b[:, 0:T - 1], mu, dst[:, 1:T], ALU.mult, ALU.add), key)

            filled(dve, ("qd", 0, 1))
            split_lo(2)
            filled(dve, ("kvi", 0, 1))
            split_lo(3)
            evac(V.tensor_copy(par[:, 0:T], take(dve, ("par", 0))[:, :]), ("par", 0))
            evac(V.tensor_copy(par[:, T:PARAM_TILES * P], take(dve, ("par", 1))[:, 0:PARAM_TILES * P - T]), ("par", 1))
            evacuated(dve, ("par", 0))
            evacuated(dve, ("par", 1))
            c0 = PARAM_AT["mu_r"]
            link(V.tensor_scalar(omm, par[:, c0:c0 + 13], -1.0, 1.0, ALU.mult, ALU.add))
            c0 = PARAM_AT["k_a"]
            V.tensor_scalar(omka, par[:, c0:c0 + 4], -1.0, 1.0, ALU.mult, ALU.add).then_inc(sem("derived"), 1)
            dve.wait_ge(sem("derived"), 1)
            shift(("wa", 0, 0), tmp[2], pcol("mu_wa"))
            split_lo(4)
            for m in range(2):
                evacuated(dve, ("qd", 0, m))
                evacuated(dve, ("kvi", 0, m))
            variance("ss_q", T, 1.0 / 256, NORM_EPS)
            for m in range(2):
                V.scalar_tensor_tensor(qd[:, m, :], qd[:, m, :], pcol("q_norm_g", m), rs[:, :], ALU.mult, ALU.mult)\
                    .then_inc(sem("cq_ready"), 1)
            dve.wait_ge(sem("cq_ready"), 2)
            variance("ss_kv", T, 1.0 / P, NORM_EPS)
            V.scalar_tensor_tensor(ckv[:, :], ckv[:, :], pcol("kv_norm_g"), rs[:, :], ALU.mult, ALU.mult).then_inc(sem("ckv_ready"), 1)
            dve.wait_ge(sem("ckv_ready"), 1)
            b = take(dve, "ki_mean")
            evac(V.scalar_tensor_tensor(kidx[:, :], b[:, :], -1.0 / HD, kidx[:, :], ALU.mult, ALU.add), "ki_mean")

            def index_keys():
                variance("ki_var", T, 1.0 / HD, LN_EPS)
                link(V.scalar_tensor_tensor(kidx[:, :], kidx[:, :], pcol("kidx_g"), rs[:, :], ALU.mult, ALU.mult))
                V.tensor_scalar(kidx[:, :], kidx[:, :], pcol("kidx_b"), None, ALU.add).then_inc(sem("kidx_ready"), 1)
                b = take(dve, "w_idx")[:, :].rearrange("p (t n) -> p t n", t=NT)[:, :, HD:HD + 4]
                evac(V.tensor_scalar(w_idx.rearrange("p (t n) -> p t n", t=NT), b, 0.5, None, ALU.mult), "w_idx")
                evacuated(dve, "w_idx")

            logits = [0]

            def index_scores(qt):
                w = P * (qt + 1)
                s = score[:, qt, 0:w]
                for h in range(4):
                    evacuated(dve, ("lg", qt, h))
                    wi = w_idx[:, 4 * qt + h:4 * qt + h + 1]
                    r = prep[logits[0] % 4][:, 0:w]
                    if h:
                        ins = V.scalar_tensor_tensor(s, r, wi, s, ALU.mult, ALU.add)
                    else:
                        ins = V.tensor_scalar(s, r, wi, None, ALU.mult)
                    logits[0] += 1
                    ins.then_inc(sem("relu_used"), 1)
                    dve.wait_ge(sem("relu_used"), logits[0])
                V.tensor_copy(top8, s[:, 0:8]).then_inc(sem("score_ready"), 1)
                dve.wait_ge(sem("score_ready"), qt)

            rounds = [0]

            def topk_rounds(upto):
                per_tile = TOPK // 8
                while rounds[0] < upto:
                    qt, n = 1 + rounds[0] // per_tile, rounds[0] % per_tile
                    rounds[0] += 1
                    s = score[:, qt, 0:P * (qt + 1)]
                    if n == 0:
                        dve.wait_ge(sem("causal"), qt + 1)
                    link(V.max(top8, s))
                    link(V.match_replace(s, top8, s, TAKEN))
                    if n == per_tile - 1:
                        link(V.tensor_scalar(s, s, -2.0e38, MASKED, ALU.is_gt, ALU.mult))

            u = 3
            for half in range(2):
                for w, dst in enumerate((lambda i: ar[:, i, 1, :], lambda i: kt[:, i, :], lambda i: vf[:, i, :])):
                    for m in range(2):
                        i = 2 * half + m
                        shift(("rkv"[w], half, m), dst(i), pcol("mu_" + "rkv"[w], i))
                    u += 1
                    split_lo(u + 1)
                    if half == 0 and w == 1:
                        index_keys()
                    elif half == 0 and w == 2:
                        index_scores(1)
                    elif half == 1:
                        if w == 0:
                            index_scores(3)
                        topk_rounds(13 + 7 * w)
                for m in range(2):
                    b = take(dve, ("g", half, m))
                    dve.wait_ge(sem("sig_g"), 2 * half + m + 1)
                    evac(V.tensor_tensor(gate_r[:, 2 * half + m, :], b[:, :], tmp[m][:, 0:T], ALU.mult), ("g", half, m))
                u += 1
                split_lo(u + 1)
                if half == 0:
                    index_scores(2)
                    topk_rounds(7)
                else:
                    topk_rounds(34)
            for half in range(2):
                for m in range(2):
                    b = take(dve, ("ga", half, m))
                    dve.wait_ge(sem("sig_g"), 4 + 2 * half + m + 1)
                    evac(V.tensor_tensor(gate_a[:, 2 * half + m, :], b[:, :], tmp[m][:, 0:T], ALU.mult), ("ga", half, m))
                u += 1
                split_lo(min(u + 1, first_phase2_unit - 1))
                topk_rounds(41 + 7 * half)

            cum = prep[2][:, 0:516].rearrange("p (c t) -> p c t", c=NT)
            link(V.memset(prep[2][:, 0:516], 0.0))
            e_down = tmp[0][:, 0:516].rearrange("p (c t) -> p c t", c=NT)
            e_up = tmp[1][:, 0:516].rearrange("p (c t) -> p c t", c=NT)

            def chunked(t):
                return t.rearrange("p (c t) -> p c t", c=NT)

            for half in range(2):
                for m in range(2):
                    evacuated(dve, ("r", half, m))
                    evacuated(dve, ("k", half, m))
                    evacuated(dve, ("v", half, m))
                    evacuated(dve, ("ga", half, m))

            def maxima(h):
                for n in range(NT):
                    if h >= 2:
                        filled(dve, ("pT", h - 2, n))
                    elif n == 0:
                        dve.wait_ge(sem("causal"), 1)
                    w, col = P * (n + 1), NT * (h % 2) + n
                    p = prob[h % 2][n][:, :]
                    b = take(dve, ("s", h, n))
                    evac(V.tensor_tensor(p, b[:, 0:w], score[:, n, 0:w], ALU.add), ("s", h, n))
                    evacuated(dve, ("s", h, n))
                    V.tensor_reduce(negmax[:, col:col + 1], p, X_AXIS, ALU.max, negate=True).then_inc(sem("max_ready"), 1)

            def probs(h):
                for n in range(NT):
                    col = NT * (h % 2) + n
                    p = prob[h % 2][n][:, :]
                    dve.wait_ge(sem("exp_ready"), NT * h + n + 1)
                    link(V.reciprocal(rsum[:, col:col + 1], sums[:, col:col + 1]))
                    V.tensor_scalar(p, p, rsum[:, col:col + 1], None, ALU.mult).then_inc(sem("prob_ready"), 1)

            def head_out(h):
                rows, i = slice(HD * (h % 2), HD * (h % 2) + HD), h // 2
                b = take(dve, ("o", h))
                evac(V.tensor_tensor(gate_a[rows, i, :], b[rows, :], gate_a[rows, i, :], ALU.mult), ("o", h))

            def attention_step(h):
                if h + 1 < NH:
                    maxima(h + 1)
                if h:
                    head_out(h - 1)
                if h + 1 < NH:
                    probs(h + 1)

            for i in range(NI):
                evacuated(dve, ("z", i))
                if i:
                    link(V.memset(cum[:, :, 0:1], 0.0))
                for c in range(NT):
                    ins = V.tensor_tensor_scan(cum[:, c, 1:P + 1], ones[:, :], prep[0][:, c * P:c * P + P], 0.0, ALU.mult, ALU.add)
                    link(ins)
                link(V.tensor_copy(mid, cum[:, :, HD]))
                V.tensor_tensor(cum, cum, mid.unsqueeze(2).to_broadcast([P, NT, P + 1]), ALU.subtract)\
                    .then_inc(sem("cum_ready"), 1)
                dve.wait_ge(sem("cum_ready"), i + 1)
                link(V.tensor_scalar(prep[0][:, 0:T], kt[:, i, :], pcol("k_k", i), None, ALU.mult))
                evacuated(dve, ("kk", i))
                link(V.tensor_scalar(rs[:, :], rs[:, :], 1e-12, None, ALU.max))
                link(V.reciprocal(rs[:, :], rs[:, :]))
                link(V.tensor_tensor(prep[0][:, 0:T], prep[0][:, 0:T], rs[:, :], ALU.mult))
                evacuated(dve, ("a", i))
                link(V.tensor_scalar(rs[:, :], prep[1][:, 0:T], pcol("k_a", i), omka[:, i:i + 1], ALU.mult, ALU.add))
                link(V.tensor_tensor(kt[:, i, :], kt[:, i, :], rs[:, :], ALU.mult))
                V.scalar_tensor_tensor(prep[3][:, 0:T], ar[:, i, 1, :], pcol("r_k", i), kt[:, i, :], ALU.mult, ALU.mult)\
                    .then_inc(sem("rk_ready"), 1)
                V.tensor_tensor(prep[1][:, 0:T], prep[0][:, 0:T], prep[1][:, 0:T], ALU.mult).then_inc(sem("b_ready"), 1)
                if i == 0:
                    maxima(0)
                    probs(0)
                attention_step(2 * i)
                dve.wait_ge(sem("exps"), 2 * i + 2)
                V.tensor_tensor(dec.rearrange("p (i c) -> p i c", i=NI)[:, i, 0:NT - 1], e_up[:, 1:NT, 0], e_down[:, 0:NT - 1, P],
                                ALU.mult)
                V.scalar_tensor_tensor(chunked(ar[:, i, 0, :]), chunked(prep[0][:, 0:T]), -1.0, e_down[:, :, 0:P], ALU.mult, ALU.mult)
                b = take(dve, ("bonus", i))
                evac(V.tensor_tensor(bonus_v[:, i, :], b[:, :], vf[:, i, :], ALU.mult), ("bonus", i))
                dve.wait_ge(sem("rk_ready"), i + 1)
                V.tensor_tensor(chunked(ar[:, i, 1, :]), chunked(ar[:, i, 1, :]), e_down[:, :, 1:P + 1], ALU.mult).then_inc(sem("prep_ready"), 1)
                attention_step(2 * i + 1)
            head_out(NH - 1)

            dve.wait_ge(sem("prep_ready"), NI)
            for c in range(NT):
                for odd in range(2):
                    hs = slice(NI * odd, NI * odd + NI)
                    for name, dst in (("gb", g_b), ("gk", g_k)):
                        for i2 in range(2):
                            h = NI * odd + 2 * i2
                            b = take(dve, (name, c, odd, i2))[:, :].rearrange("p (n a t) -> p n a t", n=2, a=2)
                            evac(V.tensor_tensor(dst[:, h:h + 2, :, :], b, mask_ar[:, :, :].unsqueeze(1).to_broadcast([P, 2, 2, P]),
                                                 ALU.mult), (name, c, odd, i2))
                    b = take(dve, ("low", c, odd))[:, :].rearrange("p (i t) -> p i t", i=NI)
                    evac(V.tensor_tensor(low[:, hs, :], b, mask_low[:, :].unsqueeze(1).to_broadcast([P, NI, P]), ALU.mult),
                         ("low", c, odd))
                    evacuated(dve, ("gb", c, odd, 0))
                    evacuated(dve, ("gb", c, odd, 1))
                    evacuated(dve, ("low", c, odd))
                    eye = ident[:, :].unsqueeze(1).to_broadcast([P, NI, P])
                    V.tensor_tensor(inv[:, hs, :], g_b[:, hs, 0, :], mask_lev[:, 0, :].unsqueeze(1).to_broadcast([P, NI, P]), ALU.mult)
                    link(V.tensor_tensor(invT[:, hs, :], low[:, hs, :], mask_lowT[:, :].unsqueeze(1).to_broadcast([P, NI, P]), ALU.mult))
                    link(V.tensor_tensor(inv[:, hs, :], inv[:, hs, :], eye, ALU.add))
                    V.tensor_tensor(invT[:, hs, :], invT[:, hs, :], eye, ALU.add).then_inc(sem(f"inv_init{odd}"), 1)
                    dve.wait_ge(sem(f"inv_init{odd}"), c + 1)
                for lev in range(1, 7):
                    for odd in range(2):
                        hs = slice(NI * odd, NI * odd + NI)
                        b = take(dve, ("w", c, lev, odd))[:, :].rearrange("p (i t) -> p i t", i=NI)
                        evac(V.tensor_tensor(wprod[:, hs, :], b, mask_lev[:, lev, :].unsqueeze(1).to_broadcast([P, NI, P]), ALU.mult),
                             ("w", c, lev, odd))
                    for odd in range(2):
                        hs = slice(NI * odd, NI * odd + NI)
                        for name, dst in (("dinv", inv), ("dinvT", invT))[0:2 if lev < 6 else 1]:
                            b = take(dve, (name, c, lev, odd))[:, :].rearrange("p (i t) -> p i t", i=NI)
                            if lev > 1:
                                evacuated(dve, (name, c, lev - 1, odd))
                            evac(V.tensor_tensor(dst[:, hs, :], b, dst[:, hs, :], ALU.add), (name, c, lev, odd))
                    if c == 0 and lev == 2:
                        for k in range(CH):
                            evacuated(dve, ("memT", k))
                        variance("ss_mem", MEM, 1.0 / D, EPS2)
                        for k in range(CH):
                            ins = V.scalar_tensor_tensor(memn[:, k, :], memT[:, k, :], pcol("norm_mem_g_2", k), rs[:, 0:MEM],
                                                         ALU.mult, ALU.mult)
                        ins.then_inc(sem("memn_scaled"), 1)
                        dve.wait_ge(sem("memn_scaled"), 1)
                if c < NT - 1:
                    for odd in range(2):
                        rows = slice(HD * odd, HD * odd + HD)
                        b = take(dve, ("p", c, odd))[rows, 0:256].rearrange("p (i d) -> p i d", i=NI)
                        f = dec[rows, :].rearrange("p (i c) -> p i c", i=NI)[:, :, c]
                        evac(V.tensor_tensor(state[rows, :, :], b, f.unsqueeze(2).to_broadcast([HD, NI, HD]), ALU.mult), ("p", c, odd))

            def rwkv_lo(i):
                dve.wait_ge(sem("mix_hi"), NI + i + 1)
                V.tensor_tensor(op_lo[:, i, :], gate_r[:, i, :], op_hi[:, i, :].bitcast(F32), ALU.subtract)\
                    .then_inc(sem("mix_ready"), 1)

            filled(dve, ("scan_x", NT - 1, 0))
            link(V.tensor_copy(memn_hi[:, :, :], memn[:, :, :]))
            V.tensor_tensor(memn_lo[:, :, :], memn[:, :, :], memn_hi[:, :, :].bitcast(F32), ALU.subtract).then_inc(sem("memn_ready"), 1)
            for i in range(NI):
                b = take(dve, ("gn_mean", i))
                y = y_scan[:, i, :]
                evac(V.scalar_tensor_tensor(y, b[:, :], -1.0 / HD, y, ALU.mult, ALU.add), ("gn_mean", i))
            for i in range(NI):
                b = take(dve, ("gn_var", i))
                evac(V.tensor_scalar(rs_gn[:, i, :], b[:, :], 1.0 / HD, GN_EPS, ALU.mult, ALU.add), ("gn_var", i))
                evacuated(dve, ("gn_var", i))
                V.reciprocal(rs_gn[:, i, :], rs_gn[:, i, :]).then_inc(sem("var_ready"), 1)
                roots[0] += 1
            for h in range(NH):
                evacuated(dve, ("o", h))
            for i in range(NI):
                dve.wait_ge(sem("mix_hi"), i + 1)
                V.tensor_tensor(op_lo[:, NI + i, :], gate_a[:, i, :], op_hi[:, NI + i, :].bitcast(F32), ALU.subtract)\
                    .then_inc(sem("mix_ready"), 1)
            dve.wait_ge(sem("rs_ready"), roots[0])
            for i in range(NI):
                y = y_scan[:, i, :]
                link(V.scalar_tensor_tensor(y, y, pcol("gn_g", i), rs_gn[:, i, :], ALU.mult, ALU.mult))
                link(V.scalar_tensor_tensor(y, y, pcol("gn_b", i), bonus_v[:, i, :], ALU.add, ALU.add))
                V.tensor_tensor(gate_r[:, i, :], y, gate_r[:, i, :], ALU.mult).then_inc(sem("gn_ready"), 1)
                dve.wait_ge(sem("gn_ready"), i + 1)
                if i:
                    rwkv_lo(i - 1)
            rwkv_lo(NI - 1)

            def residual(what, i):
                for m in range(2):
                    b = take(dve, (what, i, m))
                    x = x_res[:, 2 * i + m, :]
                    evac(V.tensor_tensor(x, b[:, :], x, ALU.add), (what, i, m))

            def pair_squares(key, sq, i):
                dve.wait_ge(sem("sq_" + key), 2 * i + 2)
                V.tensor_tensor(sq[:, 2 * i, :], sq[:, 2 * i, :], sq[:, 2 * i + 1, :], ALU.add).then_inc(sem("paired_" + key), 1)

            for i in range(4):
                if i:
                    pair_squares("y", sq2, i - 1)
                    pair_squares("yg", sq_g, i - 1)
                residual("wout", i)
            for i in range(4):
                for m in range(2):
                    evacuated(dve, ("wout", i, m))
            variance("y", T, 1.0 / D, NORM_EPS)
            evac(V.tensor_tensor(rs_mix, take(dve, "yg")[:, :], rs[:, :], ALU.mult), "yg")
            evacuated(dve, "yg")
            link(V.tensor_tensor(rs_mix, rs_mix, rs[:, :], ALU.mult))
            link(V.tensor_scalar(rs_mix, rs_mix, 1.0 / D, EPS2, ALU.mult, ALU.add))
            V.reciprocal(rs_mix, rs_mix).then_inc(sem("var_ready"), 1)
            roots[0] += 1

            def mix_norm(c):
                x = x_res[:, c, :]
                link(V.scalar_tensor_tensor(x, x, pcol("final_g", c), rs[:, :], ALU.mult, ALU.mult))
                if c == 0:
                    dve.wait_ge(sem("rs_ready"), roots[0])
                scaled_chunk("norm_mix_g_2", c, rs_mix, "mixn")
                if c:
                    lo_chunk(c - 1, "mixn")

            for i in range(4):
                mix_norm(i)
            for i in range(4, CH):
                mix_norm(i)
            lo_chunk(CH - 1, "mixn")

            for s_ in range(2):
                link(V.memset(pad_b[s_][:, 0:KB - 1], 0.0))
            taps = [0]

            def conv_taps(n):
                for _ in range(n):
                    i, k = divmod(taps[0], KB)
                    if i == CH:
                        return
                    taps[0] += 1
                    pad, y = pad_b[i % 2], conv_b[:, i, :]
                    if k == 0:
                        evacuated(dve, ("u", i, 0))
                        ins = V.tensor_scalar(y, pad[:, 0:T], pcol("conv_b_w_2", i), pcol("conv_b_bias_2", i), ALU.mult, ALU.add)
                    else:
                        ins = V.scalar_tensor_tensor(y, pad[:, k:k + T], pcol("conv_b_w_2", 8 * k + i), y, ALU.mult, ALU.add)
                    if k < KB - 1:
                        link(ins)
                    else:
                        ins.then_inc(sem("conv_ready"), 1)

            def u_input(i):
                if taps[0] < KB * (i - 1):
                    conv_taps(KB * (i - 1) - taps[0])
                evacuated(dve, ("u", i, 1))
                b = take(dve, ("u", i, 0))
                if i >= 2:
                    dve.wait_ge(sem("conv_ready"), i - 1)
                evac(V.tensor_tensor(pad_b[i % 2][:, KB - 1:KB - 1 + T], b[:, :], u_sig, ALU.mult), ("u", i, 0))

            def mem_softmax(h):
                for n in range(NT + 1):
                    if n < NT:
                        b = take(dve, ("s2", h, n))
                        link(V.tensor_reduce(negmax[:, n:n + 1], b[:, 0:MEM], X_AXIS, ALU.max, negate=True))
                        V.tensor_scalar(negmax[:, n:n + 1], negmax[:, n:n + 1], 1.0 / 16, None, ALU.mult).then_inc(sem("max2_ready"), 1)
                    if n:
                        q = n - 1
                        evacuated(dve, ("s2", h, q))
                        link(V.reciprocal(rsum[:, q:q + 1], sums[:, q:q + 1]))
                        V.tensor_scalar(prob2[q][:, :], prob2[q][:, :], rsum[:, q:q + 1], None, ALU.mult).then_inc(sem("prob2_ready"), 1)

            def mem_probs(h):
                for q in range(NT):
                    b = take(dve, ("p2T", h, q))[:, 0:MEM].rearrange("p (k t) -> p k t", t=P)
                    evac(V.tensor_copy(prob2T[:, :, q * P:q * P + P], b), ("p2T", h, q))

            def mem_out(h):
                for d in range(2):
                    b = take(dve, ("oc", h, d))
                    hi = op2_hi[:, 2 * h + d, :]
                    link(V.tensor_copy(hi, b[:, :]))
                    ins = V.tensor_tensor(op2_lo[:, 2 * h + d, :], b[:, :], hi.bitcast(F32), ALU.subtract)
                    evac(ins, ("oc", h, d))

            u_input(0)
            conv_taps(5)
            conv_taps(5)
            mem_softmax(0)
            mem_probs(0)
            mem_softmax(1)
            conv_taps(5)
            mem_out(0)
            mem_probs(1)
            mem_softmax(2)
            u_input(1)
            mem_out(1)
            mem_probs(2)
            mem_softmax(3)
            conv_taps(6)
            mem_out(2)
            mem_probs(3)
            conv_taps(10)
            u_input(2)
            mem_out(3)

            def gate_steps(branch):
                for i in range(4):
                    if branch == 0 and i == 2:
                        for c in range(NI):
                            pair_squares("ln", sq2, c)
                    if branch == 0 and i == 3:
                        ln_silu(2, 5)
                    for m in range(2):
                        evacuated(dve, ("pg", branch, i, m))
                        b = take(dve, ("y", branch, i, m))
                        mg = merged[:, 2 * i + m, :]
                        if branch == 2:
                            evac(V.tensor_tensor(mg, b[:, :], gates[m][:, :], ALU.mult), ("y", branch, i, m))
                        else:
                            evac(V.tensor_tensor(tmp[2][:, 0:T], b[:, :], gates[m][:, :], ALU.mult), ("y", branch, i, m))
                            evacuated(dve, ("y", branch, i, m))
                            link(V.tensor_tensor(mg, mg, tmp[2][:, 0:T], ALU.add))
                        if branch == 1:
                            parts(mg, merged_hi[:, 2 * i + m, :], merged_lo[:, 2 * i + m, :], "merged_ready")
                    if branch == 2:
                        conv_taps(10)
                        if i:
                            u_input(2 + i)
                        conv_taps(8)
                    if branch == 0 and i == 0:
                        conv_taps(KB * CH)
                    if branch == 0 and i == 1:
                        b = take(dve, "ln_mean")
                        for c in range(CH):
                            ins = V.scalar_tensor_tensor(conv_b[:, c, :], b[:, :], -1.0 / D, conv_b[:, c, :], ALU.mult, ALU.add)
                        evac(ins, "ln_mean")
                    if branch == 0 and i == 2:
                        variance("ln_var", T, 1.0 / D, EPS2)
                        ln_silu(0, 2)
                    if branch == 0 and i == 3:
                        ln_silu(5, CH)

            def ln_silu(first, last):
                for c in range(first, last):
                    V.scalar_tensor_tensor(tmp[0][:, 0:T], conv_b[:, c, :], pcol("ln_b_g_2", c), rs[:, :], ALU.mult, ALU.mult)\
                        .then_inc(sem("ln_scaled"), 1)
                    dve.wait_ge(sem("ln_sig"), c + 1)
                    link(V.scalar_tensor_tensor(conv_b[:, c, :], tmp[0][:, 0:T], pcol("ln_b_b_2", c), tmp[1][:, 0:T], ALU.add, ALU.mult))

            def conv3(dst, pad, weights, first, stride):
                link(V.tensor_scalar(dst, pad[:, 0:T], pcol(weights, first), None, ALU.mult))
                link(V.scalar_tensor_tensor(dst, pad[:, 1:1 + T], pcol(weights, first + stride), dst, ALU.mult, ALU.add))
                return V.scalar_tensor_tensor(dst, pad[:, 2:2 + T], pcol(weights, first + 2 * stride), dst, ALU.mult, ALU.add)

            gate_steps(2)
            for i in range(4):
                for m in range(2):
                    evacuated(dve, ("y", 2, i, m))
            for i in range(4):
                conv_taps(10)
                if i % 2:
                    u_input(6 + i // 2)
            link(V.memset(pad_a[:, 0:KA - 1], 0.0))
            for i in range(8):
                evacuated(dve, ("cv", i, 0))
                evac(V.tensor_tensor(pad_a[:, KA - 1:KA - 1 + T], take(dve, ("cv", i, 1))[:, :], tmp[0][:, 0:T], ALU.mult), ("cv", i, 1))
                evacuated(dve, ("cv", i, 1))
                evacuated(dve, ("gb", i // 2, i % 2))
                link(conv3(tmp[1][:, 0:T], pad_a, "conv_a_w_2", i, 8))
                link(V.tensor_tensor(tmp[1][:, 0:T], tmp[1][:, 0:T], work[:, i, :], ALU.mult))
                parts(tmp[1][:, 0:T], op2_hi[:, i, :], op2_lo[:, i, :], "op2_ready0")
                conv_taps(6)
            gate_steps(0)
            for c in range(CH):
                parts(conv_b[:, c, :], op2_hi[:, c, :], op2_lo[:, c, :], "op2_ready1")
            gate_steps(1)
            for i in range(4):
                if i:
                    pair_squares("f", sq_f, i - 1)
                residual("wo2", i)
            for i in range(4):
                for m in range(2):
                    evacuated(dve, ("wo2", i, m))
            variance("f", T, 1.0 / D, EPS2)
            for c in range(CH):
                scaled_chunk("norm_ffn_g_2", c, rs, "ffn")
                if c:
                    lo_chunk(c - 1, "ffn")
            lo_chunk(CH - 1, "ffn")

            for i in range(FC):
                for m in range(2):
                    b, y = take(dve, ("up", i, m)), conv_f[i % 2][m]
                    dve.wait_ge(sem("tap_ready"), 2 * i + m + 1)
                    for back in (1, 2):
                        w = pcol("conv_ffn_w_2", 2 * FC * (2 - back) + FC * m + i)
                        ins = V.scalar_tensor_tensor(y[:, back:T], b[:, 0:T - back], w, y[:, back:T], ALU.mult, ALU.add)
                        if back == 1:
                            link(ins)
                    evac(ins, ("up", i, m))
                g, y = sig_f[i % 2][:, 0:T], conv_f[i % 2]
                dve.wait_ge(sem("cg_sig"), i + 1)
                link(V.tensor_tensor(g, g, y[0][:, 0:T], ALU.mult))
                evacuated(dve, ("up", i, 1))
                link(V.tensor_tensor(g, g, y[1][:, 0:T], ALU.mult))
                lo = act_lo[:, i, :] if i < 16 else act_lo2[:, i - 16, :]
                parts(g, act_hi[:, i, :], lo, "act_ready")
            for i in range(4):
                if i:
                    pair_squares("fin", sq3, i - 1)
                residual("down", i)
            for i in range(4):
                for m in range(2):
                    evacuated(dve, ("down", i, m))
            variance("fin", T, 1.0 / D, EPS2)
            for c in range(CH):
                V.scalar_tensor_tensor(x_res[:, c, :], x_res[:, c, :], pcol("norm_final_g_2", c), rs[:, :], ALU.mult, ALU.mult)\
                    .then_inc(sem("fin_ready"), 1)
            for g in range(2):
                for t in range(1, NT, 2):
                    evac(V.tensor_copy(out_tok[t][:, g * T:g * T + T], take(dve, ("out", t, g))[:, :]), ("out", t, g))



NAMES = ["x", "norm_g", "w_in", "mu_shift", "w0", "w_up", "a0", "a_up", "k_k", "k_a", "r_k", "gn_g", "gn_b", "q_norm_g",
         "kv_norm_g", "w_uq", "w_uk", "w_uv", "w_qidx", "kidx_g", "kidx_b", "w_out", "final_g", "mem_2", "norm_mix_g_2",
         "norm_mem_g_2", "w_in_2", "b_gate_2", "conv_a_w_2", "w_a_out_2", "conv_b_w_2", "conv_b_bias_2", "ln_b_g_2",
         "ln_b_b_2", "w_b_out_2", "w_kv_2", "w_att_out_2", "w_o_2", "norm_ffn_g_2", "w_up_2", "conv_ffn_w_2", "w_down_2",
         "norm_final_g_2"]


def kernel(**inputs):
    import concourse.bacc as bacc
    from concourse.bass_utils import run_bass_kernel_spmd

    nc = bacc.Bacc("TRN2", target_bir_lowering=False, num_devices=1)
    arrays, dram = {}, {}
    for name in NAMES:
        a = np.ascontiguousarray(inputs[name])
        arrays["in_" + name] = a
        dram[name] = nc.dram_tensor("in_" + name, a.shape, mybir.dt.from_np(a.dtype), kind="ExternalInput").ap()
    out = nc.dram_tensor("out", (1, T, D), F32, kind="ExternalOutput").ap()
    build(nc, dram, out)
    r = run_bass_kernel_spmd(nc, [arrays], core_ids=[0])
    return r.results[0]["out"]
```
